# Optimizing a Trainium2 kernel written in Bass

```python
import math
import jax, jax.numpy as jnp
from jax import lax
import numpy as np

D_MODEL = 1024
BATCH = 1
SEQ = 512
DEPTH = 2

GRID_W = 64
CTX_LEN = 256
N_HEADS = 8
QK_NOPE = 64
QK_ROPE = 32
V_HEAD = 64
Q_LORA = 384
KV_LORA = 256
W_ATTN_IN = Q_LORA + KV_LORA + QK_ROPE
ATTN_SCALE = 1.0 / math.sqrt(QK_NOPE + QK_ROPE)
Q_BLOCK = 128
ROPE_THETA = 10000.0
FOURIER_GROUPS = 6
FOURIER_GROUP_W = 64
W_FOURIER = FOURIER_GROUPS * FOURIER_GROUP_W
SSM_GROUP_W = 16
SSM_GROUPS = 24
SSM_STATE = 64
W_SSM = SSM_GROUPS * SSM_GROUP_W
W_IN = W_ATTN_IN + W_FOURIER + W_SSM
N_BRANCH = 3
D_FF = 4 * D_MODEL
EPS = 1e-6

kernel_name = "hybrid_mla_fnet_s5_prefix_block"

def rms_norm(x, g):
    xf = x.astype(jnp.float32)
    y = xf * lax.rsqrt(jnp.mean(xf * xf, axis=-1, keepdims=True) + EPS)
    return (y * g.astype(jnp.float32)).astype(x.dtype)

def axial_rope_angles(n_tokens):
    rows = n_tokens // GRID_W
    r_ix, c_ix = jnp.meshgrid(jnp.arange(rows, dtype=jnp.float32),
                              jnp.arange(GRID_W, dtype=jnp.float32), indexing="ij")
    r_ix, c_ix = r_ix.reshape(-1), c_ix.reshape(-1)
    half = QK_ROPE // 2
    inv = ROPE_THETA ** (-jnp.arange(0, half, 2, dtype=jnp.float32) / half)
    ang = jnp.concatenate([r_ix[:, None] * inv, c_ix[:, None] * inv], axis=-1)
    return jnp.cos(ang), jnp.sin(ang)

def apply_rope(x, cos, sin):
    h = QK_ROPE // 2
    x1, x2 = x[..., :h], x[..., h:]
    cos, sin = cos.astype(x.dtype), sin.astype(x.dtype)
    return jnp.concatenate([x1 * cos - x2 * sin, x2 * cos + x1 * sin], axis=-1)

def mla_q(z_a, q_norm, w_uq):
    bsz, n, _ = z_a.shape
    q = (rms_norm(z_a[..., :Q_LORA], q_norm) @ w_uq).reshape(bsz, n, N_HEADS, QK_NOPE + QK_ROPE)
    return q[..., :QK_NOPE], q[..., QK_NOPE:]

def mla_kv(z_a, kv_norm, w_ukv):
    bsz, n, _ = z_a.shape
    c_kv = rms_norm(z_a[..., Q_LORA:Q_LORA + KV_LORA], kv_norm)
    kv = (c_kv @ w_ukv).reshape(bsz, n, N_HEADS, QK_NOPE + V_HEAD)
    k_rope = z_a[..., Q_LORA + KV_LORA:]
    return kv[..., :QK_NOPE], kv[..., QK_NOPE:], k_rope

def attend(q_nope, q_rope, k_nope, k_rope, v):
    s = jnp.einsum('bqhd,bkhd->bhqk', q_nope, k_nope, preferred_element_type=jnp.float32)
    s = s + jnp.einsum('bqhr,bkr->bhqk', q_rope, k_rope, preferred_element_type=jnp.float32)
    p = jax.nn.softmax(s * ATTN_SCALE, axis=-1).astype(v.dtype)
    return jnp.einsum('bhqk,bkhd->bqhd', p, v)

def latent_attention(q_nope, q_rope, k_nope, k_rope, v):
    bsz, n, h, _ = q_nope.shape
    nb = n // Q_BLOCK
    qn = q_nope.reshape(bsz, nb, Q_BLOCK, h, QK_NOPE).transpose(1, 0, 2, 3, 4)
    qr = q_rope.reshape(bsz, nb, Q_BLOCK, h, QK_ROPE).transpose(1, 0, 2, 3, 4)
    o = lax.map(lambda a: attend(a[0], a[1], k_nope, k_rope, v), (qn, qr))
    return o.transpose(1, 0, 2, 3, 4).reshape(bsz, n, h * V_HEAD)

def fourier_mix(z):
    bsz, n, _ = z.shape
    u = z.astype(jnp.float32).reshape(bsz, n, FOURIER_GROUPS, FOURIER_GROUP_W)
    y = jnp.fft.fftn(u, axes=(1, 3), norm="ortho").real
    return y.reshape(bsz, n, W_FOURIER).astype(z.dtype)

def s5_discretize(a_re, a_im, log_step, b_re, b_im):
    a = lax.complex(a_re.astype(jnp.float32), a_im.astype(jnp.float32))
    dt = jnp.exp(log_step.astype(jnp.float32))[..., None]
    a_bar = jnp.exp(dt * a)
    b = lax.complex(b_re.astype(jnp.float32), b_im.astype(jnp.float32))
    b_bar = ((a_bar - 1.0) / a)[..., None] * b
    return a_bar, b_bar

def _ssm_combine(left, right):
    a_l, b_l = left
    a_r, b_r = right
    return a_l * a_r, a_r * b_l + b_r

def ssm_scan(a_bar, bu, init, reverse):
    if init is not None:
        idx = -1 if reverse else 0
        bu = bu.at[:, idx].add(a_bar * init)
    a = jnp.broadcast_to(a_bar, (1,) + bu.shape[1:])
    _, s = lax.associative_scan(_ssm_combine, (a, bu), reverse=reverse, axis=1)
    return s

def s5_states(z, a_bar, b_bar, init_f, init_b):
    bsz, n, _ = z.shape
    u = z.astype(jnp.float32).reshape(bsz, n, SSM_GROUPS, SSM_GROUP_W)
    s_f = ssm_scan(a_bar[0], jnp.einsum('blgp,gnp->blgn', u, b_bar[0]), init_f, reverse=False)
    s_b = ssm_scan(a_bar[1], jnp.einsum('blgp,gnp->blgn', u, b_bar[1]), init_b, reverse=True)
    return s_f, s_b

def s5_readout(z, s_f, s_b, c_re, c_im, d, w_glu, b_glu):
    bsz, n, _ = z.shape
    cmat = lax.complex(c_re.astype(jnp.float32), c_im.astype(jnp.float32))
    y = (jnp.einsum('blgn,gpn->blgp', s_f, cmat[0]) + jnp.einsum('blgn,gpn->blgp', s_b, cmat[1])).real
    y = y.reshape(bsz, n, W_SSM) + d.astype(jnp.float32) * z.astype(jnp.float32)
    y = jax.nn.gelu(y).astype(z.dtype)
    return y * jax.nn.sigmoid(y @ w_glu + b_glu)

def merge_branches(h, o_attn, o_f, o_s, lp):
    g = jax.nn.sigmoid(h @ lp["w_gate"] + lp["b_gate"])
    g_a, g_f, g_s = jnp.split(g, N_BRANCH, axis=-1)
    m = (g_a * (o_attn @ lp["w_br_attn"]) + g_f * (o_f @ lp["w_br_fourier"])
         + g_s * (o_s @ lp["w_br_ssm"]))
    return m @ lp["w_out"]

def sq_relu_mlp(h, lp):
    return jnp.square(jax.nn.relu(h @ lp["w_mlp1"])) @ lp["w_mlp2"]

def hybrid_layer(x, xc, ada_lat, ada_ctx, lp, update_ctx):
    bsz, n, _ = x.shape
    sh1, sc1, g1, sh2, sc2, g2 = jnp.split(ada_lat[:, None, :], 6, axis=-1)
    csh1, csc1, cg1, csh2, csc2, cg2 = jnp.split(ada_ctx, 6)
    h = rms_norm(x, lp["ln1"]) * (1.0 + sc1) + sh1
    hc = rms_norm(xc, lp["ln1"]) * (1.0 + csc1) + csh1
    w_in = lp["w_in"]
    f0, s0 = W_ATTN_IN, W_ATTN_IN + W_FOURIER
    z = h @ w_in
    za, zf, zs = z[..., :f0], z[..., f0:s0], z[..., s0:]
    zca = hc @ w_in[:, :f0]
    zcs = hc @ w_in[:, s0:]

    cos, sin = axial_rope_angles(n)
    qn, qr = mla_q(za, lp["q_norm"], lp["w_uq"])
    qr = apply_rope(qr, cos[:, None, :], sin[:, None, :])
    kn, v, kr = mla_kv(za, lp["kv_norm"], lp["w_ukv"])
    kr = apply_rope(kr, cos, sin)
    ckn, cv, ckr = mla_kv(zca, lp["kv_norm"], lp["w_ukv"])
    o_attn = latent_attention(qn, qr, jnp.concatenate([ckn, kn], axis=1),
                              jnp.concatenate([ckr, kr], axis=1), jnp.concatenate([cv, v], axis=1))

    o_f = fourier_mix(zf)

    a_bar, b_bar = s5_discretize(lp["ssm_a_re"], lp["ssm_a_im"], lp["ssm_log_step"],
                                 lp["ssm_b_re"], lp["ssm_b_im"])
    cs_f, cs_b = s5_states(zcs, a_bar, b_bar, None, None)
    s_f, s_b = s5_states(zs, a_bar, b_bar, cs_f[:, -1], cs_b[:, 0])
    o_s = s5_readout(zs, s_f, s_b, lp["ssm_c_re"], lp["ssm_c_im"], lp["ssm_d"], lp["w_glu"], lp["b_glu"])

    x = x + g1 * merge_branches(h, o_attn, o_f, o_s, lp)
    x = x + g2 * sq_relu_mlp(rms_norm(x, lp["ln2"]) * (1.0 + sc2) + sh2, lp)

    if update_ctx:
        lc = xc.shape[1]
        cqn, cqr = mla_q(zca, lp["q_norm"], lp["w_uq"])
        co_attn = attend(cqn, cqr, ckn, ckr, cv).reshape(bsz, lc, N_HEADS * V_HEAD)
        co_f = fourier_mix(hc @ w_in[:, f0:s0])
        co_s = s5_readout(zcs, cs_f, cs_b, lp["ssm_c_re"], lp["ssm_c_im"], lp["ssm_d"],
                          lp["w_glu"], lp["b_glu"])
        xc = xc + cg1 * merge_branches(hc, co_attn, co_f, co_s, lp)
        xc = xc + cg2 * sq_relu_mlp(rms_norm(xc, lp["ln2"]) * (1.0 + csc2) + csh2, lp)
    return x, xc

def setup_inputs(seed: int = 0) -> dict:
    key = jax.random.key(seed)
    ks = iter(jax.random.split(key, 40))
    f32 = jnp.float32

    def nrm(shape, scale):
        return jax.random.normal(next(ks), shape, f32) * scale

    def gain(shape):
        return 1.0 + 0.02 * jax.random.normal(next(ks), shape, f32)

    L = DEPTH
    n_idx = jnp.arange(SSM_STATE, dtype=f32)
    return {
        "x": nrm((BATCH, SEQ, D_MODEL), 1.0),
        "c": nrm((BATCH, D_MODEL), 1.0),
        "ctx": nrm((BATCH, CTX_LEN, D_MODEL), 1.0),
        "c_ctx": nrm((D_MODEL,), 1.0),
        "ada_w": nrm((L, D_MODEL, 6 * D_MODEL), D_MODEL ** -0.5),
        "ada_b": nrm((L, 6 * D_MODEL), 0.02),
        "ln1": gain((L, D_MODEL)),
        "ln2": gain((L, D_MODEL)),
        "w_in": nrm((L, D_MODEL, W_IN), D_MODEL ** -0.5),
        "q_norm": gain((L, Q_LORA)),
        "w_uq": nrm((L, Q_LORA, N_HEADS * (QK_NOPE + QK_ROPE)), Q_LORA ** -0.5),
        "kv_norm": gain((L, KV_LORA)),
        "w_ukv": nrm((L, KV_LORA, N_HEADS * (QK_NOPE + V_HEAD)), KV_LORA ** -0.5),
        "ssm_a_re": -0.5 + nrm((L, 2, SSM_GROUPS, SSM_STATE), 0.01),
        "ssm_a_im": jnp.pi * n_idx + nrm((L, 2, SSM_GROUPS, SSM_STATE), 0.01),
        "ssm_log_step": jax.random.uniform(next(ks), (L, 2, SSM_GROUPS), f32,
                                           minval=math.log(1e-3), maxval=math.log(1e-1)),
        "ssm_b_re": nrm((L, 2, SSM_GROUPS, SSM_STATE, SSM_GROUP_W), (2 * SSM_GROUP_W) ** -0.5),
        "ssm_b_im": nrm((L, 2, SSM_GROUPS, SSM_STATE, SSM_GROUP_W), (2 * SSM_GROUP_W) ** -0.5),
        "ssm_c_re": nrm((L, 2, SSM_GROUPS, SSM_GROUP_W, SSM_STATE), 0.5),
        "ssm_c_im": nrm((L, 2, SSM_GROUPS, SSM_GROUP_W, SSM_STATE), 0.5),
        "ssm_d": nrm((L, W_SSM), 1.0),
        "w_glu": nrm((L, W_SSM, W_SSM), W_SSM ** -0.5),
        "b_glu": nrm((L, W_SSM), 0.02),
        "w_br_attn": nrm((L, N_HEADS * V_HEAD, D_MODEL), (N_HEADS * V_HEAD) ** -0.5),
        "w_br_fourier": nrm((L, W_FOURIER, D_MODEL), W_FOURIER ** -0.5),
        "w_br_ssm": nrm((L, W_SSM, D_MODEL), W_SSM ** -0.5),
        "w_gate": nrm((L, D_MODEL, N_BRANCH * D_MODEL), D_MODEL ** -0.5),
        "b_gate": nrm((L, N_BRANCH * D_MODEL), 0.02),
        "w_out": nrm((L, D_MODEL, D_MODEL), D_MODEL ** -0.5),
        "w_mlp1": nrm((L, D_MODEL, D_FF), D_MODEL ** -0.5),
        "w_mlp2": nrm((L, D_FF, D_MODEL), D_FF ** -0.5),
        "final_norm": gain((D_MODEL,)),
    }

def reference(x, c, ctx, c_ctx, ada_w, ada_b, ln1, ln2, w_in, q_norm, w_uq, kv_norm, w_ukv,
              ssm_a_re, ssm_a_im, ssm_log_step, ssm_b_re, ssm_b_im, ssm_c_re, ssm_c_im, ssm_d,
              w_glu, b_glu, w_br_attn, w_br_fourier, w_br_ssm, w_gate, b_gate, w_out,
              w_mlp1, w_mlp2, final_norm):
    xc = ctx
    silu_c = jax.nn.silu(c)
    silu_cc = jax.nn.silu(c_ctx)
    for l in range(DEPTH):
        ada_lat = silu_c @ ada_w[l] + ada_b[l]
        ada_ctx = silu_cc @ ada_w[l] + ada_b[l]
        lp = dict(ln1=ln1[l], ln2=ln2[l], w_in=w_in[l], q_norm=q_norm[l], w_uq=w_uq[l],
                  kv_norm=kv_norm[l], w_ukv=w_ukv[l], ssm_a_re=ssm_a_re[l], ssm_a_im=ssm_a_im[l],
                  ssm_log_step=ssm_log_step[l], ssm_b_re=ssm_b_re[l], ssm_b_im=ssm_b_im[l],
                  ssm_c_re=ssm_c_re[l], ssm_c_im=ssm_c_im[l], ssm_d=ssm_d[l], w_glu=w_glu[l],
                  b_glu=b_glu[l], w_br_attn=w_br_attn[l], w_br_fourier=w_br_fourier[l],
                  w_br_ssm=w_br_ssm[l], w_gate=w_gate[l], b_gate=b_gate[l], w_out=w_out[l],
                  w_mlp1=w_mlp1[l], w_mlp2=w_mlp2[l])
        x, xc = hybrid_layer(x, xc, ada_lat, ada_ctx, lp, update_ctx=(l < DEPTH - 1))
    return rms_norm(x, final_norm)


_drawn_inputs = setup_inputs


def setup_inputs(seed=0):
    import zlib

    import numpy as np

    out = dict(_drawn_inputs(seed))
    spreads = {}
    factors = {'ln1': 6.682,
     'ln2': 2.732,
     'q_norm': 8.0,
     'kv_norm': 8.0,
     'ssm_a_re': 8.0,
     'b_glu': 8.0,
     'b_gate': 8.0,
     'final_norm': 2.888}
    for name, (base, spread) in spreads.items():
        noise = np.random.default_rng([zlib.crc32(name.encode()), seed]).standard_normal(out[name].shape)
        drawn = base * np.exp(spread * noise) if base else spread * noise
        out[name] = __import__('jax').numpy.asarray(drawn.astype(out[name].dtype))
    for name, factor in factors.items():
        out[name] = (out[name] * factor).astype(out[name].dtype)
    return out
```

```python
from contextlib import ExitStack

import numpy as np

import concourse.bass as bass
from concourse import mybir

F32 = mybir.dt.float32
F32R = mybir.dt.float32r
ALU = mybir.AluOpType
ACT = mybir.ActivationFunctionType
AXX = mybir.AxisListType.X

P = 128
D = 1024
KD = D // P
LAT, CTX = 512, 256
TOK = LAT + CTX
DEPTH = 2
HEADS = 8
NOPE, ROPE, VH = 64, 32, 64
QL, KVL = 384, 256
KQ, KKV = QL // P, KVL // P
SCALE = 1.0 / float(np.sqrt(NOPE + ROPE))
GROUPS, GP, NS = 24, 16, 64
CH = 8
NC = TOK // CH
NCL, NCC = LAT // CH, CTX // CH
EPS = 1e-6
N_IN, N_MERGE, N_OUT, QUARTERS = 12, 40, 8, 4
N_TILES = N_IN + N_MERGE + N_OUT + QUARTERS * 16
RAW_SLOTS, W_SLOTS = 2, 4
ADA_TILES = 48


class Signal:

    def __init__(self, sem, book):
        self.sem, self.book, self.new = sem, book, {}
        self.n, self.body, self.turns = 0, None, 1

    def mark(self, key, by=1):
        self.n += by
        self.new[key] = (self.n, self.body)
        return by

    def at(self, key, turn=0):
        n, body = self.book.get(key, (1, None))
        if body is not None:
            n = turn * self.book["loop", body] + n
        return n

    def start_loop(self, name):
        self.body, self.first = name, self.n

    def end_loop(self, turns):
        k = self.n - self.first
        self.new["loop", self.body] = k
        self.n += (turns - 1) * k
        self.body = None


def build(nc, A, out, book):
    ctx = ExitStack()
    with ctx:
        BASE = 16512
        CONST, RING = BASE, BASE + 8192
        HREG = RING + (RAW_SLOTS + 2 * W_SLOTS) * KD * P * 4
        REST = HREG + 2 * KD * TOK * 4

        def at(name, off, shape, dt=F32):
            return nc.alloc_sbuf_tensor_at(name, shape, dt, offset=off)

        place = [CONST]

        def const(name, shape):
            t = at(name, place[0], shape)
            n = 4
            for s in shape[1:]:
                n *= s
            place[0] += -(-n // 32) * 32
            assert place[0] <= RING
            return t

        ident = const("ident", [P, P])
        ones = const("ones", [P, P])
        rope = const("rope", [P, TOK])
        ada = const("ada", [P, DEPTH, ADA_TILES, 2])
        ada_b = const("ada_b", [P, DEPTH, ADA_TILES])
        ln = const("ln", [P, DEPTH, 2, KD])
        gain = const("gain", [P, DEPTH, 2, KD, 2])
        fnorm = const("fnorm", [P, KD])
        qkn = const("qkn", [P, DEPTH, KQ + KKV])
        b_gate = const("b_gate", [P, DEPTH, 3 * KD])
        b_glu = const("b_glu", [P, DEPTH, 3])
        ssm_d = const("ssm_d", [P, DEPTH, 3])
        cvec = const("cvec", [P, KD, 2])
        svec = const("svec", [P, KD, 2])
        eps_col = const("eps_col", [P, 1])
        a8r = const("a8r", [P, DEPTH, 2, GROUPS])
        a8i = const("a8i", [P, DEPTH, 2, GROUPS])
        sc_t1 = const("sc_t1", [P, 2, GROUPS])
        sc_t2 = const("sc_t2", [P, 2, GROUPS])
        mx = const("mx", [P, 4])
        nmx = const("nmx", [P, 4])
        sm = const("sm", [P, 4])
        rsm = const("rsm", [P, 4])

        raw = at("raw", RING, [P, RAW_SLOTS, KD * P])
        whi = at("whi", RING + RAW_SLOTS * 4096, [P, W_SLOTS, KD * P], F32R)
        wlo = at("wlo", RING + (RAW_SLOTS + W_SLOTS) * 4096, [P, W_SLOTS, KD * P], F32R)
        hh = at("hh", HREG, [P, KD, TOK], F32R)
        hl = at("hl", HREG + KD * TOK * 4, [P, KD, TOK], F32R)

        def rest(name, off, shape, dt=F32):
            return at(name, REST + off, shape, dt)

        zq = rest("zq", 0, [P, KQ, TOK])
        zkv = rest("zkv", 9216, [P, KKV, TOK])
        kk = rest("kk", 15360, [P, 2, TOK])
        zf = rest("zf", 21504, [P, 3, TOK])
        of = rest("of", 21504, [P, 3, TOK])
        zs = rest("zs", 30720, [P, 3, CH, NC])
        us = rest("us", 39936, [P, GROUPS, NC])
        osm = rest("osm", 39936, [P, 3, TOK])
        snat = rest("snat", 49152, [P, 2, GROUPS, NC])
        yp = rest("yp", 49152, [P, 3, TOK])
        yg = rest("yg", 58368, [P, 3, TOK])
        ss = rest("ss", 67584, [P, NC + 1, 2, GROUPS])
        bint = rest("bint", 89088, [P, GROUPS, 2, P])
        cout = rest("cout", 89088, [P, 2, GROUPS, P])
        toep = rest("toep", 67584, [P, GROUPS, P])
        wglu = rest("wglu", 79872, [P, 3, 3 * P])
        sig = rest("sig", 84480, [P, TOK])
        pq = rest("pq", 49152, [P, TOK // P, 3, 2 * P])
        dft_l = rest("dft_l", 67584, [P, LAT // P, 2, LAT])
        dft_c = rest("dft_c", 83968, [P, CTX // P, 2, CTX])
        c64 = rest("c64", 88064, [P, 2 * P])
        qq = rest("qq", 49152, [P, 2, TOK])
        vv = rest("vv", 55296, [P, TOK // P, P])
        pr = rest("pr", 58368, [P, 3, TOK])
        pt = rest("pt", 67584, [P, TOK // P, LAT])
        pw = rest("pw", 79872, [P, 1280])
        rt = rest("rt", 84992, [P, TOK])
        rt_k = rest("rt_k", 39936, [P, TOK])
        oah = rest("oah", 89088, [P, 4, TOK], F32R)
        oal = rest("oal", 89088 + 12288, [P, 4, TOK], F32R)
        m_sb = rest("m_sb", 0, [P, KD, TOK])
        gt = rest("gt", 24576, [P, 2, TOK])
        acc = rest("acc", 30720, [P, TOK])
        tmp = rest("tmp", 33792, [P, TOK])
        osh = rest("osh", 49152, [P, 3, TOK], F32R)
        osl = rest("osl", 58368, [P, 3, TOK], F32R)
        ofh = rest("ofh", 67584, [P, 3, TOK], F32R)
        ofl = rest("ofl", 76800, [P, 3, TOK], F32R)
        x = rest("x", 49152, [P, KD, TOK])
        nt = rest("nt", 0, [P, 2, TOK])
        sqt = rest("sqt", 6144, [P, 2, TOK])
        rstd = rest("rstd", 12288, [P, TOK])
        sq_s = rest("sq_s", 49152, [P, 2, TOK])
        rs_s = rest("rs_s", 55296, [P, TOK])
        midh = rest("midh", 0, [P, KD, TOK], F32R)
        midl = rest("midl", 24576, [P, KD, TOK], F32R)
        mr = rest("mr", 73728, [P, 2, TOK])
        ms = rest("ms", 79872, [P, 2, TOK])
        xo = rest("xo", 73728, [P, KD, LAT])
        t1 = rest("t1", 0, [P, 3072])
        t2 = rest("t2", 12288, [P, 3072])
        bin_ = rest("bin", 24576, [P, 2, GROUPS, CH, GP])
        binT = rest("binT", 49152, [P, GROUPS, 2, P])
        cz = rest("cz", 73728, [P, 2, 12, 15, GP])
        b_in = rest("b_in", 96768, [P, 2, GROUPS, GP])
        c_in = rest("c_in", 99840, [P, 2, GROUPS, GP])
        bb = rest("bb", 102912, [P, 2, GROUPS, GP])
        pw8 = rest("pw8", 105984, [P, CH + 1, 2, GROUPS])
        p_in = rest("p_in", 107712, [P, CH, 2, GROUPS])
        p_out = rest("p_out", 109248, [P, CH, 2, GROUPS])
        p_z = rest("p_z", 110784, [P, 15, 2, GROUPS])
        vsb = at("vsb", HREG, [GP, GROUPS, 15 * GP])
        ada_w = at("ada_w", HREG + 23040, [P, 4, D])
        abuf = at("abuf", HREG + 39424, [P, 24, GROUPS])

        ps = ctx.enter_context(nc.psum_tensor("ps", [P, 4, 1024], F32))

        def dram(name, shape):
            return nc.dram_tensor(name, shape, F32, kind="Internal").ap()

        bin_d = dram("bin_d", (DEPTH, P, GROUPS * 2 * P))
        cout_d = dram("cout_d", (DEPTH, P, GROUPS * 2 * P))
        toep_d = dram("toep_d", (DEPTH, P, GROUPS, P))
        zs_d = dram("zs_d", (DEPTH, 3, P, TOK))
        y_d = dram("y_d", (DEPTH, GROUPS, GP, CH, NC))
        x_d = dram("x_d", (P, KD, TOK))

        signals = []

        def signal(name):
            signals.append(Signal(ctx.enter_context(nc.semaphore(name)), book.setdefault(name, {})))
            signals[-1].name = name
            return signals[-1]

        consts_in = signal("consts_in")
        cvec_in = signal("cvec_in")
        ada_used = signal("ada_used")
        ada_ready = signal("ada_ready")
        silu_ready = signal("silu_ready")
        w_turn = signal("w_turn")
        w_split = signal("w_split")
        w_used = signal("w_used")
        ones_ready = signal("ones_ready")
        ada_full = [signal(f"ada_full{u}") for u in range(4)]
        raw_full = [signal(f"raw_full{u}") for u in range(RAW_SLOTS)]
        prep_loaded = signal("prep_loaded")
        prep_act = signal("prep_act")
        prep_dve = signal("prep_dve")
        prep_pe = signal("prep_pe")
        prep_stored = signal("prep_stored")
        prep_v_stored = signal("prep_v_stored")
        x_in = signal("x_in")
        x_spilled = signal("x_spilled")
        sq_ready = signal("sq_ready")
        sq_used = signal("sq_used")
        rms_ready = signal("rms_ready")
        rstd_ready = signal("rstd_ready")
        nt_ready = signal("nt_ready")
        hi_ready = signal("hi_ready")
        lo_ready = signal("lo_ready")
        in_act = signal("in_act")
        in_dve = signal("in_dve")
        ropes = signal("ropes")
        sn_sq = signal("sn_sq")
        sn_used = signal("sn_used")
        sn_root = signal("sn_root")
        sn_scale = signal("sn_scale")
        dft_in = signal("dft_in")
        fr_a = signal("fr_a")
        fr_pq = signal("fr_pq")
        fr_b = signal("fr_b")
        fr_evac = signal("fr_evac")
        zs_stored = signal("zs_stored")
        us_in = signal("us_in")
        bint_in = signal("bint_in")
        cout_in = signal("cout_in")
        toep_in = signal("toep_in")
        glu_w_in = signal("glu_w_in")
        bu_done = signal("bu_done")
        bu_act = signal("bu_act")
        bu_dve = signal("bu_dve")
        scan = signal("scan")
        snat_act = signal("snat_act")
        snat_dve = signal("snat_dve")
        y_done = signal("y_done")
        y_evac = signal("y_evac")
        y_stored = signal("y_stored")
        y_in = signal("y_in")
        y_skip = signal("y_skip")
        gelu = signal("gelu")
        glu_done = signal("glu_done")
        glu_sig = signal("glu_sig")
        os_ready = signal("os_ready")
        pw_in = signal("pw_in")
        q_done = signal("q_done")
        q_act = signal("q_act")
        k_done = signal("k_done")
        k_act = signal("k_act")
        v_done = signal("v_done")
        v_act = signal("v_act")
        sc_done = signal("sc_done")
        max_ready = signal("max_ready")
        nmax_ready = signal("nmax_ready")
        exp_ready = signal("exp_ready")
        rsum_ready = signal("rsum_ready")
        p_ready = signal("p_ready")
        pt_done = signal("pt_done")
        pt_evac = signal("pt_evac")
        pv_done = signal("pv_done")
        oh_ready = signal("oh_ready")
        ol_ready = signal("ol_ready")
        mh_ready = signal("mh_ready")
        ml_ready = signal("ml_ready")
        g_ready = signal("g_ready")
        br_done = signal("br_done")
        br_dve = signal("br_dve")
        m_ready = signal("m_ready")
        msplit_h = signal("msplit_h")
        msplit_l = signal("msplit_l")
        x_add = signal("x_add")
        relu_ready = signal("relu_ready")
        midh_ready = signal("midh_ready")
        msq_ready = signal("msq_ready")
        midl_ready = signal("midl_ready")
        fin_ready = signal("fin_ready")
        out_stored = signal("out_stored")

        def pair(p, n):
            return ps[:, p % 4, 0:n]

        def spans(n):
            return [(0, 512)] + ([(512, 768)] if n > 512 else [])

        def product(pe, p, w, kts, xh, xl, n, first, last):
            ins = None
            for i, (kw, kx) in enumerate(kts):
                for j, (ww, xx) in enumerate(((whi, xh), (whi, xl), (wlo, xh))):
                    for a, b in spans(n):
                        ins = pe.matmul(ps[:, p % 4, a:b], ww[:, w % W_SLOTS, kw * P:(kw + 1) * P],
                                        xx[:, kx, a:b], start=(first and i == 0 and j == 0),
                                        stop=(last and i == len(kts) - 1 and j == 2))
            return ins

        def wait_w(pe, t):
            pe.wait_ge(w_split.sem, 2 * (t + 1))

        def pe_rms(pe, key, n):
            for k in range(KD):
                pe.wait_ge(sq_ready.sem, sq_ready.at((key, k)))
                for a, b in spans(n):
                    ins = pe.matmul(ps[:, 3, a:b], ones[:, :], sqt[:, k % 2, a:b], start=(k == 0), stop=(k == KD - 1))
                ins.then_inc(sq_used.sem, sq_used.mark((key, k)))

        def pe_layer(pe, l):
            n = TOK if l == 0 else LAT
            t0 = l * N_TILES
            pe_rms(pe, (l, 1), TOK)
            pe.wait_ge(lo_ready.sem, lo_ready.at((l, 1, KD - 1)))
            for i in range(N_IN):
                w = t0 + i
                wait_w(pe, w)
                if i >= 4:
                    if i == 6:
                        pe.wait_ge(ropes.sem, ropes.at(("k", l, 3)))
                    elif i - 4 in (3, 4, 5):
                        pe.wait_ge(in_dve.sem, in_dve.at((l, i - 4)))
                    else:
                        pe.wait_ge(in_act.sem, in_act.at((l, i - 4)))
                ins = product(pe, i, w, [(k, k) for k in range(KD)], hh, hl, TOK if i < 6 else n, True, True)
                ins.then_inc(w_used.sem, w_used.mark(w))
            pe.wait_ge(in_act.sem, in_act.at((l, N_IN - 1)))
            pe.wait_ge(in_dve.sem, in_dve.at((l, 5)))
            for q, (kts, m) in enumerate(((KQ, n), (KKV, TOK))):
                for k in range(kts):
                    pe.wait_ge(sn_sq.sem, sn_sq.at((l, q, k)))
                    for a, b in spans(m):
                        ins = pe.matmul(ps[:, q, a:b], ones[:, :], sq_s[:, k % 2, a:b],
                                        start=(k == 0), stop=(k == kts - 1))
                    ins.then_inc(sn_used.sem, sn_used.mark((l, q, k)))
            pe.wait_ge(dft_in.sem, dft_in.at(l))
            blocks = range(n // P)
            for b in blocks:
                if b >= 2:
                    pe.wait_ge(fr_pq.sem, fr_pq.at((l, b - 2)))
                for i in range(3):
                    ins = pe.matmul(ps[:, 2 + b % 2, i * 256:i * 256 + 256], zf[:, i, b * P:b * P + P],
                                    c64[:, :], start=True, stop=True)
                ins.then_inc(fr_a.sem, fr_a.mark((l, b)))
            pe.wait_ge(fr_pq.sem, fr_pq.at((l, len(blocks) - 1)))
            pe.wait_ge(sn_root.sem, sn_root.at((l, 1)))
            for i in range(3):
                for (a, e), tab, b0, nb in ((spans(n)[0], dft_l, 0, 4),) + (((512, 768), dft_c, 4, 2),) * (n > 512):
                    for b in range(nb):
                        for cs in range(2):
                            ins = pe.matmul(ps[:, i, a:e], pq[:, b0 + b, i, cs * P:cs * P + P], tab[:, b, cs, :],
                                            start=(b == 0 and cs == 0), stop=(b == nb - 1 and cs == 1))
                ins.then_inc(fr_b.sem, fr_b.mark((l, i)))
            pe.wait_ge(us_in.sem, us_in.at((l, CH - 1)))
            pe.wait_ge(bint_in.sem, bint_in.at(l))
            pe.wait_ge(fr_evac.sem, fr_evac.at((l, 2)))
            for q in range(6):
                if q >= 2:
                    pe.wait_ge(bu_act.sem, bu_act.at((l, q - 2)))
                    pe.wait_ge(bu_dve.sem, bu_dve.at((l, q - 2)))
                for ri in range(2):
                    for j in range(4):
                        g = 4 * q + j
                        ins = pe.matmul(ps[:, q % 2, ri * 512 + j * NC:ri * 512 + (j + 1) * NC], bint[:, g, ri, :],
                                        us[:, g, :], start=True, stop=True)
                ins.then_inc(bu_done.sem, bu_done.mark((l, q)))
            pe.wait_ge(snat_act.sem, snat_act.at(l))
            pe.wait_ge(snat_dve.sem, snat_dve.at(l))
            pe.wait_ge(cout_in.sem, cout_in.at(l))
            pe.wait_ge(toep_in.sem, toep_in.at(l))
            for q in range(6):
                if q >= 2:
                    pe.wait_ge(y_evac.sem, y_evac.at((l, q - 2)))
                for j in range(4):
                    g = 4 * q + j
                    o = ps[:, 2 + q % 2, j * NC:(j + 1) * NC]
                    pe.matmul(o, cout[:, 0, g, :], snat[:, 0, g, :], start=True, stop=False)
                    pe.matmul(o, cout[:, 1, g, :], snat[:, 1, g, :], start=False, stop=False)
                    ins = pe.matmul(o, toep[:, g, :], us[:, g, :], start=False, stop=True)
                ins.then_inc(y_done.sem, y_done.mark((l, q)))
            pe.wait_ge(gelu.sem, gelu.at(l))
            pe.wait_ge(glu_w_in.sem, glu_w_in.at(l))
            for o in range(3):
                if o == 2:
                    pe.wait_ge(glu_sig.sem, glu_sig.at((l, 0)))
                for k in range(3):
                    for a, b in spans(TOK):
                        ins = pe.matmul(ps[:, o % 2, a:b], wglu[:, k, o * P:o * P + P], yg[:, k, a:b],
                                        start=(k == 0), stop=(k == 2))
                ins.then_inc(glu_done.sem, glu_done.mark((l, o)))
            pe.wait_ge(glu_sig.sem, glu_sig.at((l, 2)))
            nq = n // P
            pe.wait_ge(sn_scale.sem, sn_scale.at(l))
            for h2 in range(4):
                pe.wait_ge(pw_in.sem, pw_in.at((l, h2)))
                if h2:
                    pe.wait_ge(ol_ready.sem, ol_ready.at((l, h2 - 1)))
                for j in range(2):
                    for k in range(KQ):
                        for a, b in spans(n):
                            ins = pe.matmul(ps[:, j, a:b], pw[:, (j * KQ + k) * P:(j * KQ + k + 1) * P], zq[:, k, a:b],
                                            start=(k == 0), stop=(k == KQ - 1))
                    ins.then_inc(q_done.sem, q_done.mark((l, h2, j)))
                for k in range(KKV):
                    for a, b in spans(TOK):
                        ins = pe.matmul(ps[:, 2, a:b], pw[:, (6 + k) * P:(7 + k) * P], zkv[:, k, a:b],
                                        start=(k == 0), stop=(k == KKV - 1))
                ins.then_inc(k_done.sem, k_done.mark((l, h2)))
                for b in range(TOK // P):
                    for k in range(KKV):
                        ins = pe.matmul(ps[:, 3, b * P:b * P + P], zkv[:, k, b * P:b * P + P],
                                        pw[:, (8 + k) * P:(9 + k) * P], start=(k == 0), stop=(k == KKV - 1),
                                        skip_group_check=True)
                ins.then_inc(v_done.sem, v_done.mark((l, h2)))
                pe.wait_ge(ropes.sem, ropes.at(("q", l, h2, 1, 2)))
                pe.wait_ge(q_act.sem, q_act.at((l, h2, 1)))
                pe.wait_ge(k_act.sem, k_act.at((l, h2)))
                pe.wait_ge(v_act.sem, v_act.at((l, h2)))
                units = [(j, b) for j in range(2) for b in range(nq)]

                def scores(u):
                    j, b = units[u]
                    if u >= 2:
                        pe.wait_ge(exp_ready.sem, exp_ready.at((l, h2, u - 2)))
                    keys = spans(TOK) if b < 4 else [(512, 768)]
                    for a, e in keys:
                        ins = pe.matmul(ps[:, u % 2, a:e], qq[0:96, j, b * P:b * P + P], kk[0:96, j, a:e],
                                        start=True, stop=True)
                    ins.then_inc(sc_done.sem, sc_done.mark((l, h2, u)))

                scores(0)
                for u, (j, b) in enumerate(units):
                    if u + 1 < len(units):
                        scores(u + 1)
                    pe.wait_ge(p_ready.sem, p_ready.at((l, h2, u)))
                    if u >= 1:
                        pe.wait_ge(pt_evac.sem, pt_evac.at((l, h2, u - 1)))
                    kb = range(6) if b < 4 else range(4, 6)
                    for c in kb:
                        ins = pe.transpose(ps[:, 2, c * P:c * P + P], pr[:, u % 3, c * P:c * P + P], ident[:, :])
                    ins.then_inc(pt_done.sem, pt_done.mark((l, h2, u)))
                    if b == 3 or b == 5:
                        pe.wait_ge(pt_evac.sem, pt_evac.at((l, h2, u)))
                        o = ps[j * VH:(j + 1) * VH, 3, 0:512] if b == 3 else ps[j * VH:(j + 1) * VH, 3, 512:768]
                        for c in kb:
                            ins = pe.matmul(o, vv[:, c, j * VH:(j + 1) * VH], pt[:, c, 0:(512 if b == 3 else 256)],
                                            start=(c == kb[0]), stop=(c == 5))
                        ins.then_inc(pv_done.sem, pv_done.mark((l, h2, j, b)))
            pe.wait_ge(ol_ready.sem, ol_ready.at((l, 3)))
            pe.wait_ge(ml_ready.sem, ml_ready.at(l))
            for m in range(KD):
                t = t0 + N_IN + 5 * m
                seq = 6 * m
                full = [(k, k) for k in range(KD)]

                def free(i):
                    if i < 4:
                        return
                    mm, r = divmod(i - 4, 6)
                    if r in (0, 3, 5):
                        pe.wait_ge(g_ready.sem, g_ready.at((l, mm, (0, 3, 5).index(r))))
                    else:
                        pe.wait_ge(br_dve.sem, br_dve.at((l, mm, (1, 2, 4).index(r))))

                free(seq)
                wait_w(pe, t)
                product(pe, seq, t, full, hh, hl, n, True, True).then_inc(w_used.sem, w_used.mark(t))
                free(seq + 1)
                free(seq + 2)
                wait_w(pe, t + 1)
                product(pe, seq + 1, t + 1, [(k, k) for k in range(4)], oah, oal, n, True, True).then_inc(
                    br_done.sem, br_done.mark((l, m, 0)))
                product(pe, seq + 2, t + 1, [(4, 0)], osh, osl, n, True, False).then_inc(w_used.sem, w_used.mark(t + 1))
                free(seq + 3)
                wait_w(pe, t + 2)
                product(pe, seq + 3, t + 2, full, hh, hl, n, True, True).then_inc(w_used.sem, w_used.mark(t + 2))
                free(seq + 4)
                wait_w(pe, t + 3)
                product(pe, seq + 2, t + 3, [(0, 1), (1, 2)], osh, osl, n, False, True).then_inc(
                    br_done.sem, br_done.mark((l, m, 1)))
                product(pe, seq + 4, t + 3, [(2, 0), (3, 1), (4, 2)], ofh, ofl, n, True, True).then_inc(
                    w_used.sem, w_used.mark(t + 3))
                free(seq + 5)
                wait_w(pe, t + 4)
                product(pe, seq + 5, t + 4, full, hh, hl, n, True, True).then_inc(w_used.sem, w_used.mark(t + 4))
            pe.wait_ge(m_ready.sem, m_ready.at((l, KD - 1)))
            for m in range(N_OUT):
                w = t0 + N_IN + N_MERGE + m
                if m == 0:
                    pe.wait_ge(msplit_l.sem, msplit_l.at((l, KD - 1)))
                wait_w(pe, w)
                if m >= 4:
                    pe.wait_ge(x_add.sem, x_add.at((l, m - 4)))
                product(pe, m, w, [(k, k) for k in range(KD)], hh, hl, n, True, True).then_inc(
                    w_used.sem, w_used.mark(w))
            pe.wait_ge(x_add.sem, x_add.at((l, KD - 1)))
            pe_rms(pe, (l, 2), n)
            pe.wait_ge(lo_ready.sem, lo_ready.at((l, 2, KD - 1)))
            base = t0 + N_IN + N_MERGE + N_OUT
            w_used.start_loop((l, "mlp"))
            with pe.Fori(0, QUARTERS) as i:
                for m in range(KD):
                    pe.wait_ge(w_split.sem, i * 32 + 2 * (base + m + 1))
                    if m >= 4:
                        pe.wait_ge(relu_ready.sem, relu_ready.at((l, m - 4), i))
                    else:
                        pe.wait_ge(x_add.sem, i * KD + (x_add.book.get((l, KD - 1), (1,))[0]))
                    product(pe, m, m, [(k, k) for k in range(KD)], hh, hl, n, True, True).then_inc(
                        w_used.sem, w_used.mark((l, "m1", m)))
                for m in range(KD):
                    pe.wait_ge(w_split.sem, i * 32 + 2 * (base + KD + m + 1))
                    if m == 0:
                        pe.wait_ge(midl_ready.sem, midl_ready.at((l, KD - 1), i))
                    if m >= 4:
                        pe.wait_ge(x_add.sem, x_add.at((l, "mlp", m - 4), i))
                    product(pe, m, KD + m, [(k, k) for k in range(KD)], midh, midl, n, True, True).then_inc(
                        w_used.sem, w_used.mark((l, "m2", m)))
            w_used.end_loop(QUARTERS)
            pe.wait_ge(x_add.sem, x_add.at((l, "mlp", KD - 1), QUARTERS - 1))

        block = ctx.enter_context(nc.Block())

        @block.tensor
        def _(pe):
            pe.wait_ge(consts_in.sem, consts_in.at(0))
            pe.wait_ge(silu_ready.sem, silu_ready.at(0))
            ada_used.start_loop("ada")
            with pe.Fori(0, DEPTH * ADA_TILES // 4) as i:
                for u in range(4):
                    pe.wait_ge(ada_full[u].sem, i * 16 + 16)
                    o = ps[:, 3, 0:DEPTH * ADA_TILES * 2].rearrange("p (a b c) -> p a b c", b=4, c=2)
                    for k in range(KD):
                        ins = pe.matmul(o[:, i, u, :], ada_w[:, u, k * P:(k + 1) * P], svec[:, k, :],
                                        start=(k == 0), stop=(k == KD - 1), skip_group_check=True)
                    ins.then_inc(ada_used.sem, ada_used.mark(u))
            ada_used.end_loop(DEPTH * ADA_TILES // 4)
            for l in range(DEPTH):
                pe.wait_ge(prep_dve.sem, prep_dve.at((l, "bin")))
                for q in range(GROUPS // 2):
                    if q >= 2:
                        pe.wait_ge(prep_act.sem, prep_act.at((l, "binT", q - 2)))
                    for j in range(2):
                        for ri in range(2):
                            ins = pe.transpose(ps[:, q % 2, (2 * j + ri) * P:(2 * j + ri + 1) * P],
                                               bin_[:, ri, 2 * q + j, :, :].rearrange("p s q -> p (s q)"), ident[:, :])
                    ins.then_inc(prep_pe.sem, prep_pe.mark((l, "binT", q)))
                pe.wait_ge(prep_act.sem, prep_act.at((l, "binT", GROUPS // 2 - 1)))
                for half in range(2):
                    pe.wait_ge(prep_dve.sem, prep_dve.at((l, f"cz{half}")))
                    for q in range(6):
                        if q >= 2:
                            pe.wait_ge(prep_act.sem, prep_act.at((l, "v", half, q - 2)))
                        for j in range(2):
                            g = 12 * half + 2 * q + j
                            for ri in range(2):
                                ins = pe.matmul(ps[0:GP, q % 2, j * 240:j * 240 + 240], bb[:, ri, g, :],
                                                cz[:, ri, 2 * q + j, :, :].rearrange("p a b -> p (a b)"),
                                                start=(ri == 0), stop=(ri == 1))
                        ins.then_inc(prep_pe.sem, prep_pe.mark((l, "v", half, q)))
                    pe.wait_ge(prep_act.sem, prep_act.at((l, "v", half, 5)))
            pe.wait_ge(ada_ready.sem, ada_ready.at(1))
            for l in range(DEPTH):
                pe_layer(pe, l)
            pe_rms(pe, (DEPTH, 1), LAT)

        w_main = A["w_main"]
        n_all = DEPTH * N_TILES

        @block.sync
        def _(sp):
            ada4 = A["ada_w"].rearrange("(a b) p n -> a b p n", b=4)
            for u in range(4):
                sp.dma_start(ada_w[:, u, :], ada4[0, u]).then_inc(ada_full[u].sem, ada_full[u].mark(u, 16))
            with sp.Fori(1, DEPTH * ADA_TILES // 4) as i:
                for u in range(4):
                    sp.wait_ge(ada_used.sem, i * 4 + (u - 3))
                    sp.dma_start(ada_w[:, u, :], ada4[i, u]).then_inc(ada_full[u].sem, 16)
            w2 = w_main.rearrange("(a b) p n -> a b p n", b=RAW_SLOTS)
            for u in range(RAW_SLOTS):
                sp.dma_start(raw[:, u, :], w2[0, u]).then_inc(raw_full[u].sem, 16)
            with sp.Fori(1, n_all // RAW_SLOTS) as i:
                for u in range(RAW_SLOTS):
                    sp.wait_ge(w_split.sem, i * 4 + (2 * u - 2))
                    sp.dma_start(raw[:, u, :], w2[i, u]).then_inc(raw_full[u].sem, 16)

        @block.gpsimd
        def _(pool):
            def split(t0, u, i):
                pool.wait_ge(raw_full[u % 2].sem, i * 32 + 16 * (u // 2 + 1))
                if t0:
                    pool.wait_ge(w_used.sem, i * 4 + (u - 3))
                pool.sem_inc(w_turn.sem, 1)
                pool.tensor_scalar(whi[:, u, :], raw[:, u % 2, :], 1.0, 0.0, ALU.mult, ALU.add).then_inc(w_split.sem, 1)
                pool.wait_ge(w_split.sem, i * 8 + (2 * u + 1))
                pool.tensor_tensor(wlo[:, u, :], raw[:, u % 2, :], whi[:, u, :].bitcast(F32), ALU.subtract).then_inc(
                    w_split.sem, 1)

            for u in range(W_SLOTS):
                split(False, u, 0)
            with pool.Fori(1, n_all // W_SLOTS) as i:
                for u in range(W_SLOTS):
                    split(True, u, i)

        def act_rms(act, key, n):
            for k in range(KD):
                if k >= 2:
                    act.wait_ge(sq_used.sem, sq_used.at((key, k - 2)))
                act.activation(sqt[:, k % 2, 0:n], x[:, k, 0:n], ACT.Square).then_inc(
                    sq_ready.sem, sq_ready.mark((key, k)))
            act.wait_ge(sq_used.sem, sq_used.at((key, KD - 1)))
            act.activation(rstd[:, 0:n], ps[:, 3, 0:n], ACT.Sqrt, bias=eps_col[:, 0:1],
                                              scale=1.0 / D).then_inc(rms_ready.sem, rms_ready.mark(key))

        def act_norm(act, l, w, n):
            act_rms(act, (l, w), n)
            row = 0 if w == 1 else 3
            for k in range(KD):
                act.wait_ge(nt_ready.sem, nt_ready.at((l, w, k)))
                for s, (a, b) in enumerate(spans(n)):
                    ins = act.activation(hh[:, k, a:b], nt[:, k % 2, a:b], ACT.Identity,
                                         bias=ada[:, l, row * KD + k, s:s + 1])
                ins.then_inc(hi_ready.sem, hi_ready.mark((l, w, k)))

        def act_layer(act, l):
            n = TOK if l == 0 else LAT
            act_norm(act, l, 1, TOK)
            act.wait_ge(lo_ready.sem, lo_ready.at((l, 1, KD - 1)))
            if l == 1:
                act.dma_start(x_d, x[:, :, :]).then_inc(x_spilled.sem, x_spilled.mark(l, 16))
                act.wait_ge(x_spilled.sem, x_spilled.at(l))
            for dst, src in ((dft_l, "dft_l"), (dft_c, "dft_c"), (c64, "c64")):
                act.dma_start(dst[:], A[src]).then_inc(dft_in.sem, dft_in.mark(l, 16))
            act.dma_start(bint[:].rearrange("p g r s -> p (g r s)"), bin_d[l]).then_inc(
                bint_in.sem, bint_in.mark(l, 16))
            for i in (0, 1, 6, 7, 8, 9, 10, 11):
                act.wait_ge(w_used.sem, w_used.at(l * N_TILES + i))
                dst = {0: zkv[:, 0], 1: zkv[:, 1], 6: zq[:, 0], 7: zq[:, 1], 8: zq[:, 2],
                       9: zf[:, 0], 10: zf[:, 1], 11: zf[:, 2]}[i]
                m = TOK if i < 6 else n
                act.copy(dst[:, 0:m], pair(i, m)).then_inc(in_act.sem, in_act.mark((l, i)))
                if i == 6:
                    act.wait_ge(in_dve.sem, in_dve.at((l, 5)))
                    act.dma_start(zs_d[l].rearrange("i p f -> p i f"),
                                                     zs[:].rearrange("p i s c -> p i (s c)")).then_inc(
                                                         zs_stored.sem, zs_stored.mark(l, 16))
                if i == 8:
                    act.wait_ge(zs_stored.sem, zs_stored.at(l))
                    v = zs_d[l].rearrange("i (g p) (s c) -> s p (i g) c", p=GP, s=CH)
                    for s in range(CH):
                        act.dma_start(us[s * GP:(s + 1) * GP, :, :], v[s]).then_inc(us_in.sem, us_in.mark((l, s), 16))
            for q, (src, kts, m) in enumerate(((zq, KQ, n), (zkv, KKV, TOK))):
                for k in range(kts):
                    if k >= 2:
                        act.wait_ge(sn_used.sem, sn_used.at((l, q, k - 2)))
                    elif q:
                        act.wait_ge(sn_used.sem, sn_used.at((l, 0, KQ - 1)))
                    act.activation(sq_s[:, k % 2, 0:m], src[:, k, 0:m], ACT.Square).then_inc(
                        sn_sq.sem, sn_sq.mark((l, q, k)))
                act.wait_ge(sn_used.sem, sn_used.at((l, q, kts - 1)))
                if q:
                    act.wait_ge(sn_scale.sem, sn_scale.at((l, 0)))
                act.activation(rs_s[:, 0:m], ps[:, q, 0:m], ACT.Sqrt, bias=eps_col[:, 0:1],
                                                scale=1.0 / (kts * P)).then_inc(sn_root.sem, sn_root.mark((l, q)))
            act.wait_ge(sn_scale.sem, sn_scale.at(l))
            for b in range(n // P):
                act.wait_ge(fr_a.sem, fr_a.at((l, b)))
                act.copy(pq[:, b, :, :].rearrange("p i c -> p (i c)"), ps[:, 2 + b % 2, 0:768]).then_inc(
                    fr_pq.sem, fr_pq.mark((l, b)))
            for i in range(3):
                act.wait_ge(fr_b.sem, fr_b.at((l, i)))
                act.copy(of[:, i, 0:n], ps[:, i, 0:n]).then_inc(fr_evac.sem, fr_evac.mark((l, i)))
            for q in range(6):
                act.wait_ge(bu_done.sem, bu_done.at((l, q)))
                for ri in range(2):
                    v = ps[0:64, q % 2, ri * 512:ri * 512 + 4 * NC].rearrange("p (g c) -> p g c", c=NC)
                    o = ss[0:64, :, ri, 4 * q:4 * q + 4].rearrange("p j g -> p g j")
                    act.copy(o[:, :, 1 + NCC:1 + NC], v[:, :, 0:NCL])
                    ins = act.copy(o[:, :, 1:1 + NCC], v[:, :, NCL:NC])
                ins.then_inc(bu_act.sem, bu_act.mark((l, q)))
            act.dma_start(cout[:].rearrange("p r g s -> p (r g s)"), cout_d[l]).then_inc(
                cout_in.sem, cout_in.mark(l, 16))
            act.wait_ge(scan.sem, scan.at((l, 7, 3), NC // 8 - 1))
            o = snat[0:64].rearrange("p r g c -> p c (r g)")
            v = ss[0:64].rearrange("p j r g -> p j (r g)")
            act.copy(o[:, 0:NCL], v[:, NCC:NC])
            act.copy(o[:, NCL:NC], v[:, 0:NCC]).then_inc(snat_act.sem, snat_act.mark(l))
            act.wait_ge(snat_act.sem, snat_act.at(l))
            act.wait_ge(snat_dve.sem, snat_dve.at(l))
            act.dma_start(toep[:], toep_d[l]).then_inc(toep_in.sem, toep_in.mark(l, 16))
            act.dma_start(wglu[:].rearrange("p k m -> p (k m)"), A["w_glu"][l]).then_inc(
                glu_w_in.sem, glu_w_in.mark(l, 16))
            act.wait_ge(y_evac.sem, y_evac.at((l, 5)))
            for s in range(CH):
                act.dma_start(y_d[l].rearrange("g p s c -> s p g c")[s],
                                                us[s * GP:(s + 1) * GP, :, :]).then_inc(
                                                    y_stored.sem, y_stored.mark(l, 16))
            act.wait_ge(y_stored.sem, y_stored.at(l))
            act.dma_start(yp[:, :, :], y_d[l].rearrange("(i g) p s c -> (g p) i (s c)", i=3)).then_inc(
                y_in.sem, y_in.mark(l, 16))
            act.wait_ge(y_skip.sem, y_skip.at(l))
            act.activation(yg[:, :, :], yp[:, :, :], ACT.Gelu_apprx_tanh).then_inc(gelu.sem, gelu.mark(l))
            for o in range(3):
                act.wait_ge(glu_done.sem, glu_done.at((l, o)))
                if o:
                    act.wait_ge(os_ready.sem, os_ready.at((l, o - 1)))
                act.activation(sig[:, :], ps[:, o % 2, 0:TOK], ACT.Sigmoid,
                                                bias=b_glu[:, l, o:o + 1]).then_inc(glu_sig.sem, glu_sig.mark((l, o)))
            act.wait_ge(os_ready.sem, os_ready.at((l, 2)))
            nq = n // P
            for h2 in range(4):
                if h2:
                    act.wait_ge(v_done.sem, v_done.at((l, h2 - 1)))
                act.dma_start(pw[:, :], A["w_pair"][l, h2]).then_inc(pw_in.sem, pw_in.mark((l, h2), 16))
                for j in range(2):
                    act.wait_ge(q_done.sem, q_done.at((l, h2, j)))
                    act.copy(qq[0:64, j, 0:n], ps[0:64, j, 0:n]).then_inc(q_act.sem, q_act.mark((l, h2, j)))
                act.wait_ge(k_done.sem, k_done.at((l, h2)))
                act.copy(kk[0:64, 0, :], ps[0:64, 2, 0:TOK])
                act.copy(kk[0:64, 1, :], ps[64:128, 2, 0:TOK]).then_inc(k_act.sem, k_act.mark((l, h2)))
                act.wait_ge(v_done.sem, v_done.at((l, h2)))
                act.copy(vv[:].rearrange("p b v -> p (b v)"), ps[:, 3, 0:TOK]).then_inc(v_act.sem, v_act.mark((l, h2)))
                units = [(j, b) for j in range(2) for b in range(nq)]

                def exponent(u):
                    act.wait_ge(nmax_ready.sem, nmax_ready.at((l, h2, u)))
                    if u >= 3:
                        act.wait_ge(pt_done.sem, pt_done.at((l, h2, u - 3)))
                    a = 0 if units[u][1] < 4 else 512
                    act.activation(pr[:, u % 3, a:TOK], ps[:, u % 2, a:TOK], ACT.Exp,
                                                      bias=nmx[:, u % 4:u % 4 + 1], scale=SCALE,
                                                      accum_out=sm[:, u % 4:u % 4 + 1]).then_inc(
                                                          exp_ready.sem, exp_ready.mark((l, h2, u)))

                exponent(0)
                for u, (j, b) in enumerate(units):
                    if u + 1 < len(units):
                        exponent(u + 1)
                    act.wait_ge(pt_done.sem, pt_done.at((l, h2, u)))
                    q0 = (b % 4) * P
                    if b in (0, 4) and u:
                        act.wait_ge(pv_done.sem, pv_done.at((l, h2, *((j - 1, 3) if nq == 4 else ((j - 1, 5) if b == 0 else (j, 3))))))
                    k0 = 0 if b < 4 else 4
                    act.copy(pt[:, k0:6, q0:q0 + P],
                                              ps[:, 2, k0 * P:TOK].rearrange("p (k q) -> p k q", q=P)).then_inc(
                                                  pt_evac.sem, pt_evac.mark((l, h2, u)))
                act.wait_ge(pv_done.sem, pv_done.at((l, h2, 1, 3 if nq == 4 else 5)))
                act.copy(oah[:, h2, 0:n], ps[:, 3, 0:n]).then_inc(oh_ready.sem, oh_ready.mark((l, h2)))
            for dst, src in ((osh, osm), (ofh, of)):
                ins = act.copy(dst[:, :, 0:n], src[:, :, 0:n])
                ins.then_inc(mh_ready.sem, mh_ready.mark((l, dst is ofh)))
            for m in range(KD):
                for j, b in enumerate((0, 2, 1)):
                    act.wait_ge(w_used.sem, w_used.at(l * N_TILES + N_IN + 5 * m + 2 * j))
                    i = 3 * m + j
                    if i >= 2:
                        act.wait_ge(br_dve.sem, br_dve.at((l, (i - 2) // 3, (i - 2) % 3)))
                    act.activation(gt[:, i % 2, 0:n], pair(6 * m + (0, 3, 5)[j], n), ACT.Tanh,
                                                    bias=b_gate[:, l, b * KD + m:b * KD + m + 1], scale=0.5).then_inc(
                                                        g_ready.sem, g_ready.mark((l, m, j)))
            act.wait_ge(w_used.sem, w_used.at(l * N_TILES + N_IN + N_MERGE - 1))
            act.dma_start(x[:, :, :], A["x_t"] if l == 0 else x_d).then_inc(x_in.sem, x_in.mark(("out", l), 16))
            for k in range(KD):
                act.wait_ge(m_ready.sem, m_ready.at((l, k)))
                act.mul(hh[:, k, 0:n], m_sb[:, k, 0:n], 0.5).then_inc(msplit_h.sem, msplit_h.mark((l, k)))
            act.wait_ge(x_add.sem, x_add.at((l, KD - 1)))
            act_norm(act, l, 2, n)
            act.wait_ge(lo_ready.sem, lo_ready.at((l, 2, KD - 1)))
            for s in (relu_ready, midh_ready):
                s.start_loop((l, "mlp"))
            with act.Fori(0, QUARTERS) as i:
                for m in range(KD):
                    act.wait_ge(w_used.sem, w_used.at((l, "m1", m), i))
                    if m >= 2:
                        act.wait_ge(msq_ready.sem, msq_ready.at((l, m - 2), i))
                    act.activation(mr[:, m % 2, 0:n], pair(m, n), ACT.Relu).then_inc(
                        relu_ready.sem, relu_ready.mark((l, m)))
                    act.wait_ge(relu_ready.sem, relu_ready.at((l, m), i))
                    act.activation(midh[:, m, 0:n], mr[:, m % 2, 0:n], ACT.Square).then_inc(
                        midh_ready.sem, midh_ready.mark((l, m)))
            for s in (relu_ready, midh_ready):
                s.end_loop(QUARTERS)
            act.wait_ge(x_add.sem, x_add.at((l, "mlp", KD - 1), QUARTERS - 1))

        @block.scalar
        def _(act):
            act.dma_start(cvec[:], A["cvec"]).then_inc(cvec_in.sem, cvec_in.mark(0, 16))
            for dst, name in ((ident, "ident"), (rope, "rope"), (ada_b, "ada_b"), (ln, "ln"), (fnorm, "fnorm"),
                              (qkn, "qkn"), (b_gate, "b_gate"), (b_glu, "b_glu"), (ssm_d, "ssm_d")):
                act.dma_start(dst[:], A[name]).then_inc(consts_in.sem, consts_in.mark(0, 16))
            act.wait_ge(cvec_in.sem, cvec_in.at(0))
            act.activation(svec[:], cvec[:], ACT.Silu).then_inc(silu_ready.sem, silu_ready.mark(0))
            for l in range(DEPTH):
                if l:
                    act.wait_ge(prep_dve.sem, prep_dve.at((0, "cout")))
                    act.wait_ge(prep_pe.sem, prep_pe.at((0, "v", 1, 5)))
                act.dma_start(abuf[:, 0:3, :], A["ssm_a"][l]).then_inc(prep_loaded.sem, prep_loaded.mark(l, 16))
                act.dma_start(b_in[:], A["ssm_b"][l]).then_inc(prep_loaded.sem, prep_loaded.mark(l, 16))
                act.dma_start(c_in[:], A["ssm_c"][l]).then_inc(prep_loaded.sem, prep_loaded.mark(l, 16))
                act.wait_ge(prep_loaded.sem, prep_loaded.at(l))
                act.activation(abuf[:, 3, :], abuf[:, 2, :], ACT.Exp).then_inc(prep_act.sem, prep_act.mark((l, "dt")))
                act.wait_ge(prep_dve.sem, prep_dve.at((l, "dta")))
                act.activation(abuf[:, 6, :], abuf[:, 4, :], ACT.Exp).then_inc(prep_act.sem, prep_act.mark((l, "mag")))
                act.wait_ge(prep_dve.sem, prep_dve.at((l, "angle")))
                act.activation(abuf[:, 8, :], abuf[:, 7, :], ACT.Sin)
                act.activation(abuf[:, 9, :], abuf[:, 7, :], ACT.Sin, scale=0.5).then_inc(
                    prep_act.sem, prep_act.mark((l, "sin")))
                if l:
                    act.wait_ge(prep_stored.sem, prep_stored.at((0, "bin")))
                for q in range(GROUPS // 2):
                    act.wait_ge(prep_pe.sem, prep_pe.at((l, "binT", q)))
                    act.copy(binT[:, 2 * q:2 * q + 2, :, :].rearrange("p g r s -> p (g r s)"),
                                               ps[:, q % 2, 0:512]).then_inc(
                                                   prep_act.sem, prep_act.mark((l, "binT", q)))
                act.wait_ge(prep_act.sem, prep_act.at((l, "binT", GROUPS // 2 - 1)))
                act.dma_start(bin_d[l], binT[:].rearrange("p g r s -> p (g r s)")).then_inc(
                    prep_stored.sem, prep_stored.mark((l, "bin"), 16))
                if l:
                    act.wait_ge(prep_v_stored.sem, prep_v_stored.at(0))
                for half in range(2):
                    for q in range(6):
                        act.wait_ge(prep_pe.sem, prep_pe.at((l, "v", half, q)))
                        g = 12 * half + 2 * q
                        act.copy(vsb[:, g:g + 2, :].rearrange("p g f -> p (g f)"),
                                                   ps[0:GP, q % 2, 0:480]).then_inc(
                                                       prep_act.sem, prep_act.mark((l, "v", half, q)))
                act.wait_ge(prep_dve.sem, prep_dve.at((l, "cout")))
                act.dma_start(cout_d[l], bin_[:].rearrange("p r g s q -> p (r g s q)")).then_inc(
                    prep_stored.sem, prep_stored.mark((l, "cout"), 16))
                act.wait_ge(prep_act.sem, prep_act.at((l, "v", 1, 5)))
                for s in range(CH):
                    act.dma_start(toep_d[l, s * GP:(s + 1) * GP, :, :],
                                                         vsb[:, :, (7 - s) * GP:(15 - s) * GP]).then_inc(
                                                             prep_v_stored.sem, prep_v_stored.mark(l, 16))
            act.wait_ge(prep_stored.sem, prep_stored.at((1, "cout")))
            act.wait_ge(prep_v_stored.sem, prep_v_stored.at(1))
            act.wait_ge(prep_dve.sem, prep_dve.at((1, "cout")))
            act.dma_start(x[:, :, :], A["x_t"]).then_inc(x_in.sem, x_in.mark("first", 16))
            act.wait_ge(x_in.sem, x_in.at("first"))
            for l in range(DEPTH):
                act_layer(act, l)
            act_rms(act, (DEPTH, 1), LAT)
            for k in range(KD):
                act.wait_ge(fin_ready.sem, fin_ready.at(k))
                act.dma_start(out[:, k, :], xo[:, k, :]).then_inc(out_stored.sem, out_stored.mark(k, 16))
            act.wait_ge(out_stored.sem, out_stored.at(KD - 1))

        def dve_norm(dve, l, w, n):
            dve.wait_ge(rms_ready.sem, rms_ready.at((l, w)))
            dve.reciprocal(rstd[:, 0:n], rstd[:, 0:n]).then_inc(rstd_ready.sem, rstd_ready.mark((l, w)))
            dve.wait_ge(rstd_ready.sem, rstd_ready.at((l, w)))

            def lo(k):
                dve.wait_ge(hi_ready.sem, hi_ready.at((l, w, k)))
                row = 0 if w == 1 else 3
                for s, (a, b) in enumerate(spans(n)):
                    ins = dve.scalar_tensor_tensor(hl[:, k, a:b], nt[:, k % 2, a:b], ada[:, l, row * KD + k, s:s + 1],
                                                   hh[:, k, a:b].bitcast(F32), ALU.add, ALU.subtract)
                ins.then_inc(lo_ready.sem, lo_ready.mark((l, w, k)))

            for k in range(KD):
                if k >= 2:
                    dve.wait_ge(lo_ready.sem, lo_ready.at((l, w, k - 2)))
                for s, (a, b) in enumerate(spans(n)):
                    ins = dve.scalar_tensor_tensor(nt[:, k % 2, a:b], x[:, k, a:b], gain[:, l, w - 1, k, s:s + 1],
                                                   rstd[:, a:b], ALU.mult, ALU.mult)
                ins.then_inc(nt_ready.sem, nt_ready.mark((l, w, k)))
                if k:
                    lo(k - 1)
            lo(KD - 1)

        def rotate(dve, src, dst, part, n, key):
            dve.tensor_tensor(part[64:96, 0:n], src[64:96, 0:n], rope[64:96, 0:n], ALU.mult).then_inc(
                ropes.sem, ropes.mark((*key, 0)))
            dve.tensor_tensor(dst[0][64:96, 0:n], src[96:128, 0:n], rope[96:128, 0:n], ALU.mult).then_inc(
                ropes.sem, ropes.mark((*key, 1)))
            dve.wait_ge(ropes.sem, ropes.at((*key, 1)))
            dve.tensor_tensor(dst[0][64:96, 0:n], dst[0][64:96, 0:n], part[64:96, 0:n], ALU.add).then_inc(
                ropes.sem, ropes.mark((*key, 2)))
            if len(dst) > 1:
                dve.wait_ge(ropes.sem, ropes.at((*key, 2)))
                dve.tensor_copy(dst[1][64:96, 0:n], dst[0][64:96, 0:n]).then_inc(ropes.sem, ropes.mark((*key, 3)))

        def dve_layer(dve, l):
            n = TOK if l == 0 else LAT
            dve_norm(dve, l, 1, TOK)
            dve.wait_ge(w_used.sem, w_used.at(l * N_TILES + 2))
            rotate(dve, ps[:, 2, :], (kk[:, 0], kk[:, 1]), rt_k, TOK, ("k", l))
            for i in (3, 4, 5):
                dve.wait_ge(w_used.sem, w_used.at(l * N_TILES + i))
                dve.tensor_copy(zs[:, i - 3, :, :], pair(i, TOK).rearrange("p (c s) -> p s c", s=CH)).then_inc(
                    in_dve.sem, in_dve.mark((l, i)))
            for q, (src, kts, m) in enumerate(((zq, KQ, n), (zkv, KKV, TOK))):
                dve.wait_ge(sn_root.sem, sn_root.at((l, q)))
                dve.reciprocal(rs_s[:, 0:m], rs_s[:, 0:m]).then_inc(rstd_ready.sem, rstd_ready.mark((l, "s", q)))
                dve.wait_ge(rstd_ready.sem, rstd_ready.at((l, "s", q)))
                for k in range(kts):
                    ins = dve.scalar_tensor_tensor(src[:, k, 0:m], src[:, k, 0:m], qkn[:, l, q * KQ + k:q * KQ + k + 1],
                                                   rs_s[:, 0:m], ALU.mult, ALU.mult)
                ins.then_inc(sn_scale.sem, sn_scale.mark((l, 0) if q == 0 else l))
            dve.wait_ge(fr_evac.sem, fr_evac.at((l, 2)))
            for q in range(6):
                dve.wait_ge(bu_done.sem, bu_done.at((l, q)))
                for ri in range(2):
                    v = ps[64:128, q % 2, ri * 512:ri * 512 + 4 * NC].rearrange("p (g c) -> p g c", c=NC)
                    o = ss[64:128, NC:0:-1, ri, 4 * q:4 * q + 4].rearrange("p j g -> p g j")
                    ins = dve.tensor_copy(o, v)
                ins.then_inc(bu_dve.sem, bu_dve.mark((l, q)))
            dve.wait_ge(bu_act.sem, bu_act.at((l, 5)))
            dve.wait_ge(bu_dve.sem, bu_dve.at((l, 5)))
            prev = ss[:, 0:NC, :, :].rearrange("p (a b) r g -> p a b r g", b=8)
            cur = ss[:, 1:NC + 1, :, :].rearrange("p (a b) r g -> p a b r g", b=8)
            dve.memset(ss[:, 0, :, :], 0.0).then_inc(scan.sem, scan.mark((l, "zero")))
            go = scan.n
            scan.start_loop((l, "scan"))
            with dve.Fori(0, NC // 8) as i:
                for u in range(8):
                    dve.wait_ge(scan.sem, i * 32 + (4 * u + go))
                    dve.tensor_tensor(sc_t1[:], a8r[:, l], prev[:, i, u], ALU.mult).then_inc(
                        scan.sem, scan.mark((l, u, 0)))
                    dve.tensor_tensor(sc_t2[:, ::-1, :], a8i[:, l], prev[:, i, u], ALU.mult).then_inc(
                        scan.sem, scan.mark((l, u, 1)))
                    dve.wait_ge(scan.sem, scan.at((l, u, 0), i))
                    dve.tensor_tensor(cur[:, i, u], cur[:, i, u], sc_t1[:], ALU.add).then_inc(
                        scan.sem, scan.mark((l, u, 2)))
                    dve.wait_ge(scan.sem, scan.at((l, u, 2), i))
                    dve.tensor_tensor(cur[:, i, u], cur[:, i, u], sc_t2[:], ALU.add).then_inc(
                        scan.sem, scan.mark((l, u, 3)))
            scan.end_loop(NC // 8)
            dve.wait_ge(scan.sem, scan.at((l, 7, 3), NC // 8 - 1))
            o = snat[64:128].rearrange("p r g c -> p c (r g)")
            v = ss[64:128, NC - 1::-1].rearrange("p j r g -> p j (r g)")
            dve.tensor_copy(o, v).then_inc(snat_dve.sem, snat_dve.mark(l))
            for q in range(6):
                dve.wait_ge(y_done.sem, y_done.at((l, q)))
                dve.tensor_copy(us[:, 4 * q:4 * q + 4, :].rearrange("p g c -> p (g c)"),
                                                ps[:, 2 + q % 2, 0:4 * NC]).then_inc(y_evac.sem, y_evac.mark((l, q)))
            dve.wait_ge(y_in.sem, y_in.at(l))
            for i in range(3):
                ins = dve.scalar_tensor_tensor(yp[:, i, :], zs[:, i].rearrange("p s c -> p (s c)"), ssm_d[:, l, i:i + 1],
                                               yp[:, i, :], ALU.mult, ALU.add)
            ins.then_inc(y_skip.sem, y_skip.mark(l))
            for o in range(3):
                dve.wait_ge(glu_sig.sem, glu_sig.at((l, o)))
                dve.tensor_tensor(osm[:, o, :].rearrange("p (c s) -> p s c", s=CH),
                                                    yg[:, o, :].rearrange("p (s c) -> p s c", s=CH),
                                                    sig[:, :].rearrange("p (s c) -> p s c", s=CH), ALU.mult).then_inc(
                                                        os_ready.sem, os_ready.mark((l, o)))
            nq = n // P
            for h2 in range(4):
                for j in range(2):
                    dve.wait_ge(q_done.sem, q_done.at((l, h2, j)))
                    if j or h2:
                        dve.wait_ge(ropes.sem, ropes.at(("q", l, h2 - (1 - j), 1 - j, 2)))
                    rotate(dve, ps[:, j, :], (qq[:, j],), rt, n, ("q", l, h2, j))
                units = [(j, b) for j in range(2) for b in range(nq)]

                def maximum(u):
                    j, b = units[u]
                    dve.wait_ge(sc_done.sem, sc_done.at((l, h2, u)))
                    c = u % 4
                    dve.tensor_reduce(mx[:, c:c + 1], ps[:, u % 2, (0 if b < 4 else 512):TOK],
                                                         AXX, ALU.max).then_inc(
                                                             max_ready.sem, max_ready.mark((l, h2, u)))
                    dve.wait_ge(max_ready.sem, max_ready.at((l, h2, u)))
                    dve.tensor_scalar(nmx[:, c:c + 1], mx[:, c:c + 1], -SCALE, None, ALU.mult).then_inc(
                        nmax_ready.sem, nmax_ready.mark((l, h2, u)))

                maximum(0)
                for u, (j, b) in enumerate(units):
                    if u + 1 < len(units):
                        maximum(u + 1)
                    dve.wait_ge(exp_ready.sem, exp_ready.at((l, h2, u)))
                    c = u % 4
                    dve.reciprocal(rsm[:, c:c + 1], sm[:, c:c + 1]).then_inc(
                        rsum_ready.sem, rsum_ready.mark((l, h2, u)))
                    dve.wait_ge(rsum_ready.sem, rsum_ready.at((l, h2, u)))
                    a = 0 if b < 4 else 512
                    dve.tensor_scalar(pr[:, u % 3, a:TOK], pr[:, u % 3, a:TOK], rsm[:, c:c + 1],
                                                       None, ALU.mult).then_inc(p_ready.sem, p_ready.mark((l, h2, u)))
                dve.wait_ge(oh_ready.sem, oh_ready.at((l, h2)))
                dve.tensor_tensor(oal[:, h2, 0:n], ps[:, 3, 0:n], oah[:, h2, 0:n].bitcast(F32),
                                                    ALU.subtract).then_inc(ol_ready.sem, ol_ready.mark((l, h2)))
            for dst, src, hi in ((osl, osm, osh), (ofl, of, ofh)):
                dve.wait_ge(mh_ready.sem, mh_ready.at((l, dst is ofl)))
                ins = dve.tensor_tensor(dst[:, :, 0:n], src[:, :, 0:n], hi[:, :, 0:n].bitcast(F32), ALU.subtract)
            ins.then_inc(ml_ready.sem, ml_ready.mark(l))
            dve.wait_ge(ml_ready.sem, ml_ready.at(l))
            for m in range(KD):
                for j in range(3):
                    dve.wait_ge(g_ready.sem, g_ready.at((l, m, j)))
                    if j < 2:
                        dve.wait_ge(br_done.sem, br_done.at((l, m, j)))
                    else:
                        dve.wait_ge(w_used.sem, w_used.at(l * N_TILES + N_IN + 5 * m + 3))
                    if j == 0 and m:
                        dve.wait_ge(m_ready.sem, m_ready.at((l, m - 1)))
                    if j == 2:
                        dve.wait_ge(m_ready.sem, m_ready.at((l, m, "part")))
                    dve.scalar_tensor_tensor((acc, tmp, tmp)[j][:, 0:n], gt[:, (3 * m + j) % 2, 0:n], 1.0,
                                                             pair(6 * m + (1, 2, 4)[j], n), ALU.add, ALU.mult).then_inc(
                                                                 br_dve.sem, br_dve.mark((l, m, j)))
                    if j == 1:
                        dve.wait_ge(br_dve.sem, br_dve.at((l, m, 1)))
                        dve.tensor_tensor(acc[:, 0:n], acc[:, 0:n], tmp[:, 0:n], ALU.add).then_inc(
                            m_ready.sem, m_ready.mark((l, m, "part")))
                    if j == 2:
                        dve.wait_ge(br_dve.sem, br_dve.at((l, m, 2)))
                        dve.tensor_tensor(m_sb[:, m, 0:n], acc[:, 0:n], tmp[:, 0:n], ALU.add).then_inc(
                            m_ready.sem, m_ready.mark((l, m)))
            for k in range(KD):
                dve.wait_ge(msplit_h.sem, msplit_h.at((l, k)))
                dve.scalar_tensor_tensor(hl[:, k, 0:n], m_sb[:, k, 0:n], 0.5, hh[:, k, 0:n].bitcast(F32),
                                                           ALU.mult, ALU.subtract).then_inc(
                                                               msplit_l.sem, msplit_l.mark((l, k)))

            def residual(m, row):
                for s, (a, b) in enumerate(spans(n)):
                    ins = dve.scalar_tensor_tensor(x[:, m, a:b], pair(m, n)[:, a:b], ada[:, l, row * KD + m, s:s + 1],
                                                   x[:, m, a:b], ALU.mult, ALU.add)
                return ins

            dve.wait_ge(x_in.sem, x_in.at(("out", l)))
            for m in range(KD):
                dve.wait_ge(w_used.sem, w_used.at(l * N_TILES + N_IN + N_MERGE + m))
                residual(m, 2).then_inc(x_add.sem, x_add.mark((l, m)))
            dve_norm(dve, l, 2, n)
            dve.wait_ge(lo_ready.sem, lo_ready.at((l, 2, KD - 1)))
            for s in (msq_ready, midl_ready, x_add):
                s.start_loop((l, "mlp"))
            with dve.Fori(0, QUARTERS) as i:
                for m in range(KD):
                    dve.wait_ge(relu_ready.sem, relu_ready.at((l, m), i))
                    if m >= 2:
                        dve.wait_ge(midl_ready.sem, midl_ready.at((l, m - 2), i))
                    dve.tensor_tensor(ms[:, m % 2, 0:n], mr[:, m % 2, 0:n], mr[:, m % 2, 0:n],
                                                         ALU.mult).then_inc(msq_ready.sem, msq_ready.mark((l, m)))
                    dve.wait_ge(msq_ready.sem, msq_ready.at((l, m), i))
                    dve.wait_ge(midh_ready.sem, midh_ready.at((l, m), i))
                    dve.tensor_tensor(midl[:, m, 0:n], ms[:, m % 2, 0:n],
                                                          midh[:, m, 0:n].bitcast(F32), ALU.subtract).then_inc(
                                                              midl_ready.sem, midl_ready.mark((l, m)))
                for m in range(KD):
                    dve.wait_ge(w_used.sem, w_used.at((l, "m2", m), i))
                    residual(m, 5).then_inc(x_add.sem, x_add.mark((l, "mlp", m)))
            for s in (msq_ready, midl_ready, x_add):
                s.end_loop(QUARTERS)
            dve.wait_ge(x_add.sem, x_add.at((l, "mlp", KD - 1), QUARTERS - 1))

        def dve_prepare(dve, l):
            step = [0]

            def do(ins, key=None):
                step[0] += 1
                k = (l, key or step[0])
                ins.then_inc(prep_dve.sem, prep_dve.mark(k))
                dve.wait_ge(prep_dve.sem, prep_dve.at(k))

            def tt(o, a, b, op, key=None):
                do(dve.tensor_tensor(o, a, b, op), key)

            def cmul(o_re, o_im, xr, xi, yr, yi, ta, tb, negate=False, key=None):
                tt(ta, xr, yr, ALU.mult)
                tt(tb, xi, yi, ALU.mult)
                tt(o_re, ta, tb, ALU.subtract)
                tt(ta, xr, yi, ALU.mult)
                tt(tb, xi, yr, ALU.mult)
                if negate:
                    do(dve.scalar_tensor_tensor(o_im, ta, -1.0, tb, ALU.mult, ALU.subtract), key)
                else:
                    tt(o_im, ta, tb, ALU.add, key)

            e = lambda i: abuf[:, i, :]
            a_re, a_im, dt_, dr, th, mag, r = e(0), e(1), e(3), e(4), e(5), e(6), e(7)
            s1, sh, cs, t, u, ar1, wr, wi = e(8), e(9), e(10), e(11), e(12), e(13), e(14), e(15)
            if l:
                dve.wait_ge(prep_stored.sem, prep_stored.at((0, "cout")))
            dve.wait_ge(prep_loaded.sem, prep_loaded.at(l))
            dve.wait_ge(prep_act.sem, prep_act.at((l, "dt")))
            tt(th, dt_, a_im, ALU.mult)
            tt(dr, dt_, a_re, ALU.mult, "dta")
            big, two_pi = 12582912.0, 2 * np.pi
            c1 = 6.28125
            c2 = float(np.float32(np.floor((two_pi - c1) * 2**20) / 2**20))
            c3 = float(np.float32(two_pi - c1 - c2))
            do(dve.tensor_scalar(t, th, float(1 / two_pi), big, ALU.mult, ALU.add))
            do(dve.tensor_scalar(t, t, big, None, ALU.subtract))
            do(dve.scalar_tensor_tensor(r, t, -c1, th, ALU.mult, ALU.add))
            do(dve.scalar_tensor_tensor(r, t, -c2, r, ALU.mult, ALU.add))
            do(dve.scalar_tensor_tensor(r, t, -c3, r, ALU.mult, ALU.add))
            pi = float(np.nextafter(np.float32(np.pi), np.float32(0)))
            do(dve.tensor_scalar(r, r, pi, -pi, ALU.min, ALU.max), "angle")
            dve.wait_ge(prep_act.sem, prep_act.at((l, "mag")))
            dve.wait_ge(prep_act.sem, prep_act.at((l, "sin")))
            tt(t, sh, sh, ALU.mult)
            do(dve.tensor_scalar(cs, t, -2.0, 1.0, ALU.mult, ALU.add))
            p = lambda k: (pw8[:, k, 0, :], pw8[:, k, 1, :])
            do(dve.memset(pw8[:, 0, 0, :], 1.0))
            do(dve.memset(pw8[:, 0, 1, :], 0.0))
            tt(p(1)[0], mag, cs, ALU.mult)
            tt(p(1)[1], mag, s1, ALU.mult)
            for lo_, n_, by in ((1, 1, 1), (1, 2, 2), (1, 4, 4)):
                src = pw8[:, lo_:lo_ + n_]
                dst = pw8[:, lo_ + by:lo_ + by + n_]
                f = pw8[:, by]
                br, bi = (f[:, c].unsqueeze(1).to_broadcast([P, n_, GROUPS]) for c in range(2))
                ta = t1[:, 0:n_ * GROUPS].rearrange("p (a b) -> p a b", b=GROUPS)
                tb = t2[:, 0:n_ * GROUPS].rearrange("p (a b) -> p a b", b=GROUPS)
                cmul(dst[:, :, 0], dst[:, :, 1], src[:, :, 0], src[:, :, 1], br, bi, ta, tb)
            for c in range(2):
                do(dve.tensor_copy(a8r[:, l, c, :], pw8[:, CH, 0, :]))
            do(dve.tensor_copy(a8i[:, l, 0, :], pw8[:, CH, 1, :]))
            do(dve.tensor_scalar(a8i[:, l, 1, :], pw8[:, CH, 1, :], -1.0, None, ALU.mult))
            do(dve.tensor_scalar(ar1, p(1)[0], -1.0, None, ALU.add))
            tt(t, a_re, a_re, ALU.mult)
            tt(u, a_im, a_im, ALU.mult)
            tt(t, t, u, ALU.add)
            do(dve.reciprocal(u, t))
            tt(wr, ar1, a_re, ALU.mult)
            tt(t, p(1)[1], a_im, ALU.mult)
            tt(wr, wr, t, ALU.add)
            tt(wr, wr, u, ALU.mult)
            tt(wi, p(1)[1], a_re, ALU.mult)
            tt(t, ar1, a_im, ALU.mult)
            tt(wi, wi, t, ALU.subtract)
            tt(wi, wi, u, ALU.mult)
            wrb, wib = (v.unsqueeze(2).to_broadcast([P, GROUPS, GP]) for v in (wr, wi))
            ta = t1[:, 0:GROUPS * GP].rearrange("p (a b) -> p a b", b=GP)
            tb = t2[:, 0:GROUPS * GP].rearrange("p (a b) -> p a b", b=GP)
            cmul(bb[:, 0], bb[:, 1], b_in[:, 0], b_in[:, 1], wrb, wib, ta, tb)
            fw, bw = slice(0, 64), slice(64, 128)
            do(dve.tensor_copy(p_in[fw], pw8[fw, CH - 1::-1]))
            do(dve.tensor_copy(p_in[bw], pw8[bw, 0:CH]))
            do(dve.tensor_copy(p_out[fw], pw8[fw, 1:CH + 1]))
            do(dve.tensor_copy(p_out[bw], pw8[bw, CH:0:-1]))
            do(dve.memset(p_z[:], 0.0))
            do(dve.tensor_copy(p_z[fw, 7:15], pw8[fw, 0:CH]))
            do(dve.tensor_copy(p_z[bw, 0:8], pw8[bw, CH - 1::-1]))

            def wide(mat, pows, g0, ng, n_, o, negate, key):
                shape = [P, ng, n_, GP]
                f = ng * n_ * GP
                xr, xi = (mat[:, c, g0:g0 + ng].unsqueeze(2).to_broadcast(shape) for c in range(2))
                yr, yi = (pows[:, 0:n_, c, g0:g0 + ng].rearrange("p s g -> p g s").unsqueeze(3).to_broadcast(shape)
                          for c in range(2))
                ta, tb = (v[:, 0:f].rearrange("p (g s q) -> p g s q", g=ng, q=GP) for v in (t1, t2))
                cmul(o[0], o[1], xr, xi, yr, yi, ta, tb, negate, key)

            wide(bb, p_in, 0, GROUPS, CH, (bin_[:, 0], bin_[:, 1]), False, "bin")
            for half in range(2):
                if half:
                    dve.wait_ge(prep_pe.sem, prep_pe.at((l, "v", 0, 5)))
                wide(c_in, p_z, 12 * half, 12, 15, (cz[:, 0], cz[:, 1]), True, f"cz{half}")
            dve.wait_ge(prep_pe.sem, prep_pe.at((l, "binT", GROUPS // 2 - 1)))
            wide(c_in, p_out, 0, GROUPS, CH, (bin_[:, 0], bin_[:, 1]), True, "cout")

        @block.vector
        def _(dve):
            dve.memset(ones[:], 1.0).then_inc(ones_ready.sem, ones_ready.mark(0))
            dve.memset(eps_col[:], EPS).then_inc(ones_ready.sem, ones_ready.mark(1))
            dve.wait_ge(ones_ready.sem, ones_ready.at(1))
            for l in range(DEPTH):
                dve_prepare(dve, l)
            dve.wait_ge(consts_in.sem, consts_in.at(0))
            dve.wait_ge(ada_used.sem, ada_used.at(3, DEPTH * ADA_TILES // 4 - 1))
            dve.tensor_tensor(
                ada[:].rearrange("p l m c -> p (l m) c"),
                ps[:, 3, 0:DEPTH * ADA_TILES * 2].rearrange("p (m c) -> p m c", c=2),
                ada_b[:].rearrange("p l m -> p (l m)").unsqueeze(2).to_broadcast([P, DEPTH * ADA_TILES, 2]), ALU.add).then_inc(
                    ada_ready.sem, ada_ready.mark(0))
            dve.wait_ge(ada_ready.sem, ada_ready.at(0))
            for l in range(DEPTH):
                for w in range(2):
                    r0 = (1, 4)[w] * KD
                    dve.scalar_tensor_tensor(gain[:, l, w], ada[:, l, r0:r0 + KD, :], 1.0,
                                             ln[:, l, w].unsqueeze(2).to_broadcast([P, KD, 2]), ALU.add, ALU.mult)
            dve.tensor_scalar(b_gate[:], b_gate[:], 0.5, None, ALU.mult).then_inc(ada_ready.sem, ada_ready.mark(1))
            dve.wait_ge(ada_ready.sem, ada_ready.at(1))
            for l in range(DEPTH):
                dve_layer(dve, l)
            dve.wait_ge(rms_ready.sem, rms_ready.at((DEPTH, 1)))
            dve.reciprocal(rstd[:, 0:LAT], rstd[:, 0:LAT]).then_inc(rstd_ready.sem, rstd_ready.mark("fin"))
            dve.wait_ge(rstd_ready.sem, rstd_ready.at("fin"))
            for k in range(KD):
                dve.scalar_tensor_tensor(xo[:, k, :], x[:, k, 0:LAT], fnorm[:, k:k + 1],
                                                            rstd[:, 0:LAT], ALU.mult, ALU.mult).then_inc(
                                                                fin_ready.sem, fin_ready.mark(k))

        for s in signals:
            book[s.name] = s.new


def lay_out(inp):
    f = np.ascontiguousarray
    a = {k: np.asarray(v) for k, v in inp.items()}
    L = DEPTH
    rows = np.concatenate([a["x"][0], a["ctx"][0]], 0)
    t = {"x_t": f(rows.T.reshape(KD, P, TOK).transpose(1, 0, 2))}
    t["cvec"] = f(np.stack([a["c"][0], a["c_ctx"]], -1).reshape(KD, P, 2).transpose(1, 0, 2))

    def tiles(w):
        k, m = w.shape
        return w.reshape(k // P, P, m // P, P).transpose(2, 1, 0, 3).reshape(m // P, P, k)

    def cols(v):
        return np.moveaxis(v.reshape(*v.shape[:-1], -1, P), -1, 0)

    t["ada_w"] = f(np.concatenate([tiles(a["ada_w"][l]) for l in range(L)]))
    t["ada_b"] = f(cols(a["ada_b"]))
    t["ln"] = f(np.stack([cols(a["ln1"]), cols(a["ln2"])], 2))
    t["fnorm"] = f(cols(a["final_norm"]))
    t["qkn"] = f(np.concatenate([cols(a["q_norm"]), cols(a["kv_norm"])], -1))
    t["b_gate"] = f(cols(a["b_gate"]))
    t["b_glu"] = f(cols(a["b_glu"]))
    t["ssm_d"] = f(cols(a["ssm_d"]))
    swap = np.r_[ROPE // 2:ROPE, 0:ROPE // 2]
    main, pairs = [], []
    for l in range(L):
        w = a["w_in"][l]
        r0 = QL + KVL
        kr = w[:, r0:r0 + ROPE]
        kr = np.concatenate([kr, kr[:, swap]], 1)
        f0, s0 = r0 + ROPE, r0 + ROPE + 384
        w = np.concatenate([w[:, QL:r0], kr, kr, w[:, s0:], w[:, :QL], w[:, f0:s0]], 1)
        main.append(tiles(w))
        g = tiles(a["w_gate"][l])
        ba, bf, bs = (tiles(a[n][l]) for n in ("w_br_attn", "w_br_fourier", "w_br_ssm"))
        for m in range(KD):
            one = np.concatenate([ba[m], bs[m][:, :P], bs[m][:, :3 * P]], 1)
            two = np.concatenate([bs[m][:, P:], bf[m], bf[m]], 1)
            main.append(np.stack([g[m], one, g[2 * KD + m], two, g[KD + m]]))
        main.append(tiles(a["w_out"][l]))
        w1, w2 = tiles(a["w_mlp1"][l]), tiles(a["w_mlp2"][l])
        for q in range(QUARTERS):
            main.append(w1[q * KD:(q + 1) * KD])
            main.append(w2[:, :, q * D:(q + 1) * D])
        q = a["w_uq"][l].reshape(QL, HEADS, NOPE + ROPE)
        q = np.concatenate([q, q[:, :, NOPE:][:, :, swap]], 2)
        kv = a["w_ukv"][l].reshape(KVL, HEADS, NOPE + VH)
        for h in range(0, HEADS, 2):
            qt = [tiles(q[:, h + j])[0] for j in range(2)]
            kt = tiles(kv[:, h:h + 2, :NOPE].reshape(KVL, P))[0]
            vt = tiles(kv[:, h:h + 2, NOPE:].reshape(KVL, P))[0]
            pairs.append(np.concatenate([*qt, kt, vt], 1))
    t["w_main"] = f(np.concatenate(main))
    t["w_pair"] = f(np.stack(pairs).reshape(L, HEADS // 2, P, 1280))
    t["w_glu"] = f(np.stack([a["w_glu"][l].reshape(3, P, 384).transpose(1, 0, 2).reshape(P, -1) for l in range(L)]))
    la = []
    for l in range(L):
        re, im = (a[n][l].transpose(0, 2, 1).reshape(P, GROUPS) for n in ("ssm_a_re", "ssm_a_im"))
        st = np.broadcast_to(a["ssm_log_step"][l][:, None, :], (2, NS, GROUPS)).reshape(P, GROUPS)
        la.append(np.stack([re, im, st], 1))
    t["ssm_a"] = f(np.stack(la))
    t["ssm_b"] = f(np.stack([a[n].transpose(0, 1, 3, 2, 4).reshape(L, P, GROUPS, GP)
                             for n in ("ssm_b_re", "ssm_b_im")], 2))
    t["ssm_c"] = f(np.stack([a[n].transpose(0, 1, 4, 2, 3).reshape(L, P, GROUPS, GP)
                             for n in ("ssm_c_re", "ssm_c_im")], 2))
    t["ident"] = np.eye(P, dtype=np.float32)
    half = ROPE // 2
    inv = np.float32(10000.0) ** (-np.arange(0, half, 2, dtype=np.float32) / np.float32(half))
    pos = np.arange(LAT)
    ang = np.concatenate([(pos // 64).astype(np.float32)[:, None] * inv, (pos % 64).astype(np.float32)[:, None] * inv], 1)
    tab = np.zeros((P, TOK), np.float32)
    tab[64:96] = 1.0
    tab[64:80, :LAT] = tab[80:96, :LAT] = np.cos(ang).T
    tab[96:112, :LAT], tab[112:128, :LAT] = -np.sin(ang).T, np.sin(ang).T
    t["rope"] = tab

    def dft(n):
        k = np.outer(np.arange(n), np.arange(n)) % n * (2 * np.pi / n)
        return np.cos(k), np.sin(k)

    for name, n in (("dft_l", LAT), ("dft_c", CTX)):
        c, s = dft(n)
        m = np.stack([c, -s], 1) / np.sqrt(n)
        t[name] = f(m.reshape(n // P, P, 2, n).transpose(1, 0, 2, 3).astype(np.float32))
    c, s = dft(64)
    eye = np.eye(2)
    t["c64"] = f((np.concatenate([np.kron(eye, c), np.kron(eye, s)], 1) / 8.0).astype(np.float32))
    return t


def kernel(**inputs):
    import concourse.bacc as bacc
    from concourse.bass_utils import run_bass_kernel_spmd

    arrays = lay_out(inputs)
    book = {}
    for _ in range(2):
        nc = bacc.Bacc("TRN2", target_bir_lowering=False, num_devices=1)
        aps = {k: nc.dram_tensor(f"in_{k}", v.shape, F32, kind="ExternalInput").ap() for k, v in arrays.items()}
        out = nc.dram_tensor("out_t", (P, KD, LAT), F32, kind="ExternalOutput").ap()
        build(nc, aps, out, book)
    r = run_bass_kernel_spmd(nc, [{f"in_{k}": v for k, v in arrays.items()}], core_ids=[0])
    y = r.results[0]["out_t"]
    return np.ascontiguousarray(y.transpose(2, 1, 0).reshape(1, LAT, D))
```

```python
from contextlib import ExitStack

import numpy as np

import concourse.bass as bass
from concourse import mybir

F32 = mybir.dt.float32
F32R = mybir.dt.float32r
ALU = mybir.AluOpType
ACT = mybir.ActivationFunctionType
AXX = mybir.AxisListType.X

P = 128
D = 1024
KD = D // P
LAT, CTX = 512, 256
TOK = LAT + CTX
DEPTH = 2
HEADS = 8
NOPE, ROPE, VH = 64, 32, 64
QL, KVL = 384, 256
KQ, KKV = QL // P, KVL // P
SCALE = 1.0 / float(np.sqrt(NOPE + ROPE))
GROUPS, GP, NS = 24, 16, 64
CH = 8
NC = TOK // CH
NCL, NCC = LAT // CH, CTX // CH
SCAN_SPLIT = 5
EPS = 1e-6
N_IN, N_MERGE, N_OUT, QUARTERS = 12, 40, 8, 4
N_TILES = N_IN + N_MERGE + N_OUT + QUARTERS * 16
RAW_SLOTS, W_SLOTS = 2, 4
ADA_TILES = 48
ADA_PAIRS = ADA_TILES // 8
ADA_AT = ((0, 3, 4, 6), (6, 8, 9, 10))


class Signal:

    def __init__(self, sem, book):
        self.sem, self.book, self.new = sem, book, {}
        self.n, self.body, self.turns = 0, None, 1

    def mark(self, key, by=1):
        self.n += by
        self.new[key] = (self.n, self.body)
        return by

    def at(self, key, turn=0):
        n, body = self.book.get(key, (1, None))
        if body is not None:
            n = turn * self.book["loop", body] + n
        return n

    def start_loop(self, name):
        self.body, self.first = name, self.n

    def end_loop(self, turns):
        k = self.n - self.first
        self.new["loop", self.body] = k
        self.n += (turns - 1) * k
        self.body = None


def build(nc, A, out, book):
    ctx = ExitStack()
    with ctx:
        BASE = 16512
        CONST, RING = BASE, BASE + 8192
        HREG = RING + (RAW_SLOTS + 2 * W_SLOTS) * KD * P * 4
        REST = HREG + 2 * KD * TOK * 4

        def at(name, off, shape, dt=F32):
            return nc.alloc_sbuf_tensor_at(name, shape, dt, offset=off)

        place = [CONST]

        def const(name, shape):
            t = at(name, place[0], shape)
            n = 4
            for s in shape[1:]:
                n *= s
            place[0] += -(-n // 32) * 32
            assert place[0] <= RING
            return t

        ident = const("ident", [P, P])
        ones = const("ones", [P, P])
        rope = const("rope", [P, TOK])
        ada = const("ada", [P, DEPTH, ADA_TILES, 2])
        ada_b = const("ada_b", [P, DEPTH, ADA_TILES])
        ln = const("ln", [P, DEPTH, 2, KD])
        gain = const("gain", [P, DEPTH, 2, KD, 2])
        fnorm = const("fnorm", [P, KD])
        qkn = const("qkn", [P, DEPTH, KQ + KKV])
        b_gate = const("b_gate", [P, DEPTH, 3 * KD])
        b_glu = const("b_glu", [P, DEPTH, 3])
        ssm_d = const("ssm_d", [P, DEPTH, 3])
        cvec = const("cvec", [P, KD, 2])
        svec = const("svec", [P, KD, 2])
        eps_col = const("eps_col", [P, 1])
        a8r = const("a8r", [P, DEPTH, 2, GROUPS])
        a8i = const("a8i", [P, DEPTH, 2, GROUPS])
        sc_t1 = const("sc_t1", [P, 2, GROUPS])
        sc_t2 = const("sc_t2", [P, 2, GROUPS])
        mx = const("mx", [P, 4])
        nmx = const("nmx", [P, 4])
        sm = const("sm", [P, 4])
        rsm = const("rsm", [P, 4])

        raw = at("raw", RING, [P, RAW_SLOTS, KD * P])
        whi = at("whi", RING + RAW_SLOTS * 4096, [P, W_SLOTS, KD * P], F32R)
        wlo = at("wlo", RING + (RAW_SLOTS + W_SLOTS) * 4096, [P, W_SLOTS, KD * P], F32R)
        hh = at("hh", HREG, [P, KD, TOK], F32R)
        hl = at("hl", HREG + KD * TOK * 4, [P, KD, TOK], F32R)

        def rest(name, off, shape, dt=F32):
            return at(name, REST + off, shape, dt)

        zq = rest("zq", 0, [P, KQ, TOK])
        zkv = rest("zkv", 9216, [P, KKV, TOK])
        kk = rest("kk", 15360, [P, 2, TOK])
        zf = rest("zf", 21504, [P, 3, TOK])
        of = rest("of", 21504, [P, 3, TOK])
        zs = rest("zs", 30720, [P, 3, CH, NC])
        us = rest("us", 39936, [P, GROUPS, NC])
        osm = rest("osm", 39936, [P, 3, TOK])
        snat = rest("snat", 49152, [P, 2, GROUPS, NC])
        yp = rest("yp", 49152, [P, 3, TOK])
        yg = rest("yg", 58368, [P, 3, TOK])
        ss = rest("ss", 67584, [P, NC + 1, 2, GROUPS])
        bint = rest("bint", 89088, [P, GROUPS, 2, P])
        cout = rest("cout", 89088, [P, 2, GROUPS, P])
        toep = rest("toep", 67584, [P, GROUPS, P])
        wglu = rest("wglu", 79872, [P, 3, 3 * P])
        sig = rest("sig", 84480, [P, TOK])
        pq = rest("pq", 49152, [P, TOK // P, 3, 2 * P])
        dft_l = rest("dft_l", 89088, [P, LAT // P, 2, LAT])
        dft_c = rest("dft_c", 105472, [P, CTX // P, 2, CTX])
        c64 = rest("c64", 109568, [P, 2 * P])
        qq = rest("qq", 49152, [P, 2, TOK])
        vv = rest("vv", 55296, [P, TOK // P, P])
        pr = rest("pr", 58368, [P, 3, TOK])
        pt = rest("pt", 67584, [P, TOK // P, LAT])
        pws = (rest("pw0", 30720, [P, 1280]), rest("pw1", 79872, [P, 1280]))
        rt = rest("rt", 84992, [P, TOK])
        oah = rest("oah", 89088, [P, 4, TOK], F32R)
        oal = rest("oal", 89088 + 12288, [P, 4, TOK], F32R)
        m_sb = rest("m_sb", 0, [P, KD, TOK])
        gt = rest("gt", 24576, [P, 2, TOK])
        acc = rest("acc", 30720, [P, TOK])
        tmp = rest("tmp", 33792, [P, TOK])
        osh = rest("osh", 49152, [P, 3, TOK], F32R)
        osl = rest("osl", 58368, [P, 3, TOK], F32R)
        ofh = rest("ofh", 67584, [P, 3, TOK], F32R)
        ofl = rest("ofl", 76800, [P, 3, TOK], F32R)
        x = rest("x", 49152, [P, KD, TOK])
        nt = rest("nt", 0, [P, 2, TOK])
        sqt = rest("sqt", 6144, [P, 2, TOK])
        rstd = rest("rstd", 12288, [P, TOK])
        sq_s = rest("sq_s", 49152, [P, 2, TOK])
        rs_s = rest("rs_s", 55296, [P, TOK])
        rs_q = rest("rs_q", 110592, [P, TOK])
        midh = rest("midh", 0, [P, KD, TOK], F32R)
        midl = rest("midl", 24576, [P, KD, TOK], F32R)
        mr = rest("mr", 73728, [P, 2, TOK])
        ms = rest("ms", 79872, [P, 2, TOK])
        xo = rest("xo", 73728, [P, KD, LAT])
        t1 = rest("t1", 0, [P, 3072])
        t2 = rest("t2", 12288, [P, 3072])
        bin_ = rest("bin", 24576, [P, 2, GROUPS, CH, GP])
        binT = rest("binT", 49152, [P, GROUPS, 2, P])
        cz = rest("cz", 73728, [P, 2, 12, 15, GP])
        b_in = rest("b_in", 96768, [P, 2, GROUPS, GP])
        c_in = rest("c_in", 99840, [P, 2, GROUPS, GP])
        bb = rest("bb", 102912, [P, 2, GROUPS, GP])
        pw8 = rest("pw8", 105984, [P, CH + 1, 2, GROUPS])
        p_in = rest("p_in", 107712, [P, CH, 2, GROUPS])
        p_out = rest("p_out", 109248, [P, CH, 2, GROUPS])
        p_z = rest("p_z", 110784, [P, 15, 2, GROUPS])
        vsb = at("vsb", HREG, [GP, GROUPS, 15 * GP])
        ada_w = at("ada_w", RING + RAW_SLOTS * 4096, [P, 8, D])
        abuf = at("abuf", HREG + 39424, [P, 24, GROUPS])
        ada_rows = at("ada_rows", HREG + 41728, [2, 2, 512])

        ps = ctx.enter_context(nc.psum_tensor("ps", [P, 4, 1024], F32))

        def dram(name, shape):
            return nc.dram_tensor(name, shape, F32, kind="Internal").ap()

        bin_d = dram("bin_d", (DEPTH, P, GROUPS * 2 * P))
        cout_d = dram("cout_d", (DEPTH, P, GROUPS * 2 * P))
        toep_d = dram("toep_d", (DEPTH, P, GROUPS, P))
        zs_d = dram("zs_d", (DEPTH, 3, P, TOK))
        y_d = dram("y_d", (DEPTH, GROUPS, GP, CH, NC))
        x_d = dram("x_d", (P, KD, TOK))

        signals = []

        def signal(name):
            signals.append(Signal(ctx.enter_context(nc.semaphore(name)), book.setdefault(name, {})))
            signals[-1].name = name
            return signals[-1]

        consts_in = signal("consts_in")
        cvec_in = signal("cvec_in")
        ada_used = [signal(f"ada_used{u}") for u in range(8)]
        ada_row = [signal(f"ada_row{j}") for j in range(2)]
        ada_turned = signal("ada_turned")
        ada_ready = signal("ada_ready")
        silu_ready = signal("silu_ready")
        w_turn = signal("w_turn")
        w_split = signal("w_split")
        w_used = signal("w_used")
        ones_ready = signal("ones_ready")
        ada_full = [signal(f"ada_full{u}") for u in range(8)]
        raw_full = [signal(f"raw_full{u}") for u in range(RAW_SLOTS)]
        prep_loaded = signal("prep_loaded")
        prep_c_loaded = signal("prep_c_loaded")
        prep_act = signal("prep_act")
        prep_dve = signal("prep_dve")
        prep_pe = signal("prep_pe")
        prep_stored = signal("prep_stored")
        prep_v_stored = signal("prep_v_stored")
        x_in = signal("x_in")
        x_spilled = signal("x_spilled")
        sq_ready = signal("sq_ready")
        sq_used = signal("sq_used")
        rms_ready = signal("rms_ready")
        rstd_ready = signal("rstd_ready")
        nt_ready = signal("nt_ready")
        hi_ready = signal("hi_ready")
        lo_ready = signal("lo_ready")
        in_act = signal("in_act")
        in_dve = signal("in_dve")
        ropes = signal("ropes")
        sn_sq = signal("sn_sq")
        sn_used = signal("sn_used")
        sn_root = signal("sn_root")
        sn_scale = signal("sn_scale")
        dft_in = signal("dft_in")
        fr_a = signal("fr_a")
        fr_pq = signal("fr_pq")
        fr_b = signal("fr_b")
        fr_evac = signal("fr_evac")
        zs_stored = signal("zs_stored")
        us_in = signal("us_in")
        bint_in = signal("bint_in")
        cout_in = signal("cout_in")
        toep_in = signal("toep_in")
        glu_w_in = signal("glu_w_in")
        bu_done = signal("bu_done")
        bu_act = signal("bu_act")
        bu_dve = signal("bu_dve")
        scan = signal("scan")
        snat_act = signal("snat_act")
        snat_dve = signal("snat_dve")
        y_done = signal("y_done")
        y_evac = signal("y_evac")
        y_stored = signal("y_stored")
        y_in = signal("y_in")
        y_skip = signal("y_skip")
        gelu = signal("gelu")
        glu_done = signal("glu_done")
        glu_sig = signal("glu_sig")
        os_ready = signal("os_ready")
        pw_in = [signal(f"pw_in{j}") for j in range(2)]
        q_done = signal("q_done")
        q_act = signal("q_act")
        k_done = signal("k_done")
        k_act = signal("k_act")
        v_done = signal("v_done")
        v_act = signal("v_act")
        sc_done = signal("sc_done")
        max_ready = signal("max_ready")
        nmax_ready = signal("nmax_ready")
        exp_ready = signal("exp_ready")
        rsum_ready = signal("rsum_ready")
        p_ready = signal("p_ready")
        pt_done = signal("pt_done")
        pt_evac = signal("pt_evac")
        pv_done = signal("pv_done")
        oh_ready = signal("oh_ready")
        ol_ready = signal("ol_ready")
        mh_ready = signal("mh_ready")
        ml_ready = signal("ml_ready")
        g_ready = signal("g_ready")
        br_done = signal("br_done")
        br_dve = signal("br_dve")
        m_ready = signal("m_ready")
        msplit_h = signal("msplit_h")
        msplit_l = signal("msplit_l")
        x_add = signal("x_add")
        relu_ready = signal("relu_ready")
        midh_ready = signal("midh_ready")
        msq_ready = signal("msq_ready")
        midl_ready = signal("midl_ready")
        fin_ready = signal("fin_ready")
        out_stored = signal("out_stored")

        def pair(p, n):
            return ps[:, p % 4, 0:n]

        def spans(n):
            return [(0, 512)] + ([(512, 768)] if n > 512 else [])

        def product(pe, p, w, kts, xh, xl, n, first, last):
            ins = None
            for i, (kw, kx) in enumerate(kts):
                for j, (ww, xx) in enumerate(((whi, xh), (whi, xl), (wlo, xh))):
                    for a, b in spans(n):
                        ins = pe.matmul(ps[:, p % 4, a:b], ww[:, w % W_SLOTS, kw * P:(kw + 1) * P],
                                        xx[:, kx, a:b], start=(first and i == 0 and j == 0),
                                        stop=(last and i == len(kts) - 1 and j == 2))
            return ins

        def wait_w(pe, t):
            pe.wait_ge(w_split.sem, 2 * (t + 1))

        def pe_rms(pe, key, n):
            for k in range(KD):
                pe.wait_ge(sq_ready.sem, sq_ready.at((key, k)))
                for a, b in spans(n):
                    ins = pe.matmul(ps[:, 3, a:b], ones[:, :], sqt[:, k % 2, a:b], start=(k == 0), stop=(k == KD - 1))
                ins.then_inc(sq_used.sem, sq_used.mark((key, k)))

        def pe_ada(pe, first, turns):
            o = ps[:, 3, 0:DEPTH * ADA_TILES * 2].rearrange("p (a b c) -> p a b c", b=8, c=2)
            with pe.Fori(first, first + turns) as i:
                for j in range(2):
                    for u in range(4):
                        pe.wait_ge(ada_full[4 * j + u].sem, i * 16 + 16)
                        for k in range(2):
                            ins = pe.matmul(ps[0:2, 2, 512 * j:512 * j + 512], svec[:, 2 * u + k, :],
                                            ada_w[:, 4 * j + u, 512 * k:512 * k + 512], start=(u == 0 and k == 0),
                                            stop=(u == 3 and k == 1))
                        ins.then_inc(ada_used[4 * j + u].sem, 1)
                for j in range(2):
                    pe.wait_ge(ada_row[j].sem, i + 1)
                    for q in range(4):
                        ins = pe.matmul(o[:, i, 4 * j + q, :], ada_rows[:, j, q * P:(q + 1) * P], ident[0:2, 0:2],
                                        start=True, stop=True, skip_group_check=True)
                    ins.then_inc(ada_turned.sem, 1)

        def act_ada(act, first, turns):
            with act.Fori(first, first + turns) as i:
                for j in range(2):
                    act.wait_ge(ada_used[4 * j + 3].sem, i + 1)
                    if first:
                        act.wait_ge(ada_turned.sem, i * 2 + (j - 1))
                    act.copy(ada_rows[:, j, :], ps[0:2, 2, 512 * j:512 * j + 512]).then_inc(ada_row[j].sem, 1)

        def pe_layer(pe, l):
            n = TOK if l == 0 else LAT
            t0 = l * N_TILES
            pe_rms(pe, (l, 1), TOK)
            pe.wait_ge(lo_ready.sem, lo_ready.at((l, 1, KD - 1)))
            full = [(k, k) for k in range(KD)]

            def tile(i, p):
                wait_w(pe, t0 + i)
                product(pe, p, t0 + i, full, hh, hl, TOK if i < 6 else n, True, True).then_inc(
                    w_used.sem, w_used.mark(t0 + i))

            def square_sums(q, kts, m):
                for k in range(kts):
                    pe.wait_ge(sn_sq.sem, sn_sq.at((l, q, k)))
                    for a, b in spans(m):
                        ins = pe.matmul(ps[:, 2, a:b], ones[:, :], sq_s[:, k % 2, a:b],
                                        start=(k == 0), stop=(k == kts - 1))
                    ins.then_inc(sn_used.sem, sn_used.mark((l, q, k)))

            for i in range(4):
                tile(i, i)
            pe.wait_ge(in_dve.sem, in_dve.at((l, 0)))
            tile(4, 0)
            pe.wait_ge(in_dve.sem, in_dve.at((l, 1)))
            tile(5, 1)
            pe.wait_ge(in_dve.sem, in_dve.at((l, 2)))
            square_sums(1, KKV, TOK)
            pe.wait_ge(us_in.sem, us_in.at((l, CH - 1)))
            pe.wait_ge(bint_in.sem, bint_in.at(l))
            pe.wait_ge(in_act.sem, in_act.at((l, 3)))
            for q in range(6):
                if q == 1:
                    pe.wait_ge(sn_root.sem, sn_root.at((l, 1)))
                if q >= 2:
                    pe.wait_ge(bu_act.sem, bu_act.at((l, q - 2)))
                    pe.wait_ge(bu_dve.sem, bu_dve.at((l, q - 2)))
                for ri in range(2):
                    for j in range(4):
                        g = 4 * q + j
                        ins = pe.matmul(ps[:, 3 - q % 2, ri * 512 + j * NC:ri * 512 + (j + 1) * NC], bint[:, g, ri, :],
                                        us[:, g, :], start=True, stop=True)
                ins.then_inc(bu_done.sem, bu_done.mark((l, q)))
            pe.wait_ge(bu_act.sem, bu_act.at((l, 5)))
            pe.wait_ge(bu_dve.sem, bu_dve.at((l, 5)))
            tile(6, 2)
            tile(7, 3)
            pe.wait_ge(in_act.sem, in_act.at((l, 4)))
            tile(8, 0)
            pe.wait_ge(ropes.sem, ropes.at(("k", l, 3)))
            tile(9, 1)
            pe.wait_ge(in_act.sem, in_act.at((l, 6)))
            square_sums(0, KQ, n)
            pe.wait_ge(in_act.sem, in_act.at((l, 7)))
            tile(10, 3)
            pe.wait_ge(in_act.sem, in_act.at((l, 8)))
            tile(11, 0)
            pe.wait_ge(dft_in.sem, dft_in.at(l))
            pe.wait_ge(in_act.sem, in_act.at((l, N_IN - 1)))
            pe.wait_ge(sn_root.sem, sn_root.at((l, 0)))
            blocks = range(n // P)
            for b in blocks:
                if b >= 2:
                    pe.wait_ge(fr_pq.sem, fr_pq.at((l, b - 2)))
                for i in range(3):
                    ins = pe.matmul(ps[:, 1 + b % 2, i * 256:i * 256 + 256], zf[:, i, b * P:b * P + P],
                                    c64[:, :], start=True, stop=True)
                ins.then_inc(fr_a.sem, fr_a.mark((l, b)))
            pe.wait_ge(fr_pq.sem, fr_pq.at((l, len(blocks) - 1)))
            for i in range(3):
                for (a, e), tab, b0, nb in ((spans(n)[0], dft_l, 0, 4),) + (((512, 768), dft_c, 4, 2),) * (n > 512):
                    for b in range(nb):
                        for cs in range(2):
                            ins = pe.matmul(ps[:, (3, 0, 1)[i], a:e], pq[:, b0 + b, i, cs * P:cs * P + P],
                                            tab[:, b, cs, :], start=(b == 0 and cs == 0), stop=(b == nb - 1 and cs == 1))
                ins.then_inc(fr_b.sem, fr_b.mark((l, i)))
            pe.wait_ge(fr_evac.sem, fr_evac.at((l, 2)))
            pe.wait_ge(snat_act.sem, snat_act.at(l))
            pe.wait_ge(snat_dve.sem, snat_dve.at(l))
            pe.wait_ge(cout_in.sem, cout_in.at(l))
            pe.wait_ge(toep_in.sem, toep_in.at(l))
            for g in range(GROUPS):
                q, j = divmod(g, 4)
                o = ps[:, 1 + q // 2, 512 * (q % 2) + j * NC:512 * (q % 2) + (j + 1) * NC]
                pe.matmul(o, cout[:, 0, g, :], snat[:, 0, g, :], start=True, stop=False)
                pe.matmul(o, cout[:, 1, g, :], snat[:, 1, g, :], start=False, stop=False)
                ins = pe.matmul(o, toep[:, g, :], us[:, g, :], start=False, stop=True)
                if j == 3:
                    ins.then_inc(y_done.sem, y_done.mark((l, q)))
            pe.wait_ge(gelu.sem, gelu.at(l))
            pe.wait_ge(glu_w_in.sem, glu_w_in.at(l))
            for o in range(3):
                if o == 2:
                    pe.wait_ge(glu_sig.sem, glu_sig.at((l, 0)))
                for k in range(3):
                    for a, b in spans(TOK):
                        ins = pe.matmul(ps[:, o % 2, a:b], wglu[:, k, o * P:o * P + P], yg[:, k, a:b],
                                        start=(k == 0), stop=(k == 2))
                ins.then_inc(glu_done.sem, glu_done.mark((l, o)))
            pe.wait_ge(glu_sig.sem, glu_sig.at((l, 2)))
            nq = n // P
            pe.wait_ge(sn_scale.sem, sn_scale.at((l, 0)))
            for h2 in range(4):
                pw = pws[h2 % 2]
                pe.wait_ge(pw_in[h2 % 2].sem, pw_in[h2 % 2].at((l, h2)))
                if h2:
                    pe.wait_ge(ol_ready.sem, ol_ready.at((l, h2 - 1)))
                for j in range(2):
                    for k in range(KQ):
                        for a, b in spans(n):
                            ins = pe.matmul(ps[:, j, a:b], pw[:, (j * KQ + k) * P:(j * KQ + k + 1) * P], zq[:, k, a:b],
                                            start=(k == 0), stop=(k == KQ - 1))
                    ins.then_inc(q_done.sem, q_done.mark((l, h2, j)))
                for k in range(KKV):
                    for a, b in spans(TOK):
                        ins = pe.matmul(ps[:, 2, a:b], pw[:, (6 + k) * P:(7 + k) * P], zkv[:, k, a:b],
                                        start=(k == 0), stop=(k == KKV - 1))
                ins.then_inc(k_done.sem, k_done.mark((l, h2)))
                for b in range(TOK // P):
                    for k in range(KKV):
                        ins = pe.matmul(ps[:, 3, b * P:b * P + P], zkv[:, k, b * P:b * P + P],
                                        pw[:, (8 + k) * P:(9 + k) * P], start=(k == 0), stop=(k == KKV - 1),
                                        skip_group_check=True)
                ins.then_inc(v_done.sem, v_done.mark((l, h2)))
                pe.wait_ge(ropes.sem, ropes.at(("q", l, h2, 1, 2)))
                pe.wait_ge(q_act.sem, q_act.at((l, h2, 1)))
                pe.wait_ge(k_act.sem, k_act.at((l, h2)))
                pe.wait_ge(v_act.sem, v_act.at((l, h2)))
                units = [(j, b) for j in range(2) for b in range(nq)]

                def scores(u):
                    j, b = units[u]
                    if u >= 2:
                        pe.wait_ge(exp_ready.sem, exp_ready.at((l, h2, u - 2)))
                    keys = spans(TOK) if b < 4 else [(512, 768)]
                    for a, e in keys:
                        ins = pe.matmul(ps[:, u % 2, a:e], qq[0:96, j, b * P:b * P + P], kk[0:96, j, a:e],
                                        start=True, stop=True)
                    ins.then_inc(sc_done.sem, sc_done.mark((l, h2, u)))

                def mix(u):
                    j, b = units[u]
                    pe.wait_ge(pt_evac.sem, pt_evac.at((l, h2, u)))
                    o = ps[j * VH:(j + 1) * VH, 3, 0:512] if b == 3 else ps[j * VH:(j + 1) * VH, 3, 512:768]
                    kb = range(6) if b < 4 else range(4, 6)
                    for c in kb:
                        ins = pe.matmul(o, vv[:, c, j * VH:(j + 1) * VH], pt[:, c, 0:(512 if b == 3 else 256)],
                                        start=(c == kb[0]), stop=(c == 5))
                    ins.then_inc(pv_done.sem, pv_done.mark((l, h2, j, b)))

                scores(0)
                scores(1)
                for u, (j, b) in enumerate(units):
                    if u + 2 < len(units):
                        scores(u + 2)
                    if u and units[u - 1][1] in (3, 5):
                        mix(u - 1)
                    pe.wait_ge(p_ready.sem, p_ready.at((l, h2, u)))
                    if u >= 1:
                        pe.wait_ge(pt_evac.sem, pt_evac.at((l, h2, u - 1)))
                    kb = range(6) if b < 4 else range(4, 6)
                    for c in kb:
                        ins = pe.transpose(ps[:, 2, c * P:c * P + P], pr[:, u % 3, c * P:c * P + P], ident[:, :])
                    ins.then_inc(pt_done.sem, pt_done.mark((l, h2, u)))
                mix(len(units) - 1)
            pe.wait_ge(ol_ready.sem, ol_ready.at((l, 3)))
            pe.wait_ge(ml_ready.sem, ml_ready.at(l))
            for m in range(KD):
                t = t0 + N_IN + 5 * m
                seq = 6 * m
                full = [(k, k) for k in range(KD)]

                def free(i):
                    if i < 4:
                        return
                    mm, r = divmod(i - 4, 6)
                    if r in (0, 3, 5):
                        pe.wait_ge(g_ready.sem, g_ready.at((l, mm, (0, 3, 5).index(r))))
                    else:
                        pe.wait_ge(br_dve.sem, br_dve.at((l, mm, (1, 2, 4).index(r))))

                free(seq)
                wait_w(pe, t)
                product(pe, seq, t, full, hh, hl, n, True, True).then_inc(w_used.sem, w_used.mark(t))
                free(seq + 1)
                free(seq + 2)
                wait_w(pe, t + 1)
                product(pe, seq + 1, t + 1, [(k, k) for k in range(4)], oah, oal, n, True, True).then_inc(
                    br_done.sem, br_done.mark((l, m, 0)))
                product(pe, seq + 2, t + 1, [(4, 0)], osh, osl, n, True, False).then_inc(w_used.sem, w_used.mark(t + 1))
                free(seq + 3)
                wait_w(pe, t + 2)
                product(pe, seq + 3, t + 2, full, hh, hl, n, True, True).then_inc(w_used.sem, w_used.mark(t + 2))
                free(seq + 4)
                wait_w(pe, t + 3)
                product(pe, seq + 2, t + 3, [(0, 1), (1, 2)], osh, osl, n, False, True).then_inc(
                    br_done.sem, br_done.mark((l, m, 1)))
                product(pe, seq + 4, t + 3, [(2, 0), (3, 1), (4, 2)], ofh, ofl, n, True, True).then_inc(
                    w_used.sem, w_used.mark(t + 3))
                free(seq + 5)
                wait_w(pe, t + 4)
                product(pe, seq + 5, t + 4, full, hh, hl, n, True, True).then_inc(w_used.sem, w_used.mark(t + 4))
            pe.wait_ge(m_ready.sem, m_ready.at((l, KD - 1)))
            for m in range(N_OUT):
                w = t0 + N_IN + N_MERGE + m
                if m == 0:
                    pe.wait_ge(msplit_l.sem, msplit_l.at((l, KD - 1)))
                wait_w(pe, w)
                if m >= 4:
                    pe.wait_ge(x_add.sem, x_add.at((l, m - 4)))
                product(pe, m, w, [(k, k) for k in range(KD)], hh, hl, n, True, True).then_inc(
                    w_used.sem, w_used.mark(w))
            pe.wait_ge(x_add.sem, x_add.at((l, KD - 1)))
            pe_rms(pe, (l, 2), n)
            pe.wait_ge(lo_ready.sem, lo_ready.at((l, 2, KD - 1)))
            base = t0 + N_IN + N_MERGE + N_OUT
            w_used.start_loop((l, "mlp"))
            with pe.Fori(0, QUARTERS) as i:
                for m in range(KD):
                    pe.wait_ge(w_split.sem, i * 32 + 2 * (base + m + 1))
                    if m >= 4:
                        pe.wait_ge(relu_ready.sem, relu_ready.at((l, m - 4), i))
                    else:
                        pe.wait_ge(x_add.sem, i * KD + (x_add.book.get((l, KD - 1), (1,))[0]))
                    product(pe, m, m, [(k, k) for k in range(KD)], hh, hl, n, True, True).then_inc(
                        w_used.sem, w_used.mark((l, "m1", m)))
                for m in range(KD):
                    pe.wait_ge(w_split.sem, i * 32 + 2 * (base + KD + m + 1))
                    if m == 0:
                        pe.wait_ge(midl_ready.sem, midl_ready.at((l, KD - 1), i))
                    if m >= 4:
                        pe.wait_ge(x_add.sem, x_add.at((l, "mlp", m - 4), i))
                    product(pe, m, KD + m, [(k, k) for k in range(KD)], midh, midl, n, True, True).then_inc(
                        w_used.sem, w_used.mark((l, "m2", m)))
            w_used.end_loop(QUARTERS)
            pe.wait_ge(x_add.sem, x_add.at((l, "mlp", KD - 1), QUARTERS - 1))

        block = ctx.enter_context(nc.Block())

        @block.tensor
        def _(pe):
            pe.wait_ge(consts_in.sem, consts_in.at(0))
            pe.wait_ge(silu_ready.sem, silu_ready.at(0))
            for l in range(DEPTH):
                pe_ada(pe, ADA_AT[l][0], ADA_AT[l][1] - ADA_AT[l][0])
                pe.wait_ge(prep_dve.sem, prep_dve.at((l, "bin")))
                for q in range(GROUPS // 2):
                    if q >= 2:
                        pe.wait_ge(prep_act.sem, prep_act.at((l, "binT", q - 2)))
                    for j in range(2):
                        for ri in range(2):
                            ins = pe.transpose(ps[:, q % 2, (2 * j + ri) * P:(2 * j + ri + 1) * P],
                                               bin_[:, ri, 2 * q + j, :, :].rearrange("p s q -> p (s q)"), ident[:, :])
                    ins.then_inc(prep_pe.sem, prep_pe.mark((l, "binT", q)))
                pe.wait_ge(prep_act.sem, prep_act.at((l, "binT", GROUPS // 2 - 1)))
                for half in range(2):
                    pe_ada(pe, ADA_AT[l][1 + half], ADA_AT[l][2 + half] - ADA_AT[l][1 + half])
                    pe.wait_ge(prep_dve.sem, prep_dve.at((l, f"cz{half}")))
                    for q in range(6):
                        if q >= 2:
                            pe.wait_ge(prep_act.sem, prep_act.at((l, "v", half, q - 2)))
                        for j in range(2):
                            g = 12 * half + 2 * q + j
                            for ri in range(2):
                                ins = pe.matmul(ps[0:GP, q % 2, j * 240:j * 240 + 240], bb[:, ri, g, :],
                                                cz[:, ri, 2 * q + j, :, :].rearrange("p a b -> p (a b)"),
                                                start=(ri == 0), stop=(ri == 1))
                        ins.then_inc(prep_pe.sem, prep_pe.mark((l, "v", half, q)))
                    pe.wait_ge(prep_act.sem, prep_act.at((l, "v", half, 5)))
            pe_ada(pe, ADA_AT[1][3], DEPTH * ADA_PAIRS - ADA_AT[1][3])
            pe.wait_ge(ada_ready.sem, ada_ready.at(1))
            for l in range(DEPTH):
                pe_layer(pe, l)
            pe_rms(pe, (DEPTH, 1), LAT)

        w_main = A["w_main"]
        n_all = DEPTH * N_TILES

        @block.sync
        def _(sp):
            ada8 = A["ada_w"].rearrange("(a b) p n -> a b p n", b=8)
            for u in range(8):
                sp.dma_start(ada_w[:, u, :], ada8[0, u]).then_inc(ada_full[u].sem, 16)
            with sp.Fori(1, DEPTH * ADA_PAIRS) as i:
                for u in range(8):
                    sp.wait_ge(ada_used[u].sem, i)
                    sp.dma_start(ada_w[:, u, :], ada8[i, u]).then_inc(ada_full[u].sem, 16)
            w2 = w_main.rearrange("(a b) p n -> a b p n", b=RAW_SLOTS)
            for u in range(RAW_SLOTS):
                sp.dma_start(raw[:, u, :], w2[0, u]).then_inc(raw_full[u].sem, 16)
            with sp.Fori(1, n_all // RAW_SLOTS) as i:
                for u in range(RAW_SLOTS):
                    sp.wait_ge(w_split.sem, i * 4 + (2 * u - 2))
                    sp.dma_start(raw[:, u, :], w2[i, u]).then_inc(raw_full[u].sem, 16)

        @block.gpsimd
        def _(pool):
            def split(t0, u, i):
                pool.wait_ge(raw_full[u % 2].sem, i * 32 + 16 * (u // 2 + 1))
                if t0:
                    pool.wait_ge(w_used.sem, i * 4 + (u - 3))
                pool.sem_inc(w_turn.sem, 1)
                pool.tensor_scalar(whi[:, u, :], raw[:, u % 2, :], 1.0, 0.0, ALU.mult, ALU.add).then_inc(w_split.sem, 1)
                pool.wait_ge(w_split.sem, i * 8 + (2 * u + 1))
                pool.tensor_tensor(wlo[:, u, :], raw[:, u % 2, :], whi[:, u, :].bitcast(F32), ALU.subtract).then_inc(
                    w_split.sem, 1)

            pool.wait_ge(ada_turned.sem, DEPTH * ADA_PAIRS * 2)
            for u in range(W_SLOTS):
                split(False, u, 0)
            with pool.Fori(1, n_all // W_SLOTS) as i:
                for u in range(W_SLOTS):
                    split(True, u, i)

        def act_rms(act, key, n):
            for k in range(KD):
                if k >= 2:
                    act.wait_ge(sq_used.sem, sq_used.at((key, k - 2)))
                act.activation(sqt[:, k % 2, 0:n], x[:, k, 0:n], ACT.Square).then_inc(
                    sq_ready.sem, sq_ready.mark((key, k)))
            act.wait_ge(sq_used.sem, sq_used.at((key, KD - 1)))
            act.activation(rstd[:, 0:n], ps[:, 3, 0:n], ACT.Sqrt, bias=eps_col[:, 0:1],
                                              scale=1.0 / D).then_inc(rms_ready.sem, rms_ready.mark(key))

        def act_norm(act, l, w, n):
            act_rms(act, (l, w), n)
            row = 0 if w == 1 else 3
            for k in range(KD):
                act.wait_ge(nt_ready.sem, nt_ready.at((l, w, k)))
                for s, (a, b) in enumerate(spans(n)):
                    ins = act.activation(hh[:, k, a:b], nt[:, k % 2, a:b], ACT.Identity,
                                         bias=ada[:, l, row * KD + k, s:s + 1])
                ins.then_inc(hi_ready.sem, hi_ready.mark((l, w, k)))

        def act_layer(act, l):
            n = TOK if l == 0 else LAT
            act_norm(act, l, 1, TOK)
            act.wait_ge(lo_ready.sem, lo_ready.at((l, 1, KD - 1)))
            if l == 1:
                act.dma_start(x_d, x[:, :, :]).then_inc(x_spilled.sem, x_spilled.mark(l, 16))
                act.wait_ge(x_spilled.sem, x_spilled.at(l))
            act.dma_start(bint[:].rearrange("p g r s -> p (g r s)"), bin_d[l]).then_inc(bint_in.sem, bint_in.mark(l, 16))

            def evacuate(i, dst, p):
                act.wait_ge(w_used.sem, w_used.at(l * N_TILES + i))
                m = TOK if i < 6 else n
                act.copy(dst[:, 0:m], pair(p, m)).then_inc(in_act.sem, in_act.mark((l, i)))

            def square(q, src, k, m):
                if k >= 2:
                    act.wait_ge(sn_used.sem, sn_used.at((l, q, k - 2)))
                act.activation(sq_s[:, k % 2, 0:m], src[:, k, 0:m], ACT.Square).then_inc(sn_sq.sem, sn_sq.mark((l, q, k)))

            act.wait_ge(in_dve.sem, in_dve.at((l, 2)))
            act.dma_start(zs_d[l].rearrange("i p f -> p i f"), zs[:].rearrange("p i s c -> p i (s c)")).then_inc(
                zs_stored.sem, zs_stored.mark(l, 16))
            evacuate(3, zkv[:, 0], 3)
            act.wait_ge(zs_stored.sem, zs_stored.at(l))
            v = zs_d[l].rearrange("i (g p) (s c) -> s p (i g) c", p=GP, s=CH)
            for s in range(CH):
                act.dma_start(us[s * GP:(s + 1) * GP, :, :], v[s]).then_inc(us_in.sem, us_in.mark((l, s), 16))
            evacuate(4, zkv[:, 1], 0)
            act.wait_ge(in_act.sem, in_act.at((l, 4)))
            for k in range(KKV):
                square(1, zkv, k, TOK)
            act.wait_ge(sn_used.sem, sn_used.at((l, 1, KKV - 1)))
            act.activation(rs_s[:, :], ps[:, 2, 0:TOK], ACT.Sqrt, bias=eps_col[:, 0:1], scale=1.0 / (KKV * P)).then_inc(
                sn_root.sem, sn_root.mark((l, 1)))
            for q in range(6):
                act.wait_ge(bu_done.sem, bu_done.at((l, q)))
                for ri in range(2):
                    v = ps[0:64, 3 - q % 2, ri * 512:ri * 512 + 4 * NC].rearrange("p (g c) -> p g c", c=NC)
                    o = ss[0:64, :, ri, 4 * q:4 * q + 4].rearrange("p j g -> p g j")
                    act.copy(o[:, :, 1 + NCC:1 + NC], v[:, :, 0:NCL])
                    ins = act.copy(o[:, :, 1:1 + NCC], v[:, :, NCL:NC])
                ins.then_inc(bu_act.sem, bu_act.mark((l, q)))
            for dst, src in ((dft_l, "dft_l"), (dft_c, "dft_c"), (c64, "c64")):
                act.dma_start(dst[:], A[src]).then_inc(dft_in.sem, dft_in.mark(l, 16))
            for k in range(2):
                evacuate(6 + k, zq[:, k], 2 + k)
                act.wait_ge(in_act.sem, in_act.at((l, 6 + k)))
                square(0, zq, k, n)
            evacuate(8, zq[:, 2], 0)
            evacuate(9, zf[:, 0], 1)
            act.wait_ge(in_act.sem, in_act.at((l, 8)))
            square(0, zq, 2, n)
            act.wait_ge(sn_used.sem, sn_used.at((l, 0, KQ - 1)))
            act.activation(rs_q[:, 0:n], ps[:, 2, 0:n], ACT.Sqrt, bias=eps_col[:, 0:1], scale=1.0 / (KQ * P)).then_inc(
                sn_root.sem, sn_root.mark((l, 0)))
            evacuate(10, zf[:, 1], 3)
            evacuate(11, zf[:, 2], 0)
            for b in range(n // P):
                act.wait_ge(fr_a.sem, fr_a.at((l, b)))
                act.copy(pq[:, b, :, :].rearrange("p i c -> p (i c)"), ps[:, 1 + b % 2, 0:768]).then_inc(
                    fr_pq.sem, fr_pq.mark((l, b)))
            for i in range(3):
                act.wait_ge(fr_b.sem, fr_b.at((l, i)))
                act.copy(of[:, i, 0:n], ps[:, (3, 0, 1)[i], 0:n]).then_inc(fr_evac.sem, fr_evac.mark((l, i)))
            act.wait_ge(sn_scale.sem, sn_scale.at((l, 0)))
            act.dma_start(cout[:].rearrange("p r g s -> p (r g s)"), cout_d[l]).then_inc(cout_in.sem, cout_in.mark(l, 16))
            act.wait_ge(scan.sem, scan.at((l, 1, 7, 3), NC // 8 - SCAN_SPLIT - 1))
            o = snat[0:64].rearrange("p r g c -> p c (r g)")
            v = ss[0:64].rearrange("p j r g -> p j (r g)")
            act.copy(o[:, 0:NCL], v[:, NCC:NC])
            act.copy(o[:, NCL:NC], v[:, 0:NCC]).then_inc(snat_act.sem, snat_act.mark(l))
            act.wait_ge(snat_act.sem, snat_act.at(l))
            act.wait_ge(snat_dve.sem, snat_dve.at(l))
            act.dma_start(toep[:], toep_d[l]).then_inc(toep_in.sem, toep_in.mark(l, 16))
            act.dma_start(wglu[:].rearrange("p k m -> p (k m)"), A["w_glu"][l]).then_inc(
                glu_w_in.sem, glu_w_in.mark(l, 16))
            act.wait_ge(y_evac.sem, y_evac.at((l, 5)))
            for s in range(CH):
                act.dma_start(y_d[l].rearrange("g p s c -> s p g c")[s],
                                                us[s * GP:(s + 1) * GP, :, :]).then_inc(
                                                    y_stored.sem, y_stored.mark(l, 16))
            act.wait_ge(y_stored.sem, y_stored.at(l))
            act.dma_start(yp[:, :, :], y_d[l].rearrange("(i g) p s c -> (g p) i (s c)", i=3)).then_inc(
                y_in.sem, y_in.mark(l, 16))
            act.wait_ge(y_skip.sem, y_skip.at(l))
            act.dma_start(pws[0][:, :], A["w_pair"][l, 0]).then_inc(pw_in[0].sem, pw_in[0].mark((l, 0), 16))
            act.activation(yg[:, :, :], yp[:, :, :], ACT.Gelu_apprx_tanh).then_inc(gelu.sem, gelu.mark(l))
            for o in range(3):
                act.wait_ge(glu_done.sem, glu_done.at((l, o)))
                if o:
                    act.wait_ge(os_ready.sem, os_ready.at((l, o - 1)))
                act.activation(sig[:, :], ps[:, o % 2, 0:TOK], ACT.Sigmoid,
                                                bias=b_glu[:, l, o:o + 1]).then_inc(glu_sig.sem, glu_sig.mark((l, o)))
            act.wait_ge(os_ready.sem, os_ready.at((l, 2)))
            nq = n // P
            for h2 in range(4):
                if h2 < 3:
                    if h2:
                        act.wait_ge(v_done.sem, v_done.at((l, h2 - 1)))
                    act.dma_start(pws[(h2 + 1) % 2][:, :], A["w_pair"][l, h2 + 1]).then_inc(
                        pw_in[(h2 + 1) % 2].sem, pw_in[(h2 + 1) % 2].mark((l, h2 + 1), 16))
                for j in range(2):
                    act.wait_ge(q_done.sem, q_done.at((l, h2, j)))
                    act.copy(qq[0:64, j, 0:n], ps[0:64, j, 0:n]).then_inc(q_act.sem, q_act.mark((l, h2, j)))
                act.wait_ge(k_done.sem, k_done.at((l, h2)))
                act.copy(kk[0:64, 0, :], ps[0:64, 2, 0:TOK])
                act.copy(kk[0:64, 1, :], ps[64:128, 2, 0:TOK]).then_inc(k_act.sem, k_act.mark((l, h2)))
                act.wait_ge(v_done.sem, v_done.at((l, h2)))
                act.copy(vv[:].rearrange("p b v -> p (b v)"), ps[:, 3, 0:TOK]).then_inc(v_act.sem, v_act.mark((l, h2)))
                units = [(j, b) for j in range(2) for b in range(nq)]

                def exponent(u):
                    act.wait_ge(nmax_ready.sem, nmax_ready.at((l, h2, u)))
                    if u >= 3:
                        act.wait_ge(pt_done.sem, pt_done.at((l, h2, u - 3)))
                    a = 0 if units[u][1] < 4 else 512
                    act.activation(pr[:, u % 3, a:TOK], ps[:, u % 2, a:TOK], ACT.Exp,
                                                      bias=nmx[:, u % 4:u % 4 + 1], scale=SCALE,
                                                      accum_out=sm[:, u % 4:u % 4 + 1]).then_inc(
                                                          exp_ready.sem, exp_ready.mark((l, h2, u)))

                exponent(0)
                for u, (j, b) in enumerate(units):
                    if u + 1 < len(units):
                        exponent(u + 1)
                    act.wait_ge(pt_done.sem, pt_done.at((l, h2, u)))
                    q0 = (b % 4) * P
                    if b in (0, 4) and u:
                        act.wait_ge(pv_done.sem, pv_done.at((l, h2, *((j - 1, 3) if nq == 4 else ((j - 1, 5) if b == 0 else (j, 3))))))
                    k0 = 0 if b < 4 else 4
                    act.copy(pt[:, k0:6, q0:q0 + P],
                                              ps[:, 2, k0 * P:TOK].rearrange("p (k q) -> p k q", q=P)).then_inc(
                                                  pt_evac.sem, pt_evac.mark((l, h2, u)))
                act.wait_ge(pv_done.sem, pv_done.at((l, h2, 1, 3 if nq == 4 else 5)))
                act.copy(oah[:, h2, 0:n], ps[:, 3, 0:n]).then_inc(oh_ready.sem, oh_ready.mark((l, h2)))
            for dst, src in ((osh, osm), (ofh, of)):
                ins = act.copy(dst[:, :, 0:n], src[:, :, 0:n])
                ins.then_inc(mh_ready.sem, mh_ready.mark((l, dst is ofh)))
            for m in range(KD):
                for j, b in enumerate((0, 2, 1)):
                    act.wait_ge(w_used.sem, w_used.at(l * N_TILES + N_IN + 5 * m + 2 * j))
                    i = 3 * m + j
                    if i >= 2:
                        act.wait_ge(br_dve.sem, br_dve.at((l, (i - 2) // 3, (i - 2) % 3)))
                    act.activation(gt[:, i % 2, 0:n], pair(6 * m + (0, 3, 5)[j], n), ACT.Tanh,
                                                    bias=b_gate[:, l, b * KD + m:b * KD + m + 1], scale=0.5).then_inc(
                                                        g_ready.sem, g_ready.mark((l, m, j)))
            act.wait_ge(w_used.sem, w_used.at(l * N_TILES + N_IN + N_MERGE - 1))
            act.dma_start(x[:, :, :], A["x_t"] if l == 0 else x_d).then_inc(x_in.sem, x_in.mark(("out", l), 16))
            for k in range(KD):
                act.wait_ge(m_ready.sem, m_ready.at((l, k)))
                act.mul(hh[:, k, 0:n], m_sb[:, k, 0:n], 0.5).then_inc(msplit_h.sem, msplit_h.mark((l, k)))
            act.wait_ge(x_add.sem, x_add.at((l, KD - 1)))
            act_norm(act, l, 2, n)
            act.wait_ge(lo_ready.sem, lo_ready.at((l, 2, KD - 1)))
            for s in (relu_ready, midh_ready):
                s.start_loop((l, "mlp"))
            with act.Fori(0, QUARTERS) as i:
                for m in range(KD):
                    act.wait_ge(w_used.sem, w_used.at((l, "m1", m), i))
                    if m >= 2:
                        act.wait_ge(msq_ready.sem, msq_ready.at((l, m - 2), i))
                    act.activation(mr[:, m % 2, 0:n], pair(m, n), ACT.Relu).then_inc(
                        relu_ready.sem, relu_ready.mark((l, m)))
                    act.wait_ge(relu_ready.sem, relu_ready.at((l, m), i))
                    act.activation(midh[:, m, 0:n], mr[:, m % 2, 0:n], ACT.Square).then_inc(
                        midh_ready.sem, midh_ready.mark((l, m)))
            for s in (relu_ready, midh_ready):
                s.end_loop(QUARTERS)
            act.wait_ge(x_add.sem, x_add.at((l, "mlp", KD - 1), QUARTERS - 1))

        @block.scalar
        def _(act):
            act.dma_start(cvec[:], A["cvec"]).then_inc(cvec_in.sem, cvec_in.mark(0, 16))
            for dst, name in ((ident, "ident"), (rope, "rope"), (ada_b, "ada_b"), (ln, "ln"), (fnorm, "fnorm"),
                              (qkn, "qkn"), (b_gate, "b_gate"), (b_glu, "b_glu"), (ssm_d, "ssm_d")):
                act.dma_start(dst[:], A[name]).then_inc(consts_in.sem, consts_in.mark(0, 16))
            act.wait_ge(cvec_in.sem, cvec_in.at(0))
            act.activation(svec[:], cvec[:], ACT.Silu).then_inc(silu_ready.sem, silu_ready.mark(0))
            def load_ab(l):
                act.dma_start(abuf[:, 0:3, :], A["ssm_a"][l]).then_inc(prep_loaded.sem, prep_loaded.mark(l, 16))
                act.dma_start(b_in[:], A["ssm_b"][l]).then_inc(prep_loaded.sem, prep_loaded.mark(l, 16))

            def load_c(l):
                act.dma_start(c_in[:], A["ssm_c"][l]).then_inc(prep_c_loaded.sem, prep_c_loaded.mark(l, 16))

            def exponents(l):
                act.wait_ge(prep_loaded.sem, prep_loaded.at(l))
                act.activation(abuf[:, 3, :], abuf[:, 2, :], ACT.Exp).then_inc(prep_act.sem, prep_act.mark((l, "dt")))
                act.wait_ge(prep_dve.sem, prep_dve.at((l, "dta")))
                act.activation(abuf[:, 6, :], abuf[:, 4, :], ACT.Exp).then_inc(prep_act.sem, prep_act.mark((l, "mag")))
                act.wait_ge(prep_dve.sem, prep_dve.at((l, "angle")))
                act.activation(abuf[:, 8, :], abuf[:, 7, :], ACT.Sin)
                act.activation(abuf[:, 9, :], abuf[:, 7, :], ACT.Sin, scale=0.5).then_inc(
                    prep_act.sem, prep_act.mark((l, "sin")))

            def evacuate_inputs(l):
                if l:
                    act.wait_ge(prep_stored.sem, prep_stored.at((0, "bin")))
                for q in range(GROUPS // 2):
                    act.wait_ge(prep_pe.sem, prep_pe.at((l, "binT", q)))
                    act.copy(binT[:, 2 * q:2 * q + 2, :, :].rearrange("p g r s -> p (g r s)"), ps[:, q % 2, 0:512]).then_inc(
                        prep_act.sem, prep_act.mark((l, "binT", q)))
                act.wait_ge(prep_act.sem, prep_act.at((l, "binT", GROUPS // 2 - 1)))
                act.dma_start(bin_d[l], binT[:].rearrange("p g r s -> p (g r s)")).then_inc(
                    prep_stored.sem, prep_stored.mark((l, "bin"), 16))

            def evacuate_kernels(l, half):
                if l and half == 0:
                    act.wait_ge(prep_v_stored.sem, prep_v_stored.at(0))
                for q in range(6):
                    act.wait_ge(prep_pe.sem, prep_pe.at((l, "v", half, q)))
                    g = 12 * half + 2 * q
                    act.copy(vsb[:, g:g + 2, :].rearrange("p g f -> p (g f)"), ps[0:GP, q % 2, 0:480]).then_inc(
                        prep_act.sem, prep_act.mark((l, "v", half, q)))
                if half:
                    act.wait_ge(prep_act.sem, prep_act.at((l, "v", 1, 5)))
                    for s in range(CH):
                        act.dma_start(toep_d[l, s * GP:(s + 1) * GP, :, :], vsb[:, :, (7 - s) * GP:(15 - s) * GP]).then_inc(
                            prep_v_stored.sem, prep_v_stored.mark(l, 16))

            def store_outputs(l):
                act.wait_ge(prep_dve.sem, prep_dve.at((l, "cout")))
                act.dma_start(cout_d[l], bin_[:].rearrange("p r g s q -> p (r g s q)")).then_inc(
                    prep_stored.sem, prep_stored.mark((l, "cout"), 16))

            load_ab(0)
            load_c(0)
            exponents(0)
            act_ada(act, 0, 1)
            act_ada(act, 1, ADA_AT[0][1] - 1)
            evacuate_inputs(0)
            act_ada(act, ADA_AT[0][1], ADA_AT[0][2] - ADA_AT[0][1])
            evacuate_kernels(0, 0)
            load_ab(1)
            act_ada(act, ADA_AT[0][2], 1)
            store_outputs(0)
            exponents(1)
            act_ada(act, ADA_AT[0][2] + 1, ADA_AT[0][3] - ADA_AT[0][2] - 1)
            evacuate_kernels(0, 1)
            load_c(1)
            act_ada(act, ADA_AT[1][0], ADA_AT[1][1] - ADA_AT[1][0])
            evacuate_inputs(1)
            act_ada(act, ADA_AT[1][1], ADA_AT[1][2] - ADA_AT[1][1])
            evacuate_kernels(1, 0)
            act.wait_ge(prep_stored.sem, prep_stored.at((1, "bin")))
            act.dma_start(x[:, :, :], A["x_t"]).then_inc(x_in.sem, x_in.mark("first", 16))
            act_ada(act, ADA_AT[1][2], ADA_AT[1][3] - ADA_AT[1][2])
            evacuate_kernels(1, 1)
            store_outputs(1)
            act_ada(act, ADA_AT[1][3], DEPTH * ADA_PAIRS - ADA_AT[1][3])
            act.wait_ge(prep_stored.sem, prep_stored.at((1, "cout")))
            act.wait_ge(prep_v_stored.sem, prep_v_stored.at(1))
            act.wait_ge(prep_dve.sem, prep_dve.at((1, "cz1")))
            act.wait_ge(x_in.sem, x_in.at("first"))
            for l in range(DEPTH):
                act_layer(act, l)
            act_rms(act, (DEPTH, 1), LAT)
            for k in range(KD):
                act.wait_ge(fin_ready.sem, fin_ready.at(k))
                act.dma_start(out[:, k, :], xo[:, k, :]).then_inc(out_stored.sem, out_stored.mark(k, 16))
            act.wait_ge(out_stored.sem, out_stored.at(KD - 1))

        def dve_norm(dve, l, w, n):
            dve.wait_ge(rms_ready.sem, rms_ready.at((l, w)))
            dve.reciprocal(rstd[:, 0:n], rstd[:, 0:n]).then_inc(rstd_ready.sem, rstd_ready.mark((l, w)))
            dve.wait_ge(rstd_ready.sem, rstd_ready.at((l, w)))

            def lo(k):
                dve.wait_ge(hi_ready.sem, hi_ready.at((l, w, k)))
                row = 0 if w == 1 else 3
                for s, (a, b) in enumerate(spans(n)):
                    ins = dve.scalar_tensor_tensor(hl[:, k, a:b], nt[:, k % 2, a:b], ada[:, l, row * KD + k, s:s + 1],
                                                   hh[:, k, a:b].bitcast(F32), ALU.add, ALU.subtract)
                ins.then_inc(lo_ready.sem, lo_ready.mark((l, w, k)))

            for k in range(KD):
                if k >= 2:
                    dve.wait_ge(lo_ready.sem, lo_ready.at((l, w, k - 2)))
                for s, (a, b) in enumerate(spans(n)):
                    ins = dve.scalar_tensor_tensor(nt[:, k % 2, a:b], x[:, k, a:b], gain[:, l, w - 1, k, s:s + 1],
                                                   rstd[:, a:b], ALU.mult, ALU.mult)
                ins.then_inc(nt_ready.sem, nt_ready.mark((l, w, k)))
                if k:
                    lo(k - 1)
            lo(KD - 1)

        def rotate(dve, src, dst, part, n, key):
            dve.tensor_tensor(part[64:96, 0:n], src[64:96, 0:n], rope[64:96, 0:n], ALU.mult).then_inc(
                ropes.sem, ropes.mark((*key, 0)))
            dve.tensor_tensor(dst[0][64:96, 0:n], src[96:128, 0:n], rope[96:128, 0:n], ALU.mult).then_inc(
                ropes.sem, ropes.mark((*key, 1)))
            dve.wait_ge(ropes.sem, ropes.at((*key, 1)))
            dve.tensor_tensor(dst[0][64:96, 0:n], dst[0][64:96, 0:n], part[64:96, 0:n], ALU.add).then_inc(
                ropes.sem, ropes.mark((*key, 2)))
            if len(dst) > 1:
                dve.wait_ge(ropes.sem, ropes.at((*key, 2)))
                dve.tensor_copy(dst[1][64:96, 0:n], dst[0][64:96, 0:n]).then_inc(ropes.sem, ropes.mark((*key, 3)))

        def dve_layer(dve, l):
            n = TOK if l == 0 else LAT
            dve_norm(dve, l, 1, TOK)
            for i in range(3):
                dve.wait_ge(w_used.sem, w_used.at(l * N_TILES + i))
                dve.tensor_copy(zs[:, i, :, :], pair(i, TOK).rearrange("p (c s) -> p s c", s=CH)).then_inc(
                    in_dve.sem, in_dve.mark((l, i)))
            dve.wait_ge(w_used.sem, w_used.at(l * N_TILES + 5))
            rotate(dve, ps[:, 1, :], (kk[:, 0], kk[:, 1]), kk[:, 1], TOK, ("k", l))

            def scale(q, src, rs, kts, m):
                dve.wait_ge(sn_root.sem, sn_root.at((l, q)))
                dve.reciprocal(rs[:, 0:m], rs[:, 0:m]).then_inc(rstd_ready.sem, rstd_ready.mark((l, "s", q)))
                dve.wait_ge(rstd_ready.sem, rstd_ready.at((l, "s", q)))
                for k in range(kts):
                    ins = dve.scalar_tensor_tensor(src[:, k, 0:m], src[:, k, 0:m], qkn[:, l, q * KQ + k:q * KQ + k + 1],
                                                   rs[:, 0:m], ALU.mult, ALU.mult)
                ins.then_inc(sn_scale.sem, sn_scale.mark((l, q)))

            scale(1, zkv, rs_s, KKV, TOK)
            dve.memset(ss[:, 0, :, :], 0.0).then_inc(scan.sem, scan.mark((l, "zero")))
            for q in range(6):
                dve.wait_ge(bu_done.sem, bu_done.at((l, q)))
                for ri in range(2):
                    v = ps[64:128, 3 - q % 2, ri * 512:ri * 512 + 4 * NC].rearrange("p (g c) -> p g c", c=NC)
                    o = ss[64:128, NC:0:-1, ri, 4 * q:4 * q + 4].rearrange("p j g -> p g j")
                    ins = dve.tensor_copy(o, v)
                ins.then_inc(bu_dve.sem, bu_dve.mark((l, q)))
            dve.wait_ge(bu_act.sem, bu_act.at((l, 5)))
            dve.wait_ge(bu_dve.sem, bu_dve.at((l, 5)))
            prev = ss[:, 0:NC, :, :].rearrange("p (a b) r g -> p a b r g", b=8)
            cur = ss[:, 1:NC + 1, :, :].rearrange("p (a b) r g -> p a b r g", b=8)
            go = scan.n

            def steps(part, first, last):
                scan.start_loop((l, part))
                with dve.Fori(first, last) as i:
                    for u in range(8):
                        dve.wait_ge(scan.sem, i * 32 + (4 * u + go))
                        dve.tensor_tensor(sc_t1[:], a8r[:, l], prev[:, i, u], ALU.mult).then_inc(
                            scan.sem, scan.mark((l, part, u, 0)))
                        dve.tensor_tensor(sc_t2[:, ::-1, :], a8i[:, l], prev[:, i, u], ALU.mult).then_inc(
                            scan.sem, scan.mark((l, part, u, 1)))
                        dve.wait_ge(scan.sem, i * 32 + (4 * u + go + 1))
                        dve.tensor_tensor(cur[:, i, u], cur[:, i, u], sc_t1[:], ALU.add).then_inc(
                            scan.sem, scan.mark((l, part, u, 2)))
                        dve.wait_ge(scan.sem, i * 32 + (4 * u + go + 3))
                        dve.tensor_tensor(cur[:, i, u], cur[:, i, u], sc_t2[:], ALU.add).then_inc(
                            scan.sem, scan.mark((l, part, u, 3)))
                scan.end_loop(last - first)

            steps(0, 0, SCAN_SPLIT)
            scale(0, zq, rs_q, KQ, n)
            steps(1, SCAN_SPLIT, NC // 8)
            dve.wait_ge(scan.sem, scan.at((l, 1, 7, 3), NC // 8 - SCAN_SPLIT - 1))
            dve.wait_ge(fr_b.sem, fr_b.at((l, 2)))
            o = snat[64:128].rearrange("p r g c -> p c (r g)")
            v = ss[64:128, NC - 1::-1].rearrange("p j r g -> p j (r g)")
            dve.tensor_copy(o, v).then_inc(snat_dve.sem, snat_dve.mark(l))
            for q in range(6):
                dve.wait_ge(y_done.sem, y_done.at((l, q)))
                dve.tensor_copy(us[:, 4 * q:4 * q + 4, :].rearrange("p g c -> p (g c)"),
                                                ps[:, 1 + q // 2, 512 * (q % 2):512 * (q % 2) + 4 * NC]).then_inc(y_evac.sem, y_evac.mark((l, q)))
            dve.wait_ge(y_in.sem, y_in.at(l))
            for i in range(3):
                ins = dve.scalar_tensor_tensor(yp[:, i, :], zs[:, i].rearrange("p s c -> p (s c)"), ssm_d[:, l, i:i + 1],
                                               yp[:, i, :], ALU.mult, ALU.add)
            ins.then_inc(y_skip.sem, y_skip.mark(l))
            for o in range(3):
                dve.wait_ge(glu_sig.sem, glu_sig.at((l, o)))
                dve.tensor_tensor(osm[:, o, :].rearrange("p (c s) -> p s c", s=CH),
                                                    yg[:, o, :].rearrange("p (s c) -> p s c", s=CH),
                                                    sig[:, :].rearrange("p (s c) -> p s c", s=CH), ALU.mult).then_inc(
                                                        os_ready.sem, os_ready.mark((l, o)))
            nq = n // P
            dve.wait_ge(os_ready.sem, os_ready.at((l, 2)))
            for h2 in range(4):
                for j in range(2):
                    dve.wait_ge(q_done.sem, q_done.at((l, h2, j)))
                    if j or h2:
                        dve.wait_ge(ropes.sem, ropes.at(("q", l, h2 - (1 - j), 1 - j, 2)))
                    rotate(dve, ps[:, j, :], (qq[:, j],), rt, n, ("q", l, h2, j))
                units = [(j, b) for j in range(2) for b in range(nq)]

                def maximum(u):
                    j, b = units[u]
                    dve.wait_ge(sc_done.sem, sc_done.at((l, h2, u)))
                    c = u % 4
                    dve.tensor_reduce(mx[:, c:c + 1], ps[:, u % 2, (0 if b < 4 else 512):TOK],
                                                         AXX, ALU.max).then_inc(
                                                             max_ready.sem, max_ready.mark((l, h2, u)))
                    dve.wait_ge(max_ready.sem, max_ready.at((l, h2, u)))
                    dve.tensor_scalar(nmx[:, c:c + 1], mx[:, c:c + 1], -SCALE, None, ALU.mult).then_inc(
                        nmax_ready.sem, nmax_ready.mark((l, h2, u)))

                maximum(0)
                maximum(1)
                for u, (j, b) in enumerate(units):
                    dve.wait_ge(exp_ready.sem, exp_ready.at((l, h2, u)))
                    c = u % 4
                    dve.reciprocal(rsm[:, c:c + 1], sm[:, c:c + 1]).then_inc(
                        rsum_ready.sem, rsum_ready.mark((l, h2, u)))
                    dve.wait_ge(rsum_ready.sem, rsum_ready.at((l, h2, u)))
                    a = 0 if b < 4 else 512
                    dve.tensor_scalar(pr[:, u % 3, a:TOK], pr[:, u % 3, a:TOK], rsm[:, c:c + 1],
                                                       None, ALU.mult).then_inc(p_ready.sem, p_ready.mark((l, h2, u)))
                    if u + 2 < len(units):
                        maximum(u + 2)
                dve.wait_ge(oh_ready.sem, oh_ready.at((l, h2)))
                dve.tensor_tensor(oal[:, h2, 0:n], ps[:, 3, 0:n], oah[:, h2, 0:n].bitcast(F32),
                                                    ALU.subtract).then_inc(ol_ready.sem, ol_ready.mark((l, h2)))
            for dst, src, hi in ((osl, osm, osh), (ofl, of, ofh)):
                dve.wait_ge(mh_ready.sem, mh_ready.at((l, dst is ofl)))
                ins = dve.tensor_tensor(dst[:, :, 0:n], src[:, :, 0:n], hi[:, :, 0:n].bitcast(F32), ALU.subtract)
            ins.then_inc(ml_ready.sem, ml_ready.mark(l))
            dve.wait_ge(ml_ready.sem, ml_ready.at(l))
            for m in range(KD):
                for j in range(3):
                    dve.wait_ge(g_ready.sem, g_ready.at((l, m, j)))
                    if j < 2:
                        dve.wait_ge(br_done.sem, br_done.at((l, m, j)))
                    else:
                        dve.wait_ge(w_used.sem, w_used.at(l * N_TILES + N_IN + 5 * m + 3))
                    if j == 0 and m:
                        dve.wait_ge(m_ready.sem, m_ready.at((l, m - 1)))
                    if j == 2:
                        dve.wait_ge(m_ready.sem, m_ready.at((l, m, "part")))
                    dve.scalar_tensor_tensor((acc, tmp, tmp)[j][:, 0:n], gt[:, (3 * m + j) % 2, 0:n], 1.0,
                                                             pair(6 * m + (1, 2, 4)[j], n), ALU.add, ALU.mult).then_inc(
                                                                 br_dve.sem, br_dve.mark((l, m, j)))
                    if j == 1:
                        dve.wait_ge(br_dve.sem, br_dve.at((l, m, 1)))
                        dve.tensor_tensor(acc[:, 0:n], acc[:, 0:n], tmp[:, 0:n], ALU.add).then_inc(
                            m_ready.sem, m_ready.mark((l, m, "part")))
                    if j == 2:
                        dve.wait_ge(br_dve.sem, br_dve.at((l, m, 2)))
                        dve.tensor_tensor(m_sb[:, m, 0:n], acc[:, 0:n], tmp[:, 0:n], ALU.add).then_inc(
                            m_ready.sem, m_ready.mark((l, m)))
            for k in range(KD):
                dve.wait_ge(msplit_h.sem, msplit_h.at((l, k)))
                dve.scalar_tensor_tensor(hl[:, k, 0:n], m_sb[:, k, 0:n], 0.5, hh[:, k, 0:n].bitcast(F32),
                                                           ALU.mult, ALU.subtract).then_inc(
                                                               msplit_l.sem, msplit_l.mark((l, k)))

            def residual(m, row):
                for s, (a, b) in enumerate(spans(n)):
                    ins = dve.scalar_tensor_tensor(x[:, m, a:b], pair(m, n)[:, a:b], ada[:, l, row * KD + m, s:s + 1],
                                                   x[:, m, a:b], ALU.mult, ALU.add)
                return ins

            dve.wait_ge(x_in.sem, x_in.at(("out", l)))
            for m in range(KD):
                dve.wait_ge(w_used.sem, w_used.at(l * N_TILES + N_IN + N_MERGE + m))
                residual(m, 2).then_inc(x_add.sem, x_add.mark((l, m)))
            dve_norm(dve, l, 2, n)
            dve.wait_ge(lo_ready.sem, lo_ready.at((l, 2, KD - 1)))
            for s in (msq_ready, midl_ready, x_add):
                s.start_loop((l, "mlp"))
            with dve.Fori(0, QUARTERS) as i:
                for m in range(KD):
                    dve.wait_ge(relu_ready.sem, relu_ready.at((l, m), i))
                    if m >= 2:
                        dve.wait_ge(midl_ready.sem, midl_ready.at((l, m - 2), i))
                    dve.tensor_tensor(ms[:, m % 2, 0:n], mr[:, m % 2, 0:n], mr[:, m % 2, 0:n],
                                                         ALU.mult).then_inc(msq_ready.sem, msq_ready.mark((l, m)))
                    dve.wait_ge(msq_ready.sem, msq_ready.at((l, m), i))
                    dve.wait_ge(midh_ready.sem, midh_ready.at((l, m), i))
                    dve.tensor_tensor(midl[:, m, 0:n], ms[:, m % 2, 0:n],
                                                          midh[:, m, 0:n].bitcast(F32), ALU.subtract).then_inc(
                                                              midl_ready.sem, midl_ready.mark((l, m)))
                for m in range(KD):
                    dve.wait_ge(w_used.sem, w_used.at((l, "m2", m), i))
                    residual(m, 5).then_inc(x_add.sem, x_add.mark((l, "mlp", m)))
            for s in (msq_ready, midl_ready, x_add):
                s.end_loop(QUARTERS)
            dve.wait_ge(x_add.sem, x_add.at((l, "mlp", KD - 1), QUARTERS - 1))

        def dve_prepare(dve, l):
            step = [0]

            def do(ins, key=None):
                step[0] += 1
                k = (l, key or step[0])
                ins.then_inc(prep_dve.sem, prep_dve.mark(k))
                dve.wait_ge(prep_dve.sem, prep_dve.at(k))

            def tt(o, a, b, op, key=None):
                do(dve.tensor_tensor(o, a, b, op), key)

            def cmul(o_re, o_im, xr, xi, yr, yi, ta, tb, negate=False, key=None):
                tt(ta, xr, yr, ALU.mult)
                tt(tb, xi, yi, ALU.mult)
                tt(o_re, ta, tb, ALU.subtract)
                tt(ta, xr, yi, ALU.mult)
                tt(tb, xi, yr, ALU.mult)
                if negate:
                    do(dve.scalar_tensor_tensor(o_im, ta, -1.0, tb, ALU.mult, ALU.subtract), key)
                else:
                    tt(o_im, ta, tb, ALU.add, key)

            e = lambda i: abuf[:, i, :]
            a_re, a_im, dt_, dr, th, mag, r = e(0), e(1), e(3), e(4), e(5), e(6), e(7)
            s1, sh, cs, t, u, ar1, wr, wi = e(8), e(9), e(10), e(11), e(12), e(13), e(14), e(15)
            dve.wait_ge(prep_loaded.sem, prep_loaded.at(l))
            dve.wait_ge(prep_act.sem, prep_act.at((l, "dt")))
            tt(th, dt_, a_im, ALU.mult)
            tt(dr, dt_, a_re, ALU.mult, "dta")
            big, two_pi = 12582912.0, 2 * np.pi
            c1 = 6.28125
            c2 = float(np.float32(np.floor((two_pi - c1) * 2**20) / 2**20))
            c3 = float(np.float32(two_pi - c1 - c2))
            do(dve.tensor_scalar(t, th, float(1 / two_pi), big, ALU.mult, ALU.add))
            do(dve.tensor_scalar(t, t, big, None, ALU.subtract))
            do(dve.scalar_tensor_tensor(r, t, -c1, th, ALU.mult, ALU.add))
            do(dve.scalar_tensor_tensor(r, t, -c2, r, ALU.mult, ALU.add))
            do(dve.scalar_tensor_tensor(r, t, -c3, r, ALU.mult, ALU.add))
            pi = float(np.nextafter(np.float32(np.pi), np.float32(0)))
            do(dve.tensor_scalar(r, r, pi, -pi, ALU.min, ALU.max), "angle")
            dve.wait_ge(prep_act.sem, prep_act.at((l, "mag")))
            dve.wait_ge(prep_act.sem, prep_act.at((l, "sin")))
            tt(t, sh, sh, ALU.mult)
            do(dve.tensor_scalar(cs, t, -2.0, 1.0, ALU.mult, ALU.add))
            p = lambda k: (pw8[:, k, 0, :], pw8[:, k, 1, :])
            do(dve.memset(pw8[:, 0, 0, :], 1.0))
            do(dve.memset(pw8[:, 0, 1, :], 0.0))
            tt(p(1)[0], mag, cs, ALU.mult)
            tt(p(1)[1], mag, s1, ALU.mult)
            for lo_, n_, by in ((1, 1, 1), (1, 2, 2), (1, 4, 4)):
                src = pw8[:, lo_:lo_ + n_]
                dst = pw8[:, lo_ + by:lo_ + by + n_]
                f = pw8[:, by]
                br, bi = (f[:, c].unsqueeze(1).to_broadcast([P, n_, GROUPS]) for c in range(2))
                ta = t1[:, 0:n_ * GROUPS].rearrange("p (a b) -> p a b", b=GROUPS)
                tb = t2[:, 0:n_ * GROUPS].rearrange("p (a b) -> p a b", b=GROUPS)
                cmul(dst[:, :, 0], dst[:, :, 1], src[:, :, 0], src[:, :, 1], br, bi, ta, tb)
            for c in range(2):
                do(dve.tensor_copy(a8r[:, l, c, :], pw8[:, CH, 0, :]))
            do(dve.tensor_copy(a8i[:, l, 0, :], pw8[:, CH, 1, :]))
            do(dve.tensor_scalar(a8i[:, l, 1, :], pw8[:, CH, 1, :], -1.0, None, ALU.mult))
            do(dve.tensor_scalar(ar1, p(1)[0], -1.0, None, ALU.add))
            tt(t, a_re, a_re, ALU.mult)
            tt(u, a_im, a_im, ALU.mult)
            tt(t, t, u, ALU.add)
            do(dve.reciprocal(u, t))
            tt(wr, ar1, a_re, ALU.mult)
            tt(t, p(1)[1], a_im, ALU.mult)
            tt(wr, wr, t, ALU.add)
            tt(wr, wr, u, ALU.mult)
            tt(wi, p(1)[1], a_re, ALU.mult)
            tt(t, ar1, a_im, ALU.mult)
            tt(wi, wi, t, ALU.subtract)
            tt(wi, wi, u, ALU.mult)
            if l:
                dve.wait_ge(prep_pe.sem, prep_pe.at((0, "v", 1, 5)))
                dve.wait_ge(prep_stored.sem, prep_stored.at((0, "cout")))
            wrb, wib = (v.unsqueeze(2).to_broadcast([P, GROUPS, GP]) for v in (wr, wi))
            ta = t1[:, 0:GROUPS * GP].rearrange("p (a b) -> p a b", b=GP)
            tb = t2[:, 0:GROUPS * GP].rearrange("p (a b) -> p a b", b=GP)
            cmul(bb[:, 0], bb[:, 1], b_in[:, 0], b_in[:, 1], wrb, wib, ta, tb)
            fw, bw = slice(0, 64), slice(64, 128)
            do(dve.tensor_copy(p_in[fw], pw8[fw, CH - 1::-1]))
            do(dve.tensor_copy(p_in[bw], pw8[bw, 0:CH]))
            do(dve.tensor_copy(p_out[fw], pw8[fw, 1:CH + 1]))
            do(dve.tensor_copy(p_out[bw], pw8[bw, CH:0:-1]))
            do(dve.memset(p_z[:], 0.0))
            do(dve.tensor_copy(p_z[fw, 7:15], pw8[fw, 0:CH]))
            do(dve.tensor_copy(p_z[bw, 0:8], pw8[bw, CH - 1::-1]))

            def wide(mat, pows, g0, ng, n_, o, negate, key):
                shape = [P, ng, n_, GP]
                f = ng * n_ * GP
                xr, xi = (mat[:, c, g0:g0 + ng].unsqueeze(2).to_broadcast(shape) for c in range(2))
                yr, yi = (pows[:, 0:n_, c, g0:g0 + ng].rearrange("p s g -> p g s").unsqueeze(3).to_broadcast(shape)
                          for c in range(2))
                ta, tb = (v[:, 0:f].rearrange("p (g s q) -> p g s q", g=ng, q=GP) for v in (t1, t2))
                cmul(o[0], o[1], xr, xi, yr, yi, ta, tb, negate, key)

            wide(bb, p_in, 0, GROUPS, CH, (bin_[:, 0], bin_[:, 1]), False, "bin")
            dve.wait_ge(prep_c_loaded.sem, prep_c_loaded.at(l))
            wide(c_in, p_z, 0, 12, 15, (cz[:, 0], cz[:, 1]), True, "cz0")
            dve.wait_ge(prep_pe.sem, prep_pe.at((l, "binT", GROUPS // 2 - 1)))
            wide(c_in, p_out, 0, GROUPS, CH, (bin_[:, 0], bin_[:, 1]), True, "cout")
            dve.wait_ge(prep_pe.sem, prep_pe.at((l, "v", 0, 5)))
            wide(c_in, p_z, 12, 12, 15, (cz[:, 0], cz[:, 1]), True, "cz1")

        @block.vector
        def _(dve):
            dve.memset(ones[:], 1.0).then_inc(ones_ready.sem, ones_ready.mark(0))
            dve.memset(eps_col[:], EPS).then_inc(ones_ready.sem, ones_ready.mark(1))
            dve.wait_ge(ones_ready.sem, ones_ready.at(1))
            for l in range(DEPTH):
                dve_prepare(dve, l)
            dve.wait_ge(consts_in.sem, consts_in.at(0))
            dve.wait_ge(ada_turned.sem, DEPTH * ADA_PAIRS * 2)
            dve.tensor_tensor(
                ada[:].rearrange("p l m c -> p (l m) c"),
                ps[:, 3, 0:DEPTH * ADA_TILES * 2].rearrange("p (m c) -> p m c", c=2),
                ada_b[:].rearrange("p l m -> p (l m)").unsqueeze(2).to_broadcast([P, DEPTH * ADA_TILES, 2]), ALU.add).then_inc(
                    ada_ready.sem, ada_ready.mark(0))
            dve.wait_ge(ada_ready.sem, ada_ready.at(0))
            for l in range(DEPTH):
                for w in range(2):
                    r0 = (1, 4)[w] * KD
                    dve.scalar_tensor_tensor(gain[:, l, w], ada[:, l, r0:r0 + KD, :], 1.0,
                                             ln[:, l, w].unsqueeze(2).to_broadcast([P, KD, 2]), ALU.add, ALU.mult)
            dve.tensor_scalar(b_gate[:], b_gate[:], 0.5, None, ALU.mult).then_inc(ada_ready.sem, ada_ready.mark(1))
            dve.wait_ge(ada_ready.sem, ada_ready.at(1))
            for l in range(DEPTH):
                dve_layer(dve, l)
            dve.wait_ge(rms_ready.sem, rms_ready.at((DEPTH, 1)))
            dve.reciprocal(rstd[:, 0:LAT], rstd[:, 0:LAT]).then_inc(rstd_ready.sem, rstd_ready.mark("fin"))
            dve.wait_ge(rstd_ready.sem, rstd_ready.at("fin"))
            for k in range(KD):
                dve.scalar_tensor_tensor(xo[:, k, :], x[:, k, 0:LAT], fnorm[:, k:k + 1],
                                                            rstd[:, 0:LAT], ALU.mult, ALU.mult).then_inc(
                                                                fin_ready.sem, fin_ready.mark(k))

        for s in signals:
            book[s.name] = s.new


def lay_out(inp):
    f = np.ascontiguousarray
    a = {k: np.asarray(v) for k, v in inp.items()}
    L = DEPTH
    rows = np.concatenate([a["x"][0], a["ctx"][0]], 0)
    t = {"x_t": f(rows.T.reshape(KD, P, TOK).transpose(1, 0, 2))}
    t["cvec"] = f(np.stack([a["c"][0], a["c_ctx"]], -1).reshape(KD, P, 2).transpose(1, 0, 2))

    def tiles(w):
        k, m = w.shape
        return w.reshape(k // P, P, m // P, P).transpose(2, 1, 0, 3).reshape(m // P, P, k)

    def cols(v):
        return np.moveaxis(v.reshape(*v.shape[:-1], -1, P), -1, 0)

    t["ada_w"] = f(a["ada_w"].reshape(L, 4, 2, P, 12, 512).transpose(0, 4, 1, 3, 2, 5).reshape(L * ADA_TILES, P, D))
    t["ada_b"] = f(cols(a["ada_b"]))
    t["ln"] = f(np.stack([cols(a["ln1"]), cols(a["ln2"])], 2))
    t["fnorm"] = f(cols(a["final_norm"]))
    t["qkn"] = f(np.concatenate([cols(a["q_norm"]), cols(a["kv_norm"])], -1))
    t["b_gate"] = f(cols(a["b_gate"]))
    t["b_glu"] = f(cols(a["b_glu"]))
    t["ssm_d"] = f(cols(a["ssm_d"]))
    swap = np.r_[ROPE // 2:ROPE, 0:ROPE // 2]
    main, pairs = [], []
    for l in range(L):
        w = a["w_in"][l]
        r0 = QL + KVL
        kr = w[:, r0:r0 + ROPE]
        kr = np.concatenate([kr, kr[:, swap]], 1)
        f0, s0 = r0 + ROPE, r0 + ROPE + 384
        w = np.concatenate([w[:, s0:], w[:, QL:r0], kr, kr, w[:, :QL], w[:, f0:s0]], 1)
        main.append(tiles(w))
        g = tiles(a["w_gate"][l])
        ba, bf, bs = (tiles(a[n][l]) for n in ("w_br_attn", "w_br_fourier", "w_br_ssm"))
        for m in range(KD):
            one = np.concatenate([ba[m], bs[m][:, :P], bs[m][:, :3 * P]], 1)
            two = np.concatenate([bs[m][:, P:], bf[m], bf[m]], 1)
            main.append(np.stack([g[m], one, g[2 * KD + m], two, g[KD + m]]))
        main.append(tiles(a["w_out"][l]))
        w1, w2 = tiles(a["w_mlp1"][l]), tiles(a["w_mlp2"][l])
        for q in range(QUARTERS):
            main.append(w1[q * KD:(q + 1) * KD])
            main.append(w2[:, :, q * D:(q + 1) * D])
        q = a["w_uq"][l].reshape(QL, HEADS, NOPE + ROPE)
        q = np.concatenate([q, q[:, :, NOPE:][:, :, swap]], 2)
        kv = a["w_ukv"][l].reshape(KVL, HEADS, NOPE + VH)
        for h in range(0, HEADS, 2):
            qt = [tiles(q[:, h + j])[0] for j in range(2)]
            kt = tiles(kv[:, h:h + 2, :NOPE].reshape(KVL, P))[0]
            vt = tiles(kv[:, h:h + 2, NOPE:].reshape(KVL, P))[0]
            pairs.append(np.concatenate([*qt, kt, vt], 1))
    t["w_main"] = f(np.concatenate(main))
    t["w_pair"] = f(np.stack(pairs).reshape(L, HEADS // 2, P, 1280))
    t["w_glu"] = f(np.stack([a["w_glu"][l].reshape(3, P, 384).transpose(1, 0, 2).reshape(P, -1) for l in range(L)]))
    la = []
    for l in range(L):
        re, im = (a[n][l].transpose(0, 2, 1).reshape(P, GROUPS) for n in ("ssm_a_re", "ssm_a_im"))
        st = np.broadcast_to(a["ssm_log_step"][l][:, None, :], (2, NS, GROUPS)).reshape(P, GROUPS)
        la.append(np.stack([re, im, st], 1))
    t["ssm_a"] = f(np.stack(la))
    t["ssm_b"] = f(np.stack([a[n].transpose(0, 1, 3, 2, 4).reshape(L, P, GROUPS, GP)
                             for n in ("ssm_b_re", "ssm_b_im")], 2))
    t["ssm_c"] = f(np.stack([a[n].transpose(0, 1, 4, 2, 3).reshape(L, P, GROUPS, GP)
                             for n in ("ssm_c_re", "ssm_c_im")], 2))
    t["ident"] = np.eye(P, dtype=np.float32)
    half = ROPE // 2
    inv = np.float32(10000.0) ** (-np.arange(0, half, 2, dtype=np.float32) / np.float32(half))
    pos = np.arange(LAT)
    ang = np.concatenate([(pos // 64).astype(np.float32)[:, None] * inv, (pos % 64).astype(np.float32)[:, None] * inv], 1)
    tab = np.zeros((P, TOK), np.float32)
    tab[64:96] = 1.0
    tab[64:80, :LAT] = tab[80:96, :LAT] = np.cos(ang).T
    tab[96:112, :LAT], tab[112:128, :LAT] = -np.sin(ang).T, np.sin(ang).T
    t["rope"] = tab

    def dft(n):
        k = np.outer(np.arange(n), np.arange(n)) % n * (2 * np.pi / n)
        return np.cos(k), np.sin(k)

    for name, n in (("dft_l", LAT), ("dft_c", CTX)):
        c, s = dft(n)
        m = np.stack([c, -s], 1) / np.sqrt(n)
        t[name] = f(m.reshape(n // P, P, 2, n).transpose(1, 0, 2, 3).astype(np.float32))
    c, s = dft(64)
    eye = np.eye(2)
    t["c64"] = f((np.concatenate([np.kron(eye, c), np.kron(eye, s)], 1) / 8.0).astype(np.float32))
    return t


def kernel(**inputs):
    import concourse.bacc as bacc
    from concourse.bass_utils import run_bass_kernel_spmd

    arrays = lay_out(inputs)
    book = {}
    for _ in range(2):
        nc = bacc.Bacc("TRN2", target_bir_lowering=False, num_devices=1)
        aps = {k: nc.dram_tensor(f"in_{k}", v.shape, F32, kind="ExternalInput").ap() for k, v in arrays.items()}
        out = nc.dram_tensor("out_t", (P, KD, LAT), F32, kind="ExternalOutput").ap()
        build(nc, aps, out, book)
    r = run_bass_kernel_spmd(nc, [{f"in_{k}": v for k, v in arrays.items()}], core_ids=[0])
    y = r.results[0]["out_t"]
    return np.ascontiguousarray(y.transpose(2, 1, 0).reshape(1, LAT, D))
```

```python
from contextlib import ExitStack

import numpy as np

import concourse.bass as bass
from concourse import mybir

F32 = mybir.dt.float32
F32R = mybir.dt.float32r
ALU = mybir.AluOpType
ACT = mybir.ActivationFunctionType
AXX = mybir.AxisListType.X

P = 128
D = 1024
KD = D // P
LAT, CTX = 512, 256
TOK = LAT + CTX
DEPTH = 2
HEADS = 8
NOPE, ROPE, VH = 64, 32, 64
QL, KVL = 384, 256
KQ, KKV = QL // P, KVL // P
SCALE = 1.0 / float(np.sqrt(NOPE + ROPE))
GROUPS, GP, NS = 24, 16, 64
CH = 8
NC = TOK // CH
NCL, NCC = LAT // CH, CTX // CH
SCAN_NORM = 12
SCAN_SPLIT = 44
SCAN_EARLY = 64
EPS = 1e-6
N_IN, N_MERGE, N_OUT, QUARTERS = 12, 40, 8, 4
N_TILES = N_IN + N_MERGE + N_OUT + QUARTERS * 16
RAW_SLOTS, W_SLOTS = 2, 4
ADA_TILES = 48
ADA_PAIRS = ADA_TILES // 8
ADA_AT = ((0, 3, 4, 6), (6, 8, 9, 10))


class Signal:

    def __init__(self, sem, book):
        self.sem, self.book, self.new = sem, book, {}
        self.n, self.body, self.first = 0, None, 0

    def mark(self, key, by=1):
        self.n += by
        self.new[key] = (self.n, self.body)
        return by

    def at(self, key, turn=0):
        n, body = self.book.get(key, (1, None))
        if body is not None:
            n = turn * self.book["loop", body] + n
        return n

    def start_loop(self, name):
        self.body, self.first = name, self.n

    def end_loop(self, turns):
        k = self.n - self.first
        self.new["loop", self.body] = k
        self.n += (turns - 1) * k
        self.body = None


def build(nc, A, out, book):
    ctx = ExitStack()
    with ctx:
        BASE = 16512
        CONST, RING = BASE, BASE + 8192
        HREG = RING + (RAW_SLOTS + 2 * W_SLOTS) * KD * P * 4
        REST = HREG + 2 * KD * TOK * 4

        def at(name, off, shape, dt=F32):
            return nc.alloc_sbuf_tensor_at(name, shape, dt, offset=off)

        place = [CONST]

        def const(name, shape):
            t = at(name, place[0], shape)
            n = 4
            for s in shape[1:]:
                n *= s
            place[0] += -(-n // 32) * 32
            assert place[0] <= RING
            return t

        ident = const("ident", [P, P])
        ones = const("ones", [P, P])
        rope = const("rope", [P, TOK])
        ada = const("ada", [P, DEPTH, ADA_TILES, 2])
        ada_b = const("ada_b", [P, DEPTH, ADA_TILES])
        ln = const("ln", [P, DEPTH, 2, KD])
        gain = const("gain", [P, DEPTH, 2, KD, 2])
        fnorm = const("fnorm", [P, KD])
        qkn = const("qkn", [P, DEPTH, KQ + KKV])
        b_gate = const("b_gate", [P, DEPTH, 3 * KD])
        b_glu = const("b_glu", [P, DEPTH, 3])
        ssm_d = const("ssm_d", [P, DEPTH, 3])
        cvec = const("cvec", [P, KD, 2])
        svec = const("svec", [P, KD, 2])
        eps_col = const("eps_col", [P, 1])
        a8 = const("a8", [P, DEPTH, 2, 2, GROUPS])
        terms = const("terms", [P, 2, 2, GROUPS])
        mx = const("mx", [P, 4])
        nmx = const("nmx", [P, 4])
        sm = const("sm", [P, 4])
        rsm = const("rsm", [P, 4])

        raw = at("raw", RING, [P, RAW_SLOTS, KD * P])
        whi = at("whi", RING + RAW_SLOTS * 4096, [P, W_SLOTS, KD * P], F32R)
        wlo = at("wlo", RING + (RAW_SLOTS + W_SLOTS) * 4096, [P, W_SLOTS, KD * P], F32R)
        hh = at("hh", HREG, [P, KD, TOK], F32R)
        hl = at("hl", HREG + KD * TOK * 4, [P, KD, TOK], F32R)

        def rest(name, off, shape, dt=F32):
            return at(name, REST + off, shape, dt)

        zq = rest("zq", 0, [P, KQ, TOK])
        zkv = rest("zkv", 9216, [P, KKV, TOK])
        kk = rest("kk", 15360, [P, 2, TOK])
        zf = rest("zf", 21504, [P, 3, TOK])
        of = rest("of", 21504, [P, 3, TOK])
        zs = rest("zs", 30720, [P, 3, CH, NC])
        us = rest("us", 39936, [P, GROUPS, NC])
        osm = rest("osm", 39936, [P, 3, TOK])
        snat = rest("snat", 49152, [P, 2, GROUPS, NC])
        yp = rest("yp", 49152, [P, 3, TOK])
        yg = rest("yg", 58368, [P, 3, TOK])
        ss = rest("ss", 67584, [P, NC + 1, 2, GROUPS])
        bint = rest("bint", 89088, [P, GROUPS, 2, P])
        cout = rest("cout", 89088, [P, 2, GROUPS, P])
        toep = rest("toep", 67584, [P, GROUPS, P])
        wglu = rest("wglu", 79872, [P, 3, 3 * P])
        pq = rest("pq", 49152, [P, TOK // P, 3, 2 * P])
        dft_l = rest("dft_l", 89088, [P, LAT // P, 2, LAT])
        dft_c = rest("dft_c", 105472, [P, CTX // P, 2, CTX])
        c64 = rest("c64", 109568, [P, 2 * P])
        qq = rest("qq", 49152, [P, 2, TOK])
        vv = rest("vv", 55296, [P, TOK // P, P])
        pr = rest("pr", 58368, [P, 3, TOK])
        pt = rest("pt", 67584, [P, TOK // P, LAT])
        pws = (rest("pw0", 30720, [P, 1280]), rest("pw1", 79872, [P, 1280]))
        pw_first = rest("pw_first", 86208, [P, (KQ + KKV) * P])
        rt = rest("rt", 84992, [P, TOK])
        oah = rest("oah", 89088, [P, 4, TOK], F32R)
        oal = rest("oal", 89088 + 12288, [P, 4, TOK], F32R)
        m_sb = rest("m_sb", 0, [P, KD, TOK])
        gt = rest("gt", 24576, [P, 2, TOK])
        acc = rest("acc", 30720, [P, TOK])
        tmp = rest("tmp", 33792, [P, TOK])
        osh = rest("osh", 49152, [P, 3, TOK], F32R)
        osl = rest("osl", 58368, [P, 3, TOK], F32R)
        ofh = rest("ofh", 67584, [P, 3, TOK], F32R)
        ofl = rest("ofl", 76800, [P, 3, TOK], F32R)
        x = rest("x", 49152, [P, KD, TOK])
        nt = rest("nt", 0, [P, 2, TOK])
        sqt = rest("sqt", 73728, [P, 2, TOK])
        sqa = rest("sqa", 79872, [P, TOK])
        root = rest("root", 6144, [P, TOK // 64])
        diag = rest("diag", 12288, [P, TOK])
        sq_s = rest("sq_s", 49152, [P, 2, TOK])
        rs_s = rest("rs_s", 55296, [P, TOK])
        rs_q = rest("rs_q", 110592, [P, TOK])
        midh = rest("midh", 0, [P, KD, TOK], F32R)
        midl = rest("midl", 24576, [P, KD, TOK], F32R)
        mr = rest("mr", 73728, [P, 2, TOK])
        ms = rest("ms", 79872, [P, 2, TOK])
        xo = rest("xo", 73728, [P, KD, LAT])
        t1 = rest("t1", 0, [P, 3072])
        t2 = rest("t2", 12288, [P, 3072])
        bin_ = rest("bin", 24576, [P, 2, GROUPS, CH, GP])
        binT = rest("binT", 49152, [P, GROUPS, 2, P])
        cz = rest("cz", 73728, [P, 2, 12, 15, GP])
        b_in = rest("b_in", 96768, [P, 2, GROUPS, GP])
        c_in = rest("c_in", 99840, [P, 2, GROUPS, GP])
        bb = rest("bb", 102912, [P, 2, GROUPS, GP])
        pw8 = rest("pw8", 105984, [P, CH + 1, 2, GROUPS])
        p_in = rest("p_in", 107712, [P, CH, 2, GROUPS])
        p_out = rest("p_out", 109248, [P, CH, 2, GROUPS])
        p_z = rest("p_z", 110784, [P, 15, 2, GROUPS])
        vsb = at("vsb", HREG, [GP, GROUPS, 15 * GP])
        ada_w = at("ada_w", RING + RAW_SLOTS * 4096, [P, 8, D])
        abuf = at("abuf", HREG + 39424, [P, 24, GROUPS])
        ada_rows = at("ada_rows", HREG + 41728, [2, 2, 512])

        ps = ctx.enter_context(nc.psum_tensor("ps", [P, 4, 1024], F32))

        def dram(name, shape):
            return nc.dram_tensor(name, shape, F32, kind="Internal").ap()

        bin_d = dram("bin_d", (DEPTH, P, GROUPS * 2 * P))
        cout_d = dram("cout_d", (DEPTH, P, GROUPS * 2 * P))
        toep_d = dram("toep_d", (DEPTH, P, GROUPS, P))
        zs_d = dram("zs_d", (DEPTH, 3, P, TOK))
        y_d = dram("y_d", (DEPTH, GROUPS, GP, CH, NC))
        x_d = dram("x_d", (P, KD, TOK))

        signals = []

        def signal(name):
            signals.append(Signal(ctx.enter_context(nc.semaphore(name)), book.setdefault(name, {})))
            signals[-1].name = name
            return signals[-1]

        consts_in = signal("consts_in")
        ident_in = signal("ident_in")
        cvec_in = signal("cvec_in")
        ada_used = [signal(f"ada_used{u}") for u in range(8)]
        ada_row = [signal(f"ada_row{j}") for j in range(2)]
        ada_turned = signal("ada_turned")
        ada_ready = signal("ada_ready")
        silu_ready = signal("silu_ready")
        w_turn = signal("w_turn")
        w_split = signal("w_split")
        w_used = signal("w_used")
        ones_ready = signal("ones_ready")
        ada_full = [signal(f"ada_full{u}") for u in range(8)]
        raw_full = [signal(f"raw_full{u}") for u in range(RAW_SLOTS)]
        prep_loaded = signal("prep_loaded")
        prep_c_loaded = signal("prep_c_loaded")
        prep_act = signal("prep_act")
        prep_dve = signal("prep_dve")
        prep_pe = signal("prep_pe")
        prep_stored = signal("prep_stored")
        prep_v_stored = signal("prep_v_stored")
        x_in = signal("x_in")
        x_spilled = signal("x_spilled")
        sq_ready = signal("sq_ready")
        sq_used = signal("sq_used")
        sq_summed = signal("sq_summed")
        rms_ready = signal("rms_ready")
        rstd_ready = signal("rstd_ready")
        diag_ready = signal("diag_ready")
        rstd_spread = signal("rstd_spread")
        nt_ready = signal("nt_ready")
        hi_ready = signal("hi_ready")
        lo_ready = signal("lo_ready")
        in_act = signal("in_act")
        in_dve = signal("in_dve")
        ropes = signal("ropes")
        sn_sq = signal("sn_sq")
        sn_used = signal("sn_used")
        sn_root = signal("sn_root")
        sn_scale = signal("sn_scale")
        dft_in = signal("dft_in")
        fr_a = signal("fr_a")
        fr_pq = signal("fr_pq")
        fr_b = signal("fr_b")
        fr_tab = signal("fr_tab")
        fr_evac = signal("fr_evac")
        zs_stored = signal("zs_stored")
        us_in = signal("us_in")
        bint_in = signal("bint_in")
        cout_in = signal("cout_in")
        toep_in = signal("toep_in")
        glu_w_in = signal("glu_w_in")
        bu_done = signal("bu_done")
        bu_act = signal("bu_act")
        bu_dve = signal("bu_dve")
        scan = signal("scan")
        snat_act = signal("snat_act")
        snat_dve = signal("snat_dve")
        y_done = signal("y_done")
        y_evac = signal("y_evac")
        y_stored = [signal(f"y_stored{i}") for i in range(3)]
        y_in = [signal(f"y_in{i}") for i in range(3)]
        y_skip = signal("y_skip")
        gelu = signal("gelu")
        glu_done = signal("glu_done")
        glu_sig = signal("glu_sig")
        os_ready = signal("os_ready")
        pw_first_in = signal("pw_first_in")
        pw_in = [signal(f"pw_in{j}") for j in range(2)]
        q_done = signal("q_done")
        q_act = signal("q_act")
        k_done = signal("k_done")
        k_act = signal("k_act")
        v_done = signal("v_done")
        v_act = signal("v_act")
        sc_done = signal("sc_done")
        max_ready = signal("max_ready")
        nmax_ready = signal("nmax_ready")
        exp_ready = signal("exp_ready")
        rsum_ready = signal("rsum_ready")
        p_ready = signal("p_ready")
        pt_done = signal("pt_done")
        pt_evac = signal("pt_evac")
        pv_done = signal("pv_done")
        oh_ready = signal("oh_ready")
        ol_ready = signal("ol_ready")
        mh_ready = signal("mh_ready")
        ml_ready = signal("ml_ready")
        g_ready = signal("g_ready")
        br_done = signal("br_done")
        br_dve = signal("br_dve")
        m_ready = signal("m_ready")
        msplit_h = signal("msplit_h")
        msplit_l = signal("msplit_l")
        x_add = signal("x_add")
        relu_ready = signal("relu_ready")
        midh_ready = signal("midh_ready")
        msq_ready = signal("msq_ready")
        midl_ready = signal("midl_ready")
        fin_ready = signal("fin_ready")
        out_stored = signal("out_stored")

        def pair(p, n):
            return ps[:, p % 4, 0:n]

        def spans(n):
            return [(0, 512)] + ([(512, 768)] if n > 512 else [])

        def product(pe, p, w, kts, xh, xl, n, first, last):
            ins = None
            for i, (kw, kx) in enumerate(kts):
                for j, (ww, xx) in enumerate(((whi, xh), (whi, xl), (wlo, xh))):
                    for a, b in spans(n):
                        ins = pe.matmul(ps[:, p % 4, a:b], ww[:, w % W_SLOTS, kw * P:(kw + 1) * P],
                                        xx[:, kx, a:b], start=(first and i == 0 and j == 0),
                                        stop=(last and i == len(kts) - 1 and j == 2))
            return ins

        def product_step(pe, p, w, k, xh, xl, n):
            return product(pe, p, w, [(k, k)], xh, xl, n, k == 0, k == KD - 1)

        def wait_w(pe, t):
            pe.wait_ge(w_split.sem, 2 * (t + 1))

        def pe_norm(pe, key, n):
            pe.wait_ge(sq_used.sem, sq_used.at((key, KD - 1)))
            for b in range(n // P):
                ins = pe.matmul(ps[:, 3, 2 * b:2 * b + 2], sqa[:, b * P:b * P + P], ones[:, 0:2], start=True, stop=True)
            ins.then_inc(sq_summed.sem, sq_summed.mark(key))
            pe.wait_ge(diag_ready.sem, diag_ready.at(key))
            for a, b in spans(n):
                ins = pe.matmul(ps[:, 3, a:b], ones[:, :], diag[:, a:b], start=True, stop=True)
            ins.then_inc(rstd_spread.sem, rstd_spread.mark(key))

        def pe_ada(pe, first, turns):
            o = ps[:, 3, 0:DEPTH * ADA_TILES * 2].rearrange("p (a b c) -> p a b c", b=8, c=2)
            with pe.Fori(first, first + turns) as i:
                for j in range(2):
                    for u in range(4):
                        pe.wait_ge(ada_full[4 * j + u].sem, i * 16 + 16)
                        for k in range(2):
                            ins = pe.matmul(ps[0:2, 2, 512 * j:512 * j + 512], svec[:, 2 * u + k, :],
                                            ada_w[:, 4 * j + u, 512 * k:512 * k + 512], start=(u == 0 and k == 0),
                                            stop=(u == 3 and k == 1))
                        ins.then_inc(ada_used[4 * j + u].sem, 1)
                for j in range(2):
                    pe.wait_ge(ada_row[j].sem, i + 1)
                    for q in range(4):
                        ins = pe.matmul(o[:, i, 4 * j + q, :], ada_rows[:, j, q * P:(q + 1) * P], ident[0:2, 0:2],
                                        start=True, stop=True, skip_group_check=True)
                    ins.then_inc(ada_turned.sem, 1)

        def act_ada(act, first, turns):
            with act.Fori(first, first + turns) as i:
                for j in range(2):
                    act.wait_ge(ada_used[4 * j + 3].sem, i + 1)
                    if first:
                        act.wait_ge(ada_turned.sem, i * 2 + (j - 1))
                    act.copy(ada_rows[:, j, :], ps[0:2, 2, 512 * j:512 * j + 512]).then_inc(ada_row[j].sem, 1)

        def pe_layer(pe, l):
            n = TOK if l == 0 else LAT
            t0 = l * N_TILES
            if l == 0:
                pe_norm(pe, (0, 1), TOK)
            full = [(k, k) for k in range(KD)]

            def tile(i, p):
                wait_w(pe, t0 + i)
                product(pe, p, t0 + i, full, hh, hl, TOK if i < 6 else n, True, True).then_inc(
                    w_used.sem, w_used.mark(t0 + i))

            def square_sums(q, kts, m):
                for k in range(kts):
                    pe.wait_ge(sn_sq.sem, sn_sq.at((l, q, k)))
                    for a, b in spans(m):
                        ins = pe.matmul(ps[:, 2, a:b], ones[:, :], sq_s[:, k % 2, a:b],
                                        start=(k == 0), stop=(k == kts - 1))
                    ins.then_inc(sn_used.sem, sn_used.mark((l, q, k)))

            for i in range(3):
                wait_w(pe, t0 + i)
            for k in range(KD):
                pe.wait_ge(lo_ready.sem, lo_ready.at((l, 1, k)))
                for i in range(3):
                    ins = product_step(pe, i, t0 + i, k, hh, hl, TOK)
                    if k == KD - 1:
                        ins.then_inc(w_used.sem, w_used.mark(t0 + i))
            tile(3, 3)
            pe.wait_ge(in_dve.sem, in_dve.at((l, 0)))
            tile(4, 0)
            pe.wait_ge(in_dve.sem, in_dve.at((l, 2)))
            square_sums(1, KKV, TOK)
            pe.wait_ge(us_in.sem, us_in.at((l, CH - 1)))
            pe.wait_ge(bint_in.sem, bint_in.at(l))
            pe.wait_ge(in_act.sem, in_act.at((l, 3)))
            for q in range(6):
                if q == 1:
                    pe.wait_ge(sn_root.sem, sn_root.at((l, 1)))
                if q >= 2:
                    pe.wait_ge(bu_act.sem, bu_act.at((l, q - 2)))
                    pe.wait_ge(bu_dve.sem, bu_dve.at((l, q - 2)))
                for ri in range(2):
                    for j in range(4):
                        g = 4 * q + j
                        ins = pe.matmul(ps[:, 3 - q % 2, ri * 512 + j * NC:ri * 512 + (j + 1) * NC], bint[:, g, ri, :],
                                        us[:, g, :], start=True, stop=True)
                ins.then_inc(bu_done.sem, bu_done.mark((l, q)))
            pe.wait_ge(bu_act.sem, bu_act.at((l, 5)))
            pe.wait_ge(bu_dve.sem, bu_dve.at((l, 5)))
            tile(5, 1)
            tile(6, 2)
            tile(7, 3)
            pe.wait_ge(in_act.sem, in_act.at((l, 4)))
            tile(8, 0)
            pe.wait_ge(in_act.sem, in_act.at((l, 5)))
            tile(9, 1)
            pe.wait_ge(in_act.sem, in_act.at((l, 6)))
            square_sums(0, KQ, n)
            pe.wait_ge(in_act.sem, in_act.at((l, 7)))
            tile(10, 3)
            pe.wait_ge(in_act.sem, in_act.at((l, 8)))
            tile(11, 0)
            pe.wait_ge(dft_in.sem, dft_in.at(l))
            pe.wait_ge(in_act.sem, in_act.at((l, N_IN - 1)))
            pe.wait_ge(sn_root.sem, sn_root.at((l, 0)))
            blocks = range(n // P)
            for b in blocks:
                if b >= 2:
                    pe.wait_ge(fr_pq.sem, fr_pq.at((l, b - 2)))
                for i in range(3):
                    ins = pe.matmul(ps[:, 1 + b % 2, i * 256:i * 256 + 256], zf[:, i, b * P:b * P + P],
                                    c64[:, :], start=True, stop=True)
                ins.then_inc(fr_a.sem, fr_a.mark((l, b)))
            pe.wait_ge(fr_pq.sem, fr_pq.at((l, len(blocks) - 1)))
            for tab, a, e, b0, nb in ((dft_l, 0, LAT, 0, 4),) + ((dft_c, LAT, TOK, 4, 2),) * (n > LAT):
                for b in range(nb):
                    for i in range(3):
                        for cs in range(2):
                            ins = pe.matmul(ps[:, (3, 0, 1)[i], a:e], pq[:, b0 + b, i, cs * P:cs * P + P],
                                            tab[:, b, cs, :], start=(b == 0 and cs == 0),
                                            stop=(b == nb - 1 and cs == 1))
                        if b0 + b == n // P - 1:
                            ins.then_inc(fr_b.sem, fr_b.mark((l, i)))
                    if b0 + b in (1, 3) and b0 + b < n // P - 1:
                        ins.then_inc(fr_tab.sem, fr_tab.mark((l, b)))
            def project_q(h2, j, kts=range(KQ)):
                first = h2 == 0 and j == 0
                if j == 0 and kts[0] == 0 and not first:
                    pe.wait_ge(pw_in[h2 % 2].sem, pw_in[h2 % 2].at((l, h2)))
                w = pw_first if first else pws[h2 % 2]
                for k in kts:
                    for a, b in spans(n):
                        ins = pe.matmul(ps[:, j, a:b], w[:, (j * KQ + k) * P:(j * KQ + k + 1) * P],
                                        zq[:, k, a:b], start=(k == 0), stop=(k == KQ - 1))
                if kts[-1] == KQ - 1:
                    ins.then_inc(q_done.sem, q_done.mark((l, h2, j)))

            def project_k(h2):
                w, k0 = (pws[h2 % 2], 2 * KQ) if h2 else (pw_first, KQ)
                for k in range(KKV):
                    for a, b in spans(TOK):
                        ins = pe.matmul(ps[:, 2, a:b], w[:, (k0 + k) * P:(k0 + k + 1) * P], zkv[:, k, a:b],
                                        start=(k == 0), stop=(k == KKV - 1))
                ins.then_inc(k_done.sem, k_done.mark((l, h2)))

            def project_v(h2):
                for b in range(TOK // P):
                    for k in range(KKV):
                        ins = pe.matmul(ps[:, 3, b * P:b * P + P], zkv[:, k, b * P:b * P + P],
                                        pws[h2 % 2][:, (8 + k) * P:(9 + k) * P], start=(k == 0), stop=(k == KKV - 1),
                                        skip_group_check=True)
                ins.then_inc(v_done.sem, v_done.mark((l, h2)))

            pe.wait_ge(pw_first_in.sem, pw_first_in.at(l))
            pe.wait_ge(sn_scale.sem, sn_scale.at((l, 0)))
            project_k(0)
            pe.wait_ge(fr_evac.sem, fr_evac.at((l, 1)))
            project_q(0, 0)
            pe.wait_ge(fr_evac.sem, fr_evac.at((l, 2)))
            pe.wait_ge(snat_act.sem, snat_act.at(l))
            pe.wait_ge(snat_dve.sem, snat_dve.at(l))
            pe.wait_ge(cout_in.sem, cout_in.at(l))
            pe.wait_ge(toep_in.sem, toep_in.at(l))
            for g in range(GROUPS):
                q, j = divmod(g, 4)
                if g == 8:
                    pe.wait_ge(k_act.sem, k_act.at((l, 0)))
                o = ps[:, 1 + q // 2, 512 * (q % 2) + j * NC:512 * (q % 2) + (j + 1) * NC]
                pe.matmul(o, cout[:, 0, g, :], snat[:, 0, g, :], start=True, stop=False)
                pe.matmul(o, cout[:, 1, g, :], snat[:, 1, g, :], start=False, stop=False)
                ins = pe.matmul(o, toep[:, g, :], us[:, g, :], start=False, stop=True)
                if j == 3:
                    ins.then_inc(y_done.sem, y_done.mark((l, q)))
            pe.wait_ge(glu_w_in.sem, glu_w_in.at(l))
            pe.wait_ge(y_evac.sem, y_evac.at((l, 5)))
            for k in range(3):
                pe.wait_ge(gelu.sem, gelu.at((l, k)))
                for o in range(3):
                    for a, b in spans(TOK):
                        ins = pe.matmul(ps[:, 1 + o, a:b], wglu[:, k, o * P:o * P + P], yg[:, k, a:b],
                                        start=(k == 0), stop=(k == 2))
                    if k == 2:
                        ins.then_inc(glu_done.sem, glu_done.mark((l, o)))
            nq = n // P
            for h2 in range(4):
                if h2:
                    project_k(h2)
                else:
                    pe.wait_ge(glu_sig.sem, glu_sig.at((l, 2)))
                    pe.wait_ge(pw_in[0].sem, pw_in[0].at((l, 0)))
                project_q(h2, 1)
                pe.wait_ge(ropes.sem, ropes.at(("q", l, h2, 0, 2)))
                pe.wait_ge(q_act.sem, q_act.at((l, h2, 0)))
                pe.wait_ge(k_act.sem, k_act.at((l, h2)))
                if h2 == 0:
                    pe.wait_ge(ropes.sem, ropes.at(("k", l, 3)))
                units = [(j, b) for j in range(2) for b in range(nq)]

                def scores(u):
                    j, b = units[u]
                    if u == 1:
                        pe.wait_ge(ropes.sem, ropes.at(("q", l, h2, 1, 2)))
                        pe.wait_ge(q_act.sem, q_act.at((l, h2, 1)))
                    if u >= 2:
                        pe.wait_ge(exp_ready.sem, exp_ready.at((l, h2, u - 2)))
                    keys = spans(TOK) if b < 4 else [(512, 768)]
                    for a, e in keys:
                        ins = pe.matmul(ps[:, u % 2, a:e], qq[0:96, j, b * P:b * P + P], kk[0:96, j, a:e],
                                        start=True, stop=True)
                    ins.then_inc(sc_done.sem, sc_done.mark((l, h2, u)))

                def mix(u):
                    j, b = units[u]
                    if u == 3:
                        pe.wait_ge(v_act.sem, v_act.at((l, h2)))
                    pe.wait_ge(pt_evac.sem, pt_evac.at((l, h2, u)))
                    o = ps[j * VH:(j + 1) * VH, 3, 0:512] if b == 3 else ps[j * VH:(j + 1) * VH, 3, 512:768]
                    kb = range(6) if b < 4 else range(4, 6)
                    for c in kb:
                        ins = pe.matmul(o, vv[:, c, j * VH:(j + 1) * VH], pt[:, c, 0:(512 if b == 3 else 256)],
                                        start=(c == kb[0]), stop=(c == 5))
                    ins.then_inc(pv_done.sem, pv_done.mark((l, h2, j, b)))

                scores(0)
                if h2:
                    pe.wait_ge(ol_ready.sem, ol_ready.at((l, h2 - 1)))
                project_v(h2)
                scores(1)
                for u, (j, b) in enumerate(units):
                    if u + 2 < len(units):
                        scores(u + 2)
                    if u and units[u - 1][1] in (3, 5):
                        mix(u - 1)
                    if h2 < 3 and u >= len(units) - 2:
                        pe.wait_ge(exp_ready.sem, exp_ready.at((l, h2, len(units) - 2)))
                        project_q(h2 + 1, 0, range(u - len(units) + 2, u - len(units) + 3))
                    pe.wait_ge(p_ready.sem, p_ready.at((l, h2, u)))
                    if u >= 1:
                        pe.wait_ge(pt_evac.sem, pt_evac.at((l, h2, u - 1)))
                    kb = range(6) if b < 4 else range(4, 6)
                    for c in kb:
                        ins = pe.transpose(ps[:, 2, c * P:c * P + P], pr[:, u % 3, c * P:c * P + P], ident[:, :])
                    ins.then_inc(pt_done.sem, pt_done.mark((l, h2, u)))
                if h2 < 3:
                    project_q(h2 + 1, 0, range(2, KQ))
                mix(len(units) - 1)
            for m in range(KD):
                t = t0 + N_IN + 5 * m
                seq = 6 * m

                def free(i):
                    if i < 4:
                        return
                    mm, r = divmod(i - 4, 6)
                    if r in (0, 3, 5):
                        pe.wait_ge(g_ready.sem, g_ready.at((l, mm, (0, 3, 5).index(r))))
                    else:
                        pe.wait_ge(br_dve.sem, br_dve.at((l, mm, (1, 2, 4).index(r))))

                free(seq)
                wait_w(pe, t)
                product(pe, seq, t, full, hh, hl, n, True, True).then_inc(w_used.sem, w_used.mark(t))
                if m == 0:
                    pe.wait_ge(ol_ready.sem, ol_ready.at((l, 3)))
                    pe.wait_ge(ml_ready.sem, ml_ready.at(l))
                free(seq + 1)
                free(seq + 2)
                wait_w(pe, t + 1)
                product(pe, seq + 1, t + 1, [(k, k) for k in range(4)], oah, oal, n, True, True).then_inc(
                    br_done.sem, br_done.mark((l, m, 0)))
                product(pe, seq + 2, t + 1, [(4, 0)], osh, osl, n, True, False).then_inc(
                    w_used.sem, w_used.mark(t + 1))
                free(seq + 3)
                wait_w(pe, t + 2)
                product(pe, seq + 3, t + 2, full, hh, hl, n, True, True).then_inc(w_used.sem, w_used.mark(t + 2))
                free(seq + 4)
                wait_w(pe, t + 3)
                product(pe, seq + 2, t + 3, [(0, 1), (1, 2)], osh, osl, n, False, True).then_inc(
                    br_done.sem, br_done.mark((l, m, 1)))
                product(pe, seq + 4, t + 3, [(2, 0), (3, 1), (4, 2)], ofh, ofl, n, True, True).then_inc(
                    w_used.sem, w_used.mark(t + 3))
                free(seq + 5)
                wait_w(pe, t + 4)
                product(pe, seq + 5, t + 4, full, hh, hl, n, True, True).then_inc(w_used.sem, w_used.mark(t + 4))
            pe.wait_ge(m_ready.sem, m_ready.at((l, KD - 1)))
            w = t0 + N_IN + N_MERGE
            for m in range(3):
                wait_w(pe, w + m)
            for k in range(KD):
                pe.wait_ge(msplit_l.sem, msplit_l.at((l, k)))
                for m in range(3):
                    ins = product_step(pe, m, w + m, k, hh, hl, n)
                    if k == KD - 1:
                        ins.then_inc(w_used.sem, w_used.mark(w + m))
            for m in range(3, N_OUT):
                wait_w(pe, w + m)
                pe.wait_ge(x_add.sem, x_add.at((l, m - 3)))
                product(pe, m % 3, w + m, full, hh, hl, n, True, True).then_inc(w_used.sem, w_used.mark(w + m))
            pe_norm(pe, (l, 2), n)
            pe.wait_ge(x_add.sem, x_add.at((l, KD - 1)))
            base = t0 + N_IN + N_MERGE + N_OUT

            def quarter(i, final):
                for m in range(KD):
                    if m < 4:
                        pe.wait_ge(x_add.sem, i * KD + (x_add.at((l, KD - 1)) - 3 + m))
                    else:
                        pe.wait_ge(relu_ready.sem, relu_ready.at((l, m - 4), i))
                    pe.wait_ge(w_split.sem, i * 32 + 2 * (base + m + 1))
                    if m == 2:
                        for k in range(KD):
                            pe.wait_ge(lo_ready.sem, lo_ready.at((l, 2, k)))
                            for mm in range(3):
                                ins = product_step(pe, mm, mm, k, hh, hl, n)
                                if k == KD - 1:
                                    ins.then_inc(w_used.sem, w_used.mark((l, "m1", mm) + final))
                    if m > 2:
                        product(pe, m, m, full, hh, hl, n, True, True).then_inc(
                            w_used.sem, w_used.mark((l, "m1", m) + final))
                for m in range(KD):
                    pe.wait_ge(w_split.sem, i * 32 + 2 * (base + KD + m + 1))
                    p = m % 3 if final else m
                    if m == 0:
                        pe.wait_ge(relu_ready.sem, relu_ready.at((l, 4), i))
                        for k in range(KD):
                            pe.wait_ge(midl_ready.sem, midl_ready.at((l, k), i))
                            ins = product_step(pe, 0, KD, k, midh, midl, n)
                        ins.then_inc(w_used.sem, w_used.mark((l, "m2", 0) + final))
                        continue
                    if m >= (3 if final else 4):
                        pe.wait_ge(x_add.sem, x_add.at((l, "mlp", m - (3 if final else 4)), i))
                    product(pe, p, KD + m, full, midh, midl, n, True, True).then_inc(
                        w_used.sem, w_used.mark((l, "m2", m) + final))

            w_used.start_loop((l, "mlp"))
            with pe.Fori(0, QUARTERS - 1) as i:
                quarter(i, ())
            w_used.end_loop(QUARTERS - 1)
            quarter(QUARTERS - 1, ("final",))
            pe_norm(pe, (l + 1, 1), n)

        block = ctx.enter_context(nc.Block())

        @block.tensor
        def _(pe):
            pe.wait_ge(ident_in.sem, ident_in.at(0))
            pe.wait_ge(silu_ready.sem, silu_ready.at(0))
            for l in range(DEPTH):
                pe_ada(pe, ADA_AT[l][0], ADA_AT[l][1] - ADA_AT[l][0])
                pe.wait_ge(prep_dve.sem, prep_dve.at((l, "bin")))
                for q in range(GROUPS // 2):
                    if q >= 2:
                        pe.wait_ge(prep_act.sem, prep_act.at((l, "binT", q - 2)))
                    for j in range(2):
                        for ri in range(2):
                            ins = pe.transpose(ps[:, q % 2, (2 * j + ri) * P:(2 * j + ri + 1) * P],
                                               bin_[:, ri, 2 * q + j, :, :].rearrange("p s q -> p (s q)"), ident[:, :])
                    ins.then_inc(prep_pe.sem, prep_pe.mark((l, "binT", q)))
                pe.wait_ge(prep_act.sem, prep_act.at((l, "binT", GROUPS // 2 - 1)))
                for half in range(2):
                    pe_ada(pe, ADA_AT[l][1 + half], ADA_AT[l][2 + half] - ADA_AT[l][1 + half])
                    pe.wait_ge(prep_dve.sem, prep_dve.at((l, f"cz{half}")))
                    for q in range(6):
                        if q >= 2:
                            pe.wait_ge(prep_act.sem, prep_act.at((l, "v", half, q - 2)))
                        for j in range(2):
                            g = 12 * half + 2 * q + j
                            for ri in range(2):
                                ins = pe.matmul(ps[0:GP, q % 2, j * 240:j * 240 + 240], bb[:, ri, g, :],
                                                cz[:, ri, 2 * q + j, :, :].rearrange("p a b -> p (a b)"),
                                                start=(ri == 0), stop=(ri == 1))
                        ins.then_inc(prep_pe.sem, prep_pe.mark((l, "v", half, q)))
                    pe.wait_ge(prep_act.sem, prep_act.at((l, "v", half, 5)))
            pe_ada(pe, ADA_AT[1][3], DEPTH * ADA_PAIRS - ADA_AT[1][3])
            pe.wait_ge(ada_ready.sem, ada_ready.at(1))
            for l in range(DEPTH):
                pe_layer(pe, l)

        w_main = A["w_main"]
        n_all = DEPTH * N_TILES

        @block.sync
        def _(sp):
            sp.wait_ge(ident_in.sem, ident_in.at(0))
            sp.wait_ge(prep_loaded.sem, prep_loaded.at(0))
            ada8 = A["ada_w"].rearrange("(a b) p n -> a b p n", b=8)
            for u in range(8):
                sp.dma_start(ada_w[:, u, :], ada8[0, u]).then_inc(ada_full[u].sem, 16)
            with sp.Fori(1, DEPTH * ADA_PAIRS) as i:
                for u in range(8):
                    sp.wait_ge(ada_used[u].sem, i)
                    sp.dma_start(ada_w[:, u, :], ada8[i, u]).then_inc(ada_full[u].sem, 16)
            w2 = w_main.rearrange("(a b) p n -> a b p n", b=RAW_SLOTS)
            for u in range(RAW_SLOTS):
                sp.dma_start(raw[:, u, :], w2[0, u]).then_inc(raw_full[u].sem, 16)
            with sp.Fori(1, n_all // RAW_SLOTS) as i:
                for u in range(RAW_SLOTS):
                    sp.wait_ge(w_split.sem, i * 4 + (2 * u - 2))
                    sp.dma_start(raw[:, u, :], w2[i, u]).then_inc(raw_full[u].sem, 16)

        @block.gpsimd
        def _(pool):
            def split(t0, u, i):
                pool.wait_ge(raw_full[u % 2].sem, i * 32 + 16 * (u // 2 + 1))
                if t0:
                    pool.wait_ge(w_used.sem, i * 4 + (u - 3))
                pool.sem_inc(w_turn.sem, 1)
                pool.tensor_scalar(whi[:, u, :], raw[:, u % 2, :], 1.0, 0.0, ALU.mult, ALU.add).then_inc(
                    w_split.sem, 1)
                pool.wait_ge(w_split.sem, i * 8 + (2 * u + 1))
                pool.tensor_tensor(wlo[:, u, :], raw[:, u % 2, :], whi[:, u, :].bitcast(F32), ALU.subtract).then_inc(
                    w_split.sem, 1)

            pool.wait_ge(ada_turned.sem, DEPTH * ADA_PAIRS * 2)
            for u in range(W_SLOTS):
                split(False, u, 0)
            with pool.Fori(1, n_all // W_SLOTS) as i:
                for u in range(W_SLOTS):
                    split(True, u, i)

        def act_squares(act, key, n):
            l, w = key
            for k in range(KD):
                if w == 2:
                    act.wait_ge(x_add.sem, x_add.at((l, k)))
                elif l:
                    act.wait_ge(x_add.sem, x_add.at((l - 1, "mlp", k), QUARTERS - 1))
                if k >= 2:
                    act.wait_ge(sq_used.sem, sq_used.at((key, max(k - 2, 1))))
                act.activation(sqt[:, k % 2, 0:n], x[:, k, 0:n], ACT.Square).then_inc(
                    sq_ready.sem, sq_ready.mark((key, k)))

        def act_root(act, key, n):
            act.wait_ge(sq_summed.sem, sq_summed.at(key))
            act.activation(root[:, 0:n // 64], ps[:, 3, 0:n // 64], ACT.Sqrt, bias=eps_col[:, 0:1],
                           scale=1.0 / D).then_inc(rms_ready.sem, rms_ready.mark(key))

        def act_norm(act, l, w, n):
            if l or w == 2:
                act_squares(act, (l, w), n)
            act_root(act, (l, w), n)
            row = 0 if w == 1 else 3
            for k in range(KD):
                act.wait_ge(nt_ready.sem, nt_ready.at((l, w, k)))
                for s, (a, b) in enumerate(spans(n)):
                    ins = act.activation(hh[:, k, a:b], nt[:, k % 2, a:b], ACT.Identity,
                                         bias=ada[:, l, row * KD + k, s:s + 1])
                ins.then_inc(hi_ready.sem, hi_ready.mark((l, w, k)))

        def act_layer(act, l):
            n = TOK if l == 0 else LAT
            act_norm(act, l, 1, TOK)
            act.wait_ge(lo_ready.sem, lo_ready.at((l, 1, KD - 1)))
            if l == 1:
                act.dma_start(x_d, x[:, :, :]).then_inc(x_spilled.sem, x_spilled.mark(l, 16))
                act.wait_ge(x_spilled.sem, x_spilled.at(l))
            act.dma_start(bint[:].rearrange("p g r s -> p (g r s)"), bin_d[l]).then_inc(
                bint_in.sem, bint_in.mark(l, 16))

            def evacuate(i, dst, p):
                act.wait_ge(w_used.sem, w_used.at(l * N_TILES + i))
                m = TOK if i < 6 else n
                act.copy(dst[:, 0:m], pair(p, m)).then_inc(in_act.sem, in_act.mark((l, i)))

            def square(q, src, k, m):
                if k >= 2:
                    act.wait_ge(sn_used.sem, sn_used.at((l, q, k - 2)))
                act.activation(sq_s[:, k % 2, 0:m], src[:, k, 0:m], ACT.Square).then_inc(
                    sn_sq.sem, sn_sq.mark((l, q, k)))

            act.wait_ge(in_dve.sem, in_dve.at((l, 2)))
            act.dma_start(zs_d[l].rearrange("i p f -> p i f"), zs[:].rearrange("p i s c -> p i (s c)")).then_inc(
                zs_stored.sem, zs_stored.mark(l, 16))
            act.wait_ge(zs_stored.sem, zs_stored.at(l))
            v = zs_d[l].rearrange("i (g p) (s c) -> s p (i g) c", p=GP, s=CH)
            for s in range(CH):
                act.dma_start(us[s * GP:(s + 1) * GP, :, :], v[s]).then_inc(us_in.sem, us_in.mark((l, s), 16))
            evacuate(3, zkv[:, 0], 3)
            evacuate(4, zkv[:, 1], 0)
            act.wait_ge(in_act.sem, in_act.at((l, 4)))
            for k in range(KKV):
                square(1, zkv, k, TOK)
            act.wait_ge(sn_used.sem, sn_used.at((l, 1, KKV - 1)))
            act.activation(rs_s[:, :], ps[:, 2, 0:TOK], ACT.Sqrt, bias=eps_col[:, 0:1], scale=1.0 / (KKV * P)).then_inc(
                
                sn_root.sem, sn_root.mark((l, 1)))
            for q in range(6):
                act.wait_ge(bu_done.sem, bu_done.at((l, q)))
                for ri in range(2):
                    v = ps[0:64, 3 - q % 2, ri * 512:ri * 512 + 4 * NC].rearrange("p (g c) -> p g c", c=NC)
                    o = ss[0:64, :, ri, 4 * q:4 * q + 4].rearrange("p j g -> p g j")
                    act.copy(o[:, :, 1 + NCC:1 + NC], v[:, :, 0:NCL])
                    ins = act.copy(o[:, :, 1:1 + NCC], v[:, :, NCL:NC])
                ins.then_inc(bu_act.sem, bu_act.mark((l, q)))
            for dst, src in ((dft_l, "dft_l"), (dft_c, "dft_c"), (c64, "c64")):
                act.dma_start(dst[:], A[src]).then_inc(dft_in.sem, dft_in.mark(l, 16))
            act.dma_start(pw_first[:, 0:KQ * P], A["w_pair"][l, 0, :, 0:KQ * P]).then_inc(
                pw_first_in.sem, pw_first_in.mark(l, 16))
            act.dma_start(pw_first[:, KQ * P:], A["w_pair"][l, 0, :, 2 * KQ * P:(2 * KQ + KKV) * P]).then_inc(
                pw_first_in.sem, pw_first_in.mark(l, 16))
            act.wait_ge(w_used.sem, w_used.at(l * N_TILES + 5))
            act.copy(kk[64:128, 1, :], ps[64:128, 1, 0:TOK]).then_inc(in_act.sem, in_act.mark((l, 5)))
            for k in range(2):
                evacuate(6 + k, zq[:, k], 2 + k)
                act.wait_ge(in_act.sem, in_act.at((l, 6 + k)))
                square(0, zq, k, n)
            evacuate(8, zq[:, 2], 0)
            evacuate(9, zf[:, 0], 1)
            act.wait_ge(in_act.sem, in_act.at((l, 8)))
            square(0, zq, 2, n)
            act.wait_ge(sn_used.sem, sn_used.at((l, 0, KQ - 1)))
            act.activation(rs_q[:, 0:n], ps[:, 2, 0:n], ACT.Sqrt, bias=eps_col[:, 0:1], scale=1.0 / (KQ * P)).then_inc(
                sn_root.sem, sn_root.mark((l, 0)))
            evacuate(10, zf[:, 1], 3)
            evacuate(11, zf[:, 2], 0)
            act.wait_ge(sn_scale.sem, sn_scale.at((l, 1)))
            for b in range(n // P):
                act.wait_ge(fr_a.sem, fr_a.at((l, b)))
                act.copy(pq[:, b, :, :].rearrange("p i c -> p (i c)"), ps[:, 1 + b % 2, 0:768]).then_inc(
                    fr_pq.sem, fr_pq.mark((l, b)))
            act.wait_ge(sn_scale.sem, sn_scale.at((l, 0)))
            flat = cout[:].rearrange("p r g s -> p (r g s)")

            def load_outputs(j):
                act.dma_start(flat[:, 2048 * j:2048 * j + 2048], cout_d[l][:, 2048 * j:2048 * j + 2048]).then_inc(
                    cout_in.sem, cout_in.mark(l, 16))

            act.wait_ge(fr_tab.sem, fr_tab.at((l, 1)))
            load_outputs(0)
            if n > LAT:
                act.wait_ge(fr_tab.sem, fr_tab.at((l, 3)))
                load_outputs(1)
            for i in range(3):
                act.wait_ge(fr_b.sem, fr_b.at((l, i)))
                act.copy(of[:, i, 0:n], ps[:, (3, 0, 1)[i], 0:n]).then_inc(fr_evac.sem, fr_evac.mark((l, i)))
            for j in range(2 if n > LAT else 1, 3):
                load_outputs(j)
            act.wait_ge(scan.sem, scan.at((l, SCAN_EARLY - 1)))
            v = ss[:].rearrange("p j r g -> p j (r g)")
            o = snat[:].rearrange("p r g c -> p c (r g)")
            act.copy(o[0:64, NCL:NC], v[0:64, 0:NCC])
            ins = act.copy(o[0:64, 0:SCAN_EARLY - NCC], v[0:64, NCC:SCAN_EARLY])
            if l:
                ins = act.copy(o[64:128, NC - SCAN_EARLY:NC], v[64:128, SCAN_EARLY - 1::-1])
            ins.then_inc(snat_act.sem, snat_act.mark((l, "early")))
            if l == 0:
                act.wait_ge(snat_dve.sem, snat_dve.at((0, "early")))
            act.wait_ge(snat_act.sem, snat_act.at((l, "early")))
            act.dma_start(toep[:], toep_d[l]).then_inc(toep_in.sem, toep_in.mark(l, 16))

            def copy_keys(h2):
                act.wait_ge(k_done.sem, k_done.at((l, h2)))
                act.copy(kk[0:64, 0, :], ps[0:64, 2, 0:TOK])
                act.copy(kk[0:64, 1, :], ps[64:128, 2, 0:TOK]).then_inc(k_act.sem, k_act.mark((l, h2)))

            copy_keys(0)
            act.wait_ge(scan.sem, scan.at((l, NC - 1)))
            act.copy(o[0:64, SCAN_EARLY - NCC:NCL], v[0:64, SCAN_EARLY:NC]).then_inc(
                snat_act.sem, snat_act.mark(l))
            act.wait_ge(snat_act.sem, snat_act.at(l))
            act.wait_ge(snat_dve.sem, snat_dve.at(l))
            act.dma_start(wglu[:].rearrange("p k m -> p (k m)"), A["w_glu"][l]).then_inc(
                glu_w_in.sem, glu_w_in.mark(l, 16))

            def store_y(i):
                act.wait_ge(y_evac.sem, y_evac.at((l, 2 * i + 1)))
                for s in range(CH):
                    act.dma_start(y_d[l].rearrange("g p s c -> s p g c")[s][:, 8 * i:8 * i + 8, :],
                                  us[s * GP:(s + 1) * GP, 8 * i:8 * i + 8, :]).then_inc(
                                      y_stored[i].sem, y_stored[i].mark(l, 16))

            def load_y(i):
                act.wait_ge(y_stored[i].sem, y_stored[i].at(l))
                act.dma_start(yp[:, i, :], y_d[l, 8 * i:8 * i + 8].rearrange("g p s c -> (g p) (s c)")).then_inc(
                    y_in[i].sem, y_in[i].mark(l, 16))

            def gelu_y(i):
                act.wait_ge(y_skip.sem, y_skip.at((l, i)))
                act.activation(yg[:, i, :], yp[:, i, :], ACT.Gelu_apprx_tanh).then_inc(gelu.sem, gelu.mark((l, i)))

            store_y(0)
            store_y(1)
            load_y(0)
            store_y(2)
            load_y(1)
            gelu_y(0)
            load_y(2)
            gelu_y(1)
            gelu_y(2)
            act.dma_start(pws[0][:, :], A["w_pair"][l, 0]).then_inc(pw_in[0].sem, pw_in[0].mark((l, 0), 16))
            act.wait_ge(gelu.sem, gelu.at((l, 2)))
            for o in range(3):
                act.wait_ge(glu_done.sem, glu_done.at((l, o)))
                act.activation(yp[:, o, :], ps[:, 1 + o, 0:TOK], ACT.Sigmoid, bias=b_glu[:, l, o:o + 1]).then_inc(
                    glu_sig.sem, glu_sig.mark((l, o)))
            act.wait_ge(os_ready.sem, os_ready.at((l, 2)))
            nq = n // P
            for h2 in range(4):
                if h2 < 3:
                    if h2:
                        act.wait_ge(v_done.sem, v_done.at((l, h2 - 1)))
                    act.dma_start(pws[(h2 + 1) % 2][:, :], A["w_pair"][l, h2 + 1]).then_inc(
                        pw_in[(h2 + 1) % 2].sem, pw_in[(h2 + 1) % 2].mark((l, h2 + 1), 16))
                act.wait_ge(q_done.sem, q_done.at((l, h2, 0)))
                act.copy(qq[0:64, 0, 0:n], ps[0:64, 0, 0:n]).then_inc(q_act.sem, q_act.mark((l, h2, 0)))
                if h2:
                    copy_keys(h2)
                act.wait_ge(q_done.sem, q_done.at((l, h2, 1)))
                act.copy(qq[0:64, 1, 0:n], ps[0:64, 1, 0:n]).then_inc(q_act.sem, q_act.mark((l, h2, 1)))
                units = [(j, b) for j in range(2) for b in range(nq)]

                def exponent(u):
                    act.wait_ge(nmax_ready.sem, nmax_ready.at((l, h2, u)))
                    if u >= 3:
                        act.wait_ge(pt_done.sem, pt_done.at((l, h2, u - 3)))
                    a = 0 if units[u][1] < 4 else 512
                    act.activation(pr[:, u % 3, a:TOK], ps[:, u % 2, a:TOK], ACT.Exp,
                                                      bias=nmx[:, u % 4:u % 4 + 1], scale=SCALE,
                                                      accum_out=sm[:, u % 4:u % 4 + 1]).then_inc(
                                                          exp_ready.sem, exp_ready.mark((l, h2, u)))

                exponent(0)
                act.wait_ge(v_done.sem, v_done.at((l, h2)))
                act.copy(vv[:].rearrange("p b v -> p (b v)"), ps[:, 3, 0:TOK]).then_inc(v_act.sem, v_act.mark((l, h2)))
                for u, (j, b) in enumerate(units):
                    if u + 1 < len(units):
                        exponent(u + 1)
                    act.wait_ge(pt_done.sem, pt_done.at((l, h2, u)))
                    q0 = (b % 4) * P
                    if b in (0, 4) and u:
                        head, block = (j - 1, nq - 1) if b == 0 else (j, 3)
                        act.wait_ge(pv_done.sem, pv_done.at((l, h2, head, block)))
                    k0 = 0 if b < 4 else 4
                    act.copy(pt[:, k0:6, q0:q0 + P],
                                              ps[:, 2, k0 * P:TOK].rearrange("p (k q) -> p k q", q=P)).then_inc(
                                                  pt_evac.sem, pt_evac.mark((l, h2, u)))
                act.wait_ge(pv_done.sem, pv_done.at((l, h2, 1, 3 if nq == 4 else 5)))
                act.copy(oah[:, h2, 0:n], ps[:, 3, 0:n]).then_inc(oh_ready.sem, oh_ready.mark((l, h2)))
            for dst, src in ((osh, osm), (ofh, of)):
                ins = act.copy(dst[:, :, 0:n], src[:, :, 0:n])
                ins.then_inc(mh_ready.sem, mh_ready.mark((l, dst is ofh)))
            act.wait_ge(ml_ready.sem, ml_ready.at(l))
            for m in range(KD):
                for j, b in enumerate((0, 2, 1)):
                    act.wait_ge(w_used.sem, w_used.at(l * N_TILES + N_IN + 5 * m + 2 * j))
                    i = 3 * m + j
                    if i >= 2:
                        act.wait_ge(br_dve.sem, br_dve.at((l, (i - 2) // 3, (i - 2) % 3)))
                    act.activation(gt[:, i % 2, 0:n], pair(6 * m + (0, 3, 5)[j], n), ACT.Tanh,
                                                    bias=b_gate[:, l, b * KD + m:b * KD + m + 1], scale=0.5).then_inc(
                                                        g_ready.sem, g_ready.mark((l, m, j)))
            act.wait_ge(w_used.sem, w_used.at(l * N_TILES + N_IN + N_MERGE - 1))
            act.dma_start(x[:, :, :], A["x_t"] if l == 0 else x_d).then_inc(x_in.sem, x_in.mark(("out", l), 16))
            for k in range(KD):
                act.wait_ge(m_ready.sem, m_ready.at((l, k)))
                act.mul(hh[:, k, 0:n], m_sb[:, k, 0:n], 0.5).then_inc(msplit_h.sem, msplit_h.mark((l, k)))
            act_norm(act, l, 2, n)
            act.wait_ge(lo_ready.sem, lo_ready.at((l, 2, KD - 1)))

            def quarter(i, final):
                for m in range(KD):
                    act.wait_ge(w_used.sem, w_used.at((l, "m1", m), i))
                    if m >= 2:
                        act.wait_ge(msq_ready.sem, msq_ready.at((l, m - 2), i))
                    act.activation(mr[:, m % 2, 0:n], pair(m, n), ACT.Relu).then_inc(
                        relu_ready.sem, relu_ready.mark((l, m) + final))
                    act.wait_ge(relu_ready.sem, relu_ready.at((l, m), i))
                    act.activation(midh[:, m, 0:n], mr[:, m % 2, 0:n], ACT.Square).then_inc(
                        midh_ready.sem, midh_ready.mark((l, m) + final))

            for s in (relu_ready, midh_ready):
                s.start_loop((l, "mlp"))
            with act.Fori(0, QUARTERS - 1) as i:
                quarter(i, ())
            for s in (relu_ready, midh_ready):
                s.end_loop(QUARTERS - 1)
            quarter(QUARTERS - 1, ("final",))
            act.wait_ge(msq_ready.sem, msq_ready.at((l, KD - 1), QUARTERS - 1))
            act.wait_ge(midh_ready.sem, midh_ready.at((l, KD - 1), QUARTERS - 1))

        @block.scalar
        def _(act):
            act.dma_start(cvec[:], A["cvec"]).then_inc(cvec_in.sem, cvec_in.mark(0, 16))
            act.dma_start(ident[:], A["ident"]).then_inc(ident_in.sem, ident_in.mark(0, 16))
            def load_ab(l):
                act.dma_start(abuf[:, 0:3, :], A["ssm_a"][l]).then_inc(prep_loaded.sem, prep_loaded.mark(l, 16))
                act.dma_start(b_in[:], A["ssm_b"][l]).then_inc(prep_loaded.sem, prep_loaded.mark(l, 16))

            def load_c(l):
                act.dma_start(c_in[:], A["ssm_c"][l]).then_inc(prep_c_loaded.sem, prep_c_loaded.mark(l, 16))

            def exponents(l):
                act.wait_ge(prep_loaded.sem, prep_loaded.at(l))
                act.activation(abuf[:, 3, :], abuf[:, 2, :], ACT.Exp).then_inc(prep_act.sem, prep_act.mark((l, "dt")))
                act.wait_ge(prep_dve.sem, prep_dve.at((l, "dta")))
                act.activation(abuf[:, 6, :], abuf[:, 4, :], ACT.Exp).then_inc(prep_act.sem, prep_act.mark((l, "mag")))
                act.wait_ge(prep_dve.sem, prep_dve.at((l, "angle")))
                act.activation(abuf[:, 8, :], abuf[:, 7, :], ACT.Sin)
                act.activation(abuf[:, 9, :], abuf[:, 7, :], ACT.Sin, scale=0.5).then_inc(
                    prep_act.sem, prep_act.mark((l, "sin")))

            def evacuate_inputs(l):
                if l:
                    act.wait_ge(prep_stored.sem, prep_stored.at((0, "bin")))
                for q in range(GROUPS // 2):
                    act.wait_ge(prep_pe.sem, prep_pe.at((l, "binT", q)))
                    act.copy(binT[:, 2 * q:2 * q + 2, :, :].rearrange("p g r s -> p (g r s)"), ps[:, q % 2, 0:512]).then_inc(
                        
                        prep_act.sem, prep_act.mark((l, "binT", q)))
                act.wait_ge(prep_act.sem, prep_act.at((l, "binT", GROUPS // 2 - 1)))
                act.dma_start(bin_d[l], binT[:].rearrange("p g r s -> p (g r s)")).then_inc(
                    prep_stored.sem, prep_stored.mark((l, "bin"), 16))

            def evacuate_kernels(l, half):
                if l and half == 0:
                    act.wait_ge(prep_v_stored.sem, prep_v_stored.at(0))
                for q in range(6):
                    act.wait_ge(prep_pe.sem, prep_pe.at((l, "v", half, q)))
                    g = 12 * half + 2 * q
                    act.copy(vsb[:, g:g + 2, :].rearrange("p g f -> p (g f)"), ps[0:GP, q % 2, 0:480]).then_inc(
                        prep_act.sem, prep_act.mark((l, "v", half, q)))
                if half:
                    act.wait_ge(prep_act.sem, prep_act.at((l, "v", 1, 5)))
                    for s in range(CH):
                        act.dma_start(toep_d[l, s * GP:(s + 1) * GP, :, :], vsb[:, :, (7 - s) * GP:(15 - s) * GP]).then_inc(
                            
                            prep_v_stored.sem, prep_v_stored.mark(l, 16))

            def store_outputs(l):
                act.wait_ge(prep_dve.sem, prep_dve.at((l, "cout")))
                act.dma_start(cout_d[l], bin_[:].rearrange("p r g s q -> p (r g s q)")).then_inc(
                    prep_stored.sem, prep_stored.mark((l, "cout"), 16))

            load_ab(0)
            load_c(0)
            act.wait_ge(cvec_in.sem, cvec_in.at(0))
            act.activation(svec[:], cvec[:], ACT.Silu).then_inc(silu_ready.sem, silu_ready.mark(0))
            exponents(0)
            for dst, name in ((rope, "rope"), (ada_b, "ada_b"), (ln, "ln"), (fnorm, "fnorm"),
                              (qkn, "qkn"), (b_gate, "b_gate"), (b_glu, "b_glu"), (ssm_d, "ssm_d")):
                act.dma_start(dst[:], A[name]).then_inc(consts_in.sem, consts_in.mark(0, 16))
            act_ada(act, 0, 1)
            act_ada(act, 1, ADA_AT[0][1] - 1)
            evacuate_inputs(0)
            act_ada(act, ADA_AT[0][1], ADA_AT[0][2] - ADA_AT[0][1])
            evacuate_kernels(0, 0)
            load_ab(1)
            act_ada(act, ADA_AT[0][2], 1)
            store_outputs(0)
            exponents(1)
            act_ada(act, ADA_AT[0][2] + 1, ADA_AT[0][3] - ADA_AT[0][2] - 1)
            evacuate_kernels(0, 1)
            load_c(1)
            act_ada(act, ADA_AT[1][0], ADA_AT[1][1] - ADA_AT[1][0])
            evacuate_inputs(1)
            act_ada(act, ADA_AT[1][1], ADA_AT[1][2] - ADA_AT[1][1])
            evacuate_kernels(1, 0)
            act.wait_ge(prep_stored.sem, prep_stored.at((1, "bin")))
            act.dma_start(x[:, :, :], A["x_t"]).then_inc(x_in.sem, x_in.mark("first", 16))
            act_ada(act, ADA_AT[1][2], ADA_AT[1][3] - ADA_AT[1][2])
            evacuate_kernels(1, 1)
            store_outputs(1)
            act.wait_ge(prep_pe.sem, prep_pe.at((1, "v", 1, 5)))
            act.wait_ge(x_in.sem, x_in.at("first"))
            act_squares(act, (0, 1), TOK)
            act_ada(act, ADA_AT[1][3], DEPTH * ADA_PAIRS - ADA_AT[1][3])
            act.wait_ge(prep_stored.sem, prep_stored.at((1, "cout")))
            act.wait_ge(prep_v_stored.sem, prep_v_stored.at(1))
            act.wait_ge(prep_dve.sem, prep_dve.at((1, "cz1")))
            act.wait_ge(x_in.sem, x_in.at("first"))
            for l in range(DEPTH):
                act_layer(act, l)
            act_squares(act, (DEPTH, 1), LAT)
            act_root(act, (DEPTH, 1), LAT)
            for k in range(KD):
                act.wait_ge(fin_ready.sem, fin_ready.at(k))
                act.dma_start(out[:, k, :], xo[:, k, :]).then_inc(out_stored.sem, out_stored.mark(k, 16))
            act.wait_ge(out_stored.sem, out_stored.at(KD - 1))

        def add_squares(dve, key, k, n):
            dve.wait_ge(sq_ready.sem, sq_ready.at((key, k)))
            if k > 1:
                dve.wait_ge(sq_used.sem, sq_used.at((key, k - 1)))
            if k:
                dve.tensor_tensor(sqa[:, 0:n], sqt[:, 0, 0:n] if k == 1 else sqa[:, 0:n], sqt[:, k % 2, 0:n],
                                  ALU.add).then_inc(sq_used.sem, sq_used.mark((key, k)))

        def invert(dve, key, n):
            dve.wait_ge(rms_ready.sem, rms_ready.at(key))
            dve.reciprocal(root[:, 0:n // 64], root[:, 0:n // 64]).then_inc(rstd_ready.sem, rstd_ready.mark(key))
            dve.wait_ge(rstd_ready.sem, rstd_ready.at(key))
            shape = [P, n // P, P]
            dve.tensor_tensor(diag[:, 0:n].rearrange("p (b t) -> p b t", t=P), ident[:, :].unsqueeze(1).to_broadcast(shape),
                              root[:, 0:n // 64:2].unsqueeze(2).to_broadcast(shape), ALU.mult).then_inc(
                                  diag_ready.sem, diag_ready.mark(key))
            dve.wait_ge(rstd_spread.sem, rstd_spread.at(key))

        def dve_norm(dve, l, w, n):
            invert(dve, (l, w), n)

            def lo(k):
                dve.wait_ge(hi_ready.sem, hi_ready.at((l, w, k)))
                row = 0 if w == 1 else 3
                for s, (a, b) in enumerate(spans(n)):
                    ins = dve.scalar_tensor_tensor(hl[:, k, a:b], nt[:, k % 2, a:b], ada[:, l, row * KD + k, s:s + 1],
                                                   hh[:, k, a:b].bitcast(F32), ALU.add, ALU.subtract)
                ins.then_inc(lo_ready.sem, lo_ready.mark((l, w, k)))

            for k in range(KD):
                if k >= 2:
                    dve.wait_ge(lo_ready.sem, lo_ready.at((l, w, k - 2)))
                for s, (a, b) in enumerate(spans(n)):
                    ins = dve.scalar_tensor_tensor(nt[:, k % 2, a:b], x[:, k, a:b], gain[:, l, w - 1, k, s:s + 1],
                                                   ps[:, 3, a:b], ALU.mult, ALU.mult)
                ins.then_inc(nt_ready.sem, nt_ready.mark((l, w, k)))
                if k:
                    lo(k - 1)
            lo(KD - 1)

        def rotate(dve, src, dst, part, n, key):
            dve.tensor_tensor(part[64:96, 0:n], src[64:96, 0:n], rope[64:96, 0:n], ALU.mult).then_inc(
                ropes.sem, ropes.mark((*key, 0)))
            dve.tensor_tensor(dst[0][64:96, 0:n], src[96:128, 0:n], rope[96:128, 0:n], ALU.mult).then_inc(
                ropes.sem, ropes.mark((*key, 1)))
            dve.wait_ge(ropes.sem, ropes.at((*key, 1)))
            dve.tensor_tensor(dst[0][64:96, 0:n], dst[0][64:96, 0:n], part[64:96, 0:n], ALU.add).then_inc(
                ropes.sem, ropes.mark((*key, 2)))
            if len(dst) > 1:
                dve.wait_ge(ropes.sem, ropes.at((*key, 2)))
                dve.tensor_copy(dst[1][64:96, 0:n], dst[0][64:96, 0:n]).then_inc(ropes.sem, ropes.mark((*key, 3)))

        def dve_layer(dve, l):
            n = TOK if l == 0 else LAT
            dve_norm(dve, l, 1, TOK)
            for i in range(3):
                dve.wait_ge(w_used.sem, w_used.at(l * N_TILES + i))
                dve.tensor_copy(zs[:, i, :, :], pair(i, TOK).rearrange("p (c s) -> p s c", s=CH)).then_inc(
                    in_dve.sem, in_dve.mark((l, i)))
            def scale(q, src, rs, kts, m):
                dve.wait_ge(sn_root.sem, sn_root.at((l, q)))
                dve.reciprocal(rs[:, 0:m], rs[:, 0:m]).then_inc(rstd_ready.sem, rstd_ready.mark((l, "s", q)))
                dve.wait_ge(rstd_ready.sem, rstd_ready.at((l, "s", q)))
                for k in range(kts):
                    ins = dve.scalar_tensor_tensor(src[:, k, 0:m], src[:, k, 0:m], qkn[:, l, q * KQ + k:q * KQ + k + 1],
                                                   rs[:, 0:m], ALU.mult, ALU.mult)
                ins.then_inc(sn_scale.sem, sn_scale.mark((l, q)))

            for q in range(6):
                dve.wait_ge(bu_done.sem, bu_done.at((l, q)))
                for ri in range(2):
                    v = ps[64:128, 3 - q % 2, ri * 512:ri * 512 + 4 * NC].rearrange("p (g c) -> p g c", c=NC)
                    o = ss[64:128, NC:0:-1, ri, 4 * q:4 * q + 4].rearrange("p j g -> p g j")
                    ins = dve.tensor_copy(o, v)
                ins.then_inc(bu_dve.sem, bu_dve.mark((l, q)))
            dve.memset(ss[:, 0, :, :], 0.0).then_inc(scan.sem, scan.mark((l, "zero")))
            dve.wait_ge(bu_act.sem, bu_act.at((l, 5)))
            dve.wait_ge(bu_dve.sem, bu_dve.at((l, 5)))

            def steps(first, last):
                for c in range(first, last):
                    dve.wait_ge(scan.sem, scan.at((l, c - 1) if c else (l, "zero")))
                    dve.tensor_tensor(terms[:], a8[:, l], ss[:, c].unsqueeze(1).to_broadcast([P, 2, 2, GROUPS]),
                                      ALU.mult).then_inc(scan.sem, scan.mark((l, c, "products")))
                    dve.wait_ge(scan.sem, scan.at((l, c, "products")))
                    dve.tensor_tensor(terms[:, 0], terms[:, 0], terms[:, 1, ::-1, :], ALU.add).then_inc(
                        scan.sem, scan.mark((l, c, "sum")))
                    dve.wait_ge(scan.sem, scan.at((l, c, "sum")))
                    dve.tensor_tensor(ss[:, c + 1], ss[:, c + 1], terms[:, 0], ALU.add).then_inc(
                        scan.sem, scan.mark((l, c)))

            steps(0, SCAN_NORM)
            scale(1, zkv, rs_s, KKV, TOK)
            steps(SCAN_NORM, SCAN_SPLIT)
            scale(0, zq, rs_q, KQ, n)
            steps(SCAN_SPLIT, SCAN_EARLY)
            steps(SCAN_EARLY, NC)
            dve.wait_ge(scan.sem, scan.at((l, NC - 1)))
            dve.wait_ge(fr_b.sem, fr_b.at((l, 2)))
            if l == 0:
                dve.tensor_copy(snat[64:128, :, :, NC - SCAN_EARLY:NC].rearrange("p r g c -> p c (r g)"),
                                ss[64:128, SCAN_EARLY - 1::-1].rearrange("p j r g -> p j (r g)")).then_inc(
                                    snat_dve.sem, snat_dve.mark((0, "early")))
            o = snat[64:128, :, :, 0:NC - SCAN_EARLY].rearrange("p r g c -> p c (r g)")
            v = ss[64:128, NC - 1:SCAN_EARLY - 1:-1].rearrange("p j r g -> p j (r g)")
            dve.tensor_copy(o, v).then_inc(snat_dve.sem, snat_dve.mark(l))
            dve.wait_ge(in_act.sem, in_act.at((l, 5)))
            rotate(dve, kk[:, 1], (kk[:, 0], kk[:, 1]), kk[:, 1], TOK, ("k", l))
            for q in range(6):
                dve.wait_ge(y_done.sem, y_done.at((l, q)))
                dve.tensor_copy(us[:, 4 * q:4 * q + 4, :].rearrange("p g c -> p (g c)"),
                                ps[:, 1 + q // 2, 512 * (q % 2):512 * (q % 2) + 4 * NC]).then_inc(
                                    y_evac.sem, y_evac.mark((l, q)))
            for i in range(3):
                dve.wait_ge(y_in[i].sem, y_in[i].at(l))
                dve.scalar_tensor_tensor(yp[:, i, :], zs[:, i].rearrange("p s c -> p (s c)"), ssm_d[:, l, i:i + 1],
                                         yp[:, i, :], ALU.mult, ALU.add).then_inc(y_skip.sem, y_skip.mark((l, i)))
            for o in range(3):
                dve.wait_ge(glu_sig.sem, glu_sig.at((l, o)))
                dve.tensor_tensor(osm[:, o, :].rearrange("p (c s) -> p s c", s=CH),
                                  yg[:, o, :].rearrange("p (s c) -> p s c", s=CH),
                                  yp[:, o, :].rearrange("p (s c) -> p s c", s=CH), ALU.mult).then_inc(
                                      os_ready.sem, os_ready.mark((l, o)))
            nq = n // P
            dve.wait_ge(os_ready.sem, os_ready.at((l, 2)))
            for h2 in range(4):
                for j in range(2):
                    dve.wait_ge(q_done.sem, q_done.at((l, h2, j)))
                    if j or h2:
                        dve.wait_ge(ropes.sem, ropes.at(("q", l, h2 - (1 - j), 1 - j, 2)))
                    rotate(dve, ps[:, j, :], (qq[:, j],), rt, n, ("q", l, h2, j))
                units = [(j, b) for j in range(2) for b in range(nq)]

                def maximum(u):
                    j, b = units[u]
                    dve.wait_ge(sc_done.sem, sc_done.at((l, h2, u)))
                    c = u % 4
                    dve.tensor_reduce(mx[:, c:c + 1], ps[:, u % 2, (0 if b < 4 else 512):TOK],
                                                         AXX, ALU.max).then_inc(
                                                             max_ready.sem, max_ready.mark((l, h2, u)))
                    dve.wait_ge(max_ready.sem, max_ready.at((l, h2, u)))
                    dve.tensor_scalar(nmx[:, c:c + 1], mx[:, c:c + 1], -SCALE, None, ALU.mult).then_inc(
                        nmax_ready.sem, nmax_ready.mark((l, h2, u)))

                maximum(0)
                maximum(1)
                for u, (j, b) in enumerate(units):
                    dve.wait_ge(exp_ready.sem, exp_ready.at((l, h2, u)))
                    c = u % 4
                    dve.reciprocal(rsm[:, c:c + 1], sm[:, c:c + 1]).then_inc(
                        rsum_ready.sem, rsum_ready.mark((l, h2, u)))
                    dve.wait_ge(rsum_ready.sem, rsum_ready.at((l, h2, u)))
                    a = 0 if b < 4 else 512
                    dve.tensor_scalar(pr[:, u % 3, a:TOK], pr[:, u % 3, a:TOK], rsm[:, c:c + 1],
                                                       None, ALU.mult).then_inc(p_ready.sem, p_ready.mark((l, h2, u)))
                    if u + 2 < len(units):
                        maximum(u + 2)
                dve.wait_ge(oh_ready.sem, oh_ready.at((l, h2)))
                dve.tensor_tensor(oal[:, h2, 0:n], ps[:, 3, 0:n], oah[:, h2, 0:n].bitcast(F32),
                                                    ALU.subtract).then_inc(ol_ready.sem, ol_ready.mark((l, h2)))
            for dst, src, hi in ((osl, osm, osh), (ofl, of, ofh)):
                dve.wait_ge(mh_ready.sem, mh_ready.at((l, dst is ofl)))
                ins = dve.tensor_tensor(dst[:, :, 0:n], src[:, :, 0:n], hi[:, :, 0:n].bitcast(F32), ALU.subtract)
            ins.then_inc(ml_ready.sem, ml_ready.mark(l))
            dve.wait_ge(ml_ready.sem, ml_ready.at(l))
            for m in range(KD):
                for j in range(3):
                    dve.wait_ge(g_ready.sem, g_ready.at((l, m, j)))
                    if j < 2:
                        dve.wait_ge(br_done.sem, br_done.at((l, m, j)))
                    else:
                        dve.wait_ge(w_used.sem, w_used.at(l * N_TILES + N_IN + 5 * m + 3))
                    if j == 0 and m:
                        dve.wait_ge(m_ready.sem, m_ready.at((l, m - 1)))
                    if j == 2:
                        dve.wait_ge(m_ready.sem, m_ready.at((l, m, "part")))
                    dve.scalar_tensor_tensor((acc, tmp, tmp)[j][:, 0:n], gt[:, (3 * m + j) % 2, 0:n], 1.0,
                                                             pair(6 * m + (1, 2, 4)[j], n), ALU.add, ALU.mult).then_inc(
                                                                 
                                                                 br_dve.sem, br_dve.mark((l, m, j)))
                    if j == 1:
                        dve.wait_ge(br_dve.sem, br_dve.at((l, m, 1)))
                        dve.tensor_tensor(acc[:, 0:n], acc[:, 0:n], tmp[:, 0:n], ALU.add).then_inc(
                            m_ready.sem, m_ready.mark((l, m, "part")))
                    if j == 2:
                        dve.wait_ge(br_dve.sem, br_dve.at((l, m, 2)))
                        dve.tensor_tensor(m_sb[:, m, 0:n], acc[:, 0:n], tmp[:, 0:n], ALU.add).then_inc(
                            m_ready.sem, m_ready.mark((l, m)))
            for k in range(KD):
                dve.wait_ge(msplit_h.sem, msplit_h.at((l, k)))
                dve.scalar_tensor_tensor(hl[:, k, 0:n], m_sb[:, k, 0:n], 0.5, hh[:, k, 0:n].bitcast(F32),
                                                           ALU.mult, ALU.subtract).then_inc(
                                                               msplit_l.sem, msplit_l.mark((l, k)))

            def residual(m, p, row):
                for s, (a, b) in enumerate(spans(n)):
                    ins = dve.scalar_tensor_tensor(x[:, m, a:b], pair(p, n)[:, a:b], ada[:, l, row * KD + m, s:s + 1],
                                                   x[:, m, a:b], ALU.mult, ALU.add)
                return ins

            dve.wait_ge(x_in.sem, x_in.at(("out", l)))
            for m in range(KD):
                dve.wait_ge(w_used.sem, w_used.at(l * N_TILES + N_IN + N_MERGE + m))
                residual(m, m % 3, 2).then_inc(x_add.sem, x_add.mark((l, m)))
                if m:
                    add_squares(dve, (l, 2), m - 1, n)
            add_squares(dve, (l, 2), KD - 1, n)
            dve_norm(dve, l, 2, n)
            dve.wait_ge(lo_ready.sem, lo_ready.at((l, 2, KD - 1)))

            def quarter(i, final):
                for m in range(KD):
                    dve.wait_ge(relu_ready.sem, relu_ready.at((l, m), i))
                    if m >= 2:
                        dve.wait_ge(midl_ready.sem, midl_ready.at((l, m - 2), i))
                    dve.tensor_tensor(ms[:, m % 2, 0:n], mr[:, m % 2, 0:n], mr[:, m % 2, 0:n], ALU.mult).then_inc(
                        msq_ready.sem, msq_ready.mark((l, m) + final))
                    dve.wait_ge(msq_ready.sem, msq_ready.at((l, m), i))
                    dve.wait_ge(midh_ready.sem, midh_ready.at((l, m), i))
                    dve.tensor_tensor(midl[:, m, 0:n], ms[:, m % 2, 0:n], midh[:, m, 0:n].bitcast(F32),
                                      ALU.subtract).then_inc(midl_ready.sem, midl_ready.mark((l, m) + final))
                for m in range(KD):
                    dve.wait_ge(w_used.sem, w_used.at((l, "m2", m), i))
                    residual(m, m % 3 if final else m, 5).then_inc(x_add.sem, x_add.mark((l, "mlp", m) + final))
                    if final and m:
                        add_squares(dve, (l + 1, 1), m - 1, n)

            for s in (msq_ready, midl_ready, x_add):
                s.start_loop((l, "mlp"))
            with dve.Fori(0, QUARTERS - 1) as i:
                quarter(i, ())
            for s in (msq_ready, midl_ready, x_add):
                s.end_loop(QUARTERS - 1)
            quarter(QUARTERS - 1, ("final",))
            add_squares(dve, (l + 1, 1), KD - 1, n)
            dve.wait_ge(x_add.sem, x_add.at((l, "mlp", KD - 1), QUARTERS - 1))

        def dve_prepare(dve, l):
            step = [0]

            def do(ins, key=None):
                step[0] += 1
                k = (l, key or step[0])
                ins.then_inc(prep_dve.sem, prep_dve.mark(k))
                dve.wait_ge(prep_dve.sem, prep_dve.at(k))

            def tt(o, a, b, op, key=None):
                do(dve.tensor_tensor(o, a, b, op), key)

            def cmul(o_re, o_im, xr, xi, yr, yi, ta, tb, negate=False, key=None):
                tt(ta, xr, yr, ALU.mult)
                tt(tb, xi, yi, ALU.mult)
                tt(o_re, ta, tb, ALU.subtract)
                tt(ta, xr, yi, ALU.mult)
                tt(tb, xi, yr, ALU.mult)
                if negate:
                    do(dve.scalar_tensor_tensor(o_im, ta, -1.0, tb, ALU.mult, ALU.subtract), key)
                else:
                    tt(o_im, ta, tb, ALU.add, key)

            e = lambda i: abuf[:, i, :]
            a_re, a_im, dt_, dr, th, mag, r = e(0), e(1), e(3), e(4), e(5), e(6), e(7)
            s1, sh, cs, t, u, ar1, wr, wi = e(8), e(9), e(10), e(11), e(12), e(13), e(14), e(15)
            dve.wait_ge(prep_loaded.sem, prep_loaded.at(l))
            dve.wait_ge(prep_act.sem, prep_act.at((l, "dt")))
            tt(th, dt_, a_im, ALU.mult)
            tt(dr, dt_, a_re, ALU.mult, "dta")
            big, two_pi = 12582912.0, 2 * np.pi
            c1 = 6.28125
            c2 = float(np.float32(np.floor((two_pi - c1) * 2**20) / 2**20))
            c3 = float(np.float32(two_pi - c1 - c2))
            do(dve.tensor_scalar(t, th, float(1 / two_pi), big, ALU.mult, ALU.add))
            do(dve.tensor_scalar(t, t, big, None, ALU.subtract))
            do(dve.scalar_tensor_tensor(r, t, -c1, th, ALU.mult, ALU.add))
            do(dve.scalar_tensor_tensor(r, t, -c2, r, ALU.mult, ALU.add))
            do(dve.scalar_tensor_tensor(r, t, -c3, r, ALU.mult, ALU.add))
            pi = float(np.nextafter(np.float32(np.pi), np.float32(0)))
            do(dve.tensor_scalar(r, r, pi, -pi, ALU.min, ALU.max), "angle")
            dve.wait_ge(prep_act.sem, prep_act.at((l, "mag")))
            dve.wait_ge(prep_act.sem, prep_act.at((l, "sin")))
            tt(t, sh, sh, ALU.mult)
            do(dve.tensor_scalar(cs, t, -2.0, 1.0, ALU.mult, ALU.add))
            p = lambda k: (pw8[:, k, 0, :], pw8[:, k, 1, :])
            do(dve.memset(pw8[:, 0, 0, :], 1.0))
            do(dve.memset(pw8[:, 0, 1, :], 0.0))
            tt(p(1)[0], mag, cs, ALU.mult)
            tt(p(1)[1], mag, s1, ALU.mult)
            for lo_, n_, by in ((1, 1, 1), (1, 2, 2), (1, 4, 4)):
                src = pw8[:, lo_:lo_ + n_]
                dst = pw8[:, lo_ + by:lo_ + by + n_]
                f = pw8[:, by]
                br, bi = (f[:, c].unsqueeze(1).to_broadcast([P, n_, GROUPS]) for c in range(2))
                ta = t1[:, 0:n_ * GROUPS].rearrange("p (a b) -> p a b", b=GROUPS)
                tb = t2[:, 0:n_ * GROUPS].rearrange("p (a b) -> p a b", b=GROUPS)
                cmul(dst[:, :, 0], dst[:, :, 1], src[:, :, 0], src[:, :, 1], br, bi, ta, tb)
            for c in range(2):
                do(dve.tensor_copy(a8[:, l, 0, c, :], pw8[:, CH, 0, :]))
            do(dve.tensor_copy(a8[:, l, 1, 0, :], pw8[:, CH, 1, :]))
            do(dve.tensor_scalar(a8[:, l, 1, 1, :], pw8[:, CH, 1, :], -1.0, None, ALU.mult))
            do(dve.tensor_scalar(ar1, p(1)[0], -1.0, None, ALU.add))
            tt(t, a_re, a_re, ALU.mult)
            tt(u, a_im, a_im, ALU.mult)
            tt(t, t, u, ALU.add)
            do(dve.reciprocal(u, t))
            tt(wr, ar1, a_re, ALU.mult)
            tt(t, p(1)[1], a_im, ALU.mult)
            tt(wr, wr, t, ALU.add)
            tt(wr, wr, u, ALU.mult)
            tt(wi, p(1)[1], a_re, ALU.mult)
            tt(t, ar1, a_im, ALU.mult)
            tt(wi, wi, t, ALU.subtract)
            tt(wi, wi, u, ALU.mult)
            if l:
                dve.wait_ge(prep_pe.sem, prep_pe.at((0, "v", 1, 5)))
                dve.wait_ge(prep_stored.sem, prep_stored.at((0, "cout")))
            wrb, wib = (v.unsqueeze(2).to_broadcast([P, GROUPS, GP]) for v in (wr, wi))
            ta = t1[:, 0:GROUPS * GP].rearrange("p (a b) -> p a b", b=GP)
            tb = t2[:, 0:GROUPS * GP].rearrange("p (a b) -> p a b", b=GP)
            cmul(bb[:, 0], bb[:, 1], b_in[:, 0], b_in[:, 1], wrb, wib, ta, tb)
            fw, bw = slice(0, 64), slice(64, 128)
            do(dve.tensor_copy(p_in[fw], pw8[fw, CH - 1::-1]))
            do(dve.tensor_copy(p_in[bw], pw8[bw, 0:CH]))
            do(dve.tensor_copy(p_out[fw], pw8[fw, 1:CH + 1]))
            do(dve.tensor_copy(p_out[bw], pw8[bw, CH:0:-1]))
            do(dve.memset(p_z[:], 0.0))
            do(dve.tensor_copy(p_z[fw, 7:15], pw8[fw, 0:CH]))
            do(dve.tensor_copy(p_z[bw, 0:8], pw8[bw, CH - 1::-1]))

            def wide(mat, pows, g0, ng, n_, o, negate, key):
                shape = [P, ng, n_, GP]
                f = ng * n_ * GP
                xr, xi = (mat[:, c, g0:g0 + ng].unsqueeze(2).to_broadcast(shape) for c in range(2))
                yr, yi = (pows[:, 0:n_, c, g0:g0 + ng].rearrange("p s g -> p g s").unsqueeze(3).to_broadcast(shape)
                          for c in range(2))
                ta, tb = (v[:, 0:f].rearrange("p (g s q) -> p g s q", g=ng, q=GP) for v in (t1, t2))
                cmul(o[0], o[1], xr, xi, yr, yi, ta, tb, negate, key)

            wide(bb, p_in, 0, GROUPS, CH, (bin_[:, 0], bin_[:, 1]), False, "bin")
            dve.wait_ge(prep_c_loaded.sem, prep_c_loaded.at(l))
            wide(c_in, p_z, 0, 12, 15, (cz[:, 0], cz[:, 1]), True, "cz0")
            dve.wait_ge(prep_pe.sem, prep_pe.at((l, "binT", GROUPS // 2 - 1)))
            wide(c_in, p_out, 0, GROUPS, CH, (bin_[:, 0], bin_[:, 1]), True, "cout")
            dve.wait_ge(prep_pe.sem, prep_pe.at((l, "v", 0, 5)))
            wide(c_in, p_z, 12, 12, 15, (cz[:, 0], cz[:, 1]), True, "cz1")

        @block.vector
        def _(dve):
            dve.memset(ones[:], 1.0).then_inc(ones_ready.sem, ones_ready.mark(0))
            dve.memset(eps_col[:], EPS).then_inc(ones_ready.sem, ones_ready.mark(1))
            dve.wait_ge(ones_ready.sem, ones_ready.at(1))
            for l in range(DEPTH):
                dve_prepare(dve, l)
            for k in range(KD):
                add_squares(dve, (0, 1), k, TOK)
            dve.wait_ge(consts_in.sem, consts_in.at(0))
            dve.wait_ge(ada_turned.sem, DEPTH * ADA_PAIRS * 2)
            dve.tensor_tensor(
                ada[:].rearrange("p l m c -> p (l m) c"),
                ps[:, 3, 0:DEPTH * ADA_TILES * 2].rearrange("p (m c) -> p m c", c=2),
                ada_b[:].rearrange("p l m -> p (l m)").unsqueeze(2).to_broadcast([P, DEPTH * ADA_TILES, 2]), ALU.add).then_inc(
                    
                    ada_ready.sem, ada_ready.mark(0))
            dve.wait_ge(ada_ready.sem, ada_ready.at(0))
            for l in range(DEPTH):
                for w in range(2):
                    r0 = (1, 4)[w] * KD
                    dve.scalar_tensor_tensor(gain[:, l, w], ada[:, l, r0:r0 + KD, :], 1.0,
                                             ln[:, l, w].unsqueeze(2).to_broadcast([P, KD, 2]), ALU.add, ALU.mult)
            dve.tensor_scalar(b_gate[:], b_gate[:], 0.5, None, ALU.mult).then_inc(ada_ready.sem, ada_ready.mark(1))
            dve.wait_ge(ada_ready.sem, ada_ready.at(1))
            for l in range(DEPTH):
                dve_layer(dve, l)
            invert(dve, (DEPTH, 1), LAT)
            for k in range(KD):
                dve.scalar_tensor_tensor(xo[:, k, :], x[:, k, 0:LAT], fnorm[:, k:k + 1],
                                                            ps[:, 3, 0:LAT], ALU.mult, ALU.mult).then_inc(
                                                                fin_ready.sem, fin_ready.mark(k))

        for s in signals:
            book[s.name] = s.new


def lay_out(inp):
    f = np.ascontiguousarray
    a = {k: np.asarray(v) for k, v in inp.items()}
    L = DEPTH
    rows = np.concatenate([a["x"][0], a["ctx"][0]], 0)
    t = {"x_t": f(rows.T.reshape(KD, P, TOK).transpose(1, 0, 2))}
    t["cvec"] = f(np.stack([a["c"][0], a["c_ctx"]], -1).reshape(KD, P, 2).transpose(1, 0, 2))

    def tiles(w):
        k, m = w.shape
        return w.reshape(k // P, P, m // P, P).transpose(2, 1, 0, 3).reshape(m // P, P, k)

    def cols(v):
        return np.moveaxis(v.reshape(*v.shape[:-1], -1, P), -1, 0)

    t["ada_w"] = f(a["ada_w"].reshape(L, 4, 2, P, 12, 512).transpose(0, 4, 1, 3, 2, 5).reshape(L * ADA_TILES, P, D))
    t["ada_b"] = f(cols(a["ada_b"]))
    t["ln"] = f(np.stack([cols(a["ln1"]), cols(a["ln2"])], 2))
    t["fnorm"] = f(cols(a["final_norm"]))
    t["qkn"] = f(np.concatenate([cols(a["q_norm"]), cols(a["kv_norm"])], -1))
    t["b_gate"] = f(cols(a["b_gate"]))
    t["b_glu"] = f(cols(a["b_glu"]))
    t["ssm_d"] = f(cols(a["ssm_d"]))
    swap = np.r_[ROPE // 2:ROPE, 0:ROPE // 2]
    main, pairs = [], []
    for l in range(L):
        w = a["w_in"][l]
        r0 = QL + KVL
        kr = w[:, r0:r0 + ROPE]
        kr = np.concatenate([kr, kr[:, swap]], 1)
        f0, s0 = r0 + ROPE, r0 + ROPE + 384
        w = np.concatenate([w[:, s0:], w[:, QL:r0], kr, kr, w[:, :QL], w[:, f0:s0]], 1)
        main.append(tiles(w))
        g = tiles(a["w_gate"][l])
        ba, bf, bs = (tiles(a[n][l]) for n in ("w_br_attn", "w_br_fourier", "w_br_ssm"))
        for m in range(KD):
            one = np.concatenate([ba[m], bs[m][:, :P], bs[m][:, :3 * P]], 1)
            two = np.concatenate([bs[m][:, P:], bf[m], bf[m]], 1)
            main.append(np.stack([g[m], one, g[2 * KD + m], two, g[KD + m]]))
        main.append(tiles(a["w_out"][l]))
        w1, w2 = tiles(a["w_mlp1"][l]), tiles(a["w_mlp2"][l])
        for q in range(QUARTERS):
            main.append(w1[q * KD:(q + 1) * KD])
            main.append(w2[:, :, q * D:(q + 1) * D])
        q = a["w_uq"][l].reshape(QL, HEADS, NOPE + ROPE)
        q = np.concatenate([q, q[:, :, NOPE:][:, :, swap]], 2)
        kv = a["w_ukv"][l].reshape(KVL, HEADS, NOPE + VH)
        for h in range(0, HEADS, 2):
            qt = [tiles(q[:, h + j])[0] for j in range(2)]
            kt = tiles(kv[:, h:h + 2, :NOPE].reshape(KVL, P))[0]
            vt = tiles(kv[:, h:h + 2, NOPE:].reshape(KVL, P))[0]
            pairs.append(np.concatenate([*qt, kt, vt], 1))
    t["w_main"] = f(np.concatenate(main))
    t["w_pair"] = f(np.stack(pairs).reshape(L, HEADS // 2, P, 1280))
    t["w_glu"] = f(np.stack([a["w_glu"][l].reshape(3, P, 384).transpose(1, 0, 2).reshape(P, -1) for l in range(L)]))
    la = []
    for l in range(L):
        re, im = (a[n][l].transpose(0, 2, 1).reshape(P, GROUPS) for n in ("ssm_a_re", "ssm_a_im"))
        st = np.broadcast_to(a["ssm_log_step"][l][:, None, :], (2, NS, GROUPS)).reshape(P, GROUPS)
        la.append(np.stack([re, im, st], 1))
    t["ssm_a"] = f(np.stack(la))
    t["ssm_b"] = f(np.stack([a[n].transpose(0, 1, 3, 2, 4).reshape(L, P, GROUPS, GP)
                             for n in ("ssm_b_re", "ssm_b_im")], 2))
    t["ssm_c"] = f(np.stack([a[n].transpose(0, 1, 4, 2, 3).reshape(L, P, GROUPS, GP)
                             for n in ("ssm_c_re", "ssm_c_im")], 2))
    t["ident"] = np.eye(P, dtype=np.float32)
    half = ROPE // 2
    inv = np.float32(10000.0) ** (-np.arange(0, half, 2, dtype=np.float32) / np.float32(half))
    pos = np.arange(LAT)
    ang = np.concatenate([(pos // 64).astype(np.float32)[:, None] * inv, (pos % 64).astype(np.float32)[:, None] * inv], 1)
    tab = np.zeros((P, TOK), np.float32)
    tab[64:96] = 1.0
    tab[64:80, :LAT] = tab[80:96, :LAT] = np.cos(ang).T
    tab[96:112, :LAT], tab[112:128, :LAT] = -np.sin(ang).T, np.sin(ang).T
    t["rope"] = tab

    def dft(n):
        k = np.outer(np.arange(n), np.arange(n)) % n * (2 * np.pi / n)
        return np.cos(k), np.sin(k)

    for name, n in (("dft_l", LAT), ("dft_c", CTX)):
        c, s = dft(n)
        m = np.stack([c, -s], 1) / np.sqrt(n)
        t[name] = f(m.reshape(n // P, P, 2, n).transpose(1, 0, 2, 3).astype(np.float32))
    c, s = dft(64)
    eye = np.eye(2)
    t["c64"] = f((np.concatenate([np.kron(eye, c), np.kron(eye, s)], 1) / 8.0).astype(np.float32))
    return t


def kernel(**inputs):
    import concourse.bacc as bacc
    from concourse.bass_utils import run_bass_kernel_spmd

    arrays = lay_out(inputs)
    book = {}
    for _ in range(2):
        nc = bacc.Bacc("TRN2", target_bir_lowering=False, num_devices=1)
        aps = {k: nc.dram_tensor(f"in_{k}", v.shape, F32, kind="ExternalInput").ap() for k, v in arrays.items()}
        out = nc.dram_tensor("out_t", (P, KD, LAT), F32, kind="ExternalOutput").ap()
        build(nc, aps, out, book)
    r = run_bass_kernel_spmd(nc, [{f"in_{k}": v for k, v in arrays.items()}], core_ids=[0])
    y = r.results[0]["out_t"]
    return np.ascontiguousarray(y.transpose(2, 1, 0).reshape(1, LAT, D))
```
